# Optimizing a Trainium2 kernel written in Bass

```python
import jax
import jax.numpy as jnp
from jax import lax
import numpy as np
import math
import jax, jax.numpy as jnp

D_MODEL = 1024
BATCH = 1
SEQ = 256
DEPTH = 2

EPS = 1e-6
MLA_HEADS = 8
MLA_Q_LORA = 256
MLA_KV_LORA = 128
MLA_NOPE = 128
MLA_ROPE = 64
MLA_V = 128
MLA_QK = MLA_NOPE + MLA_ROPE
MLA_IN = MLA_Q_LORA + MLA_KV_LORA + MLA_ROPE
ROPE_THETA = 10000.0
Q_BLOCK = 128
MLSTM_HEADS = 8
MLSTM_V = D_MODEL // MLSTM_HEADS
MLSTM_QK = MLSTM_V // 2
MLSTM_QK_TOT = MLSTM_HEADS * MLSTM_QK
MLSTM_V_TOT = MLSTM_HEADS * MLSTM_V
MLSTM_IN = 2 * MLSTM_QK_TOT + MLSTM_V_TOT + D_MODEL + 2 * MLSTM_HEADS
MLSTM_CHUNK = 64
CONV_W = 4
GATE_CAP = 15.0
D_FF = 7 * D_MODEL // 2
N_EXPERTS = 8
TOP_K = 2
N_EVEN = (DEPTH + 1) // 2
N_ODD = DEPTH // 2


def rmsnorm(x, g):
    xf = x.astype(jnp.float32)
    y = xf * lax.rsqrt(jnp.mean(xf * xf, axis=-1, keepdims=True) + EPS)
    return (y * g.astype(jnp.float32)).astype(x.dtype)

def rope_tables(positions):
    inv = 1.0 / (ROPE_THETA ** (jnp.arange(0, MLA_ROPE, 2, dtype=jnp.float32) / MLA_ROPE))
    ang = positions.astype(jnp.float32)[..., None] * inv
    return jnp.cos(ang), jnp.sin(ang)

def apply_rope(t, cos, sin):
    tf = t.astype(jnp.float32)
    t1, t2 = jnp.split(tf, 2, axis=-1)
    return jnp.concatenate([t1 * cos - t2 * sin, t1 * sin + t2 * cos], axis=-1).astype(t.dtype)

def causal_block_attention(q, k, v):
    B, S, H, DQ = q.shape
    DV = v.shape[-1]
    nb = S // Q_BLOCK
    scale = DQ ** -0.5
    kf = k.astype(jnp.float32)
    vf = v.astype(jnp.float32)
    qb = q.astype(jnp.float32).reshape(B, nb, Q_BLOCK, H, DQ).transpose(1, 0, 2, 3, 4)
    starts = jnp.arange(nb, dtype=jnp.int32) * Q_BLOCK
    kpos = jnp.arange(S, dtype=jnp.int32)

    def one_block(args):
        q_blk, start = args
        s = jnp.einsum('bqhd,bkhd->bhqk', q_blk, kf) * scale
        qpos = start + jnp.arange(Q_BLOCK, dtype=jnp.int32)
        s = jnp.where(kpos[None, :] <= qpos[:, None], s, -jnp.inf)
        p = jax.nn.softmax(s, axis=-1)
        return jnp.einsum('bhqk,bkhd->bqhd', p, vf)

    out = lax.map(one_block, (qb, starts))
    return out.transpose(1, 0, 2, 3, 4).reshape(B, S, H, DV)

def mla_mixer(xn, cos, sin, w_in, q_norm, w_qb, kv_norm, w_kvb, w_out):
    B, S, _ = xn.shape
    proj = xn @ w_in
    c_q = proj[..., :MLA_Q_LORA]
    c_kv = proj[..., MLA_Q_LORA:MLA_Q_LORA + MLA_KV_LORA]
    k_rope = proj[..., MLA_Q_LORA + MLA_KV_LORA:]
    q = (rmsnorm(c_q, q_norm) @ w_qb).reshape(B, S, MLA_HEADS, MLA_QK)
    kv = (rmsnorm(c_kv, kv_norm) @ w_kvb).reshape(B, S, MLA_HEADS, MLA_NOPE + MLA_V)
    q_rot = apply_rope(q[..., MLA_NOPE:], cos[:, :, None, :], sin[:, :, None, :])
    k_rot = apply_rope(k_rope, cos, sin)[:, :, None, :]
    qh = jnp.concatenate([q[..., :MLA_NOPE], q_rot], axis=-1)
    kh = jnp.concatenate([kv[..., :MLA_NOPE], jnp.broadcast_to(k_rot, (B, S, MLA_HEADS, MLA_ROPE))], axis=-1)
    vh = kv[..., MLA_NOPE:]
    o = causal_block_attention(qh, kh, vh)
    return o.reshape(B, S, MLA_HEADS * MLA_V).astype(xn.dtype) @ w_out

def mlstm_chunkwise(q, k, v, i_pre, log_f):
    B, S, H, DK = q.shape
    DV = v.shape[-1]
    L = MLSTM_CHUNK
    NC = S // L
    f32 = jnp.float32
    q = q.astype(f32).transpose(0, 2, 1, 3).reshape(B, H, NC, L, DK) * (DK ** -0.5)
    k = k.astype(f32).transpose(0, 2, 1, 3).reshape(B, H, NC, L, DK)
    v = v.astype(f32).transpose(0, 2, 1, 3).reshape(B, H, NC, L, DV)
    ig = i_pre.astype(f32).transpose(0, 2, 1).reshape(B, H, NC, L)
    lf = log_f.astype(f32).transpose(0, 2, 1).reshape(B, H, NC, L)
    b = jnp.cumsum(lf, axis=-1)
    b_last = b[..., -1]
    a = b_last[..., None] - b + ig
    m_loc = jnp.max(a, axis=-1)
    w = jnp.exp(a - m_loc[..., None])
    c_loc = jnp.einsum('bhcl,bhcld,bhcle->bhcde', w, k, v)
    n_loc = jnp.einsum('bhcl,bhcld->bhcd', w, k)

    def step(carry, inp):
        c, n, m = carry
        cl, nl, ml, bl = inp
        m_new = jnp.maximum(bl + m, ml)
        s_prev = jnp.exp(bl + m - m_new)
        s_loc = jnp.exp(ml - m_new)
        c_new = s_prev[..., None, None] * c + s_loc[..., None, None] * cl
        n_new = s_prev[..., None] * n + s_loc[..., None] * nl
        return (c_new, n_new, m_new), (c, n, m)

    init = (jnp.zeros((B, H, DK, DV), f32), jnp.zeros((B, H, DK), f32), jnp.zeros((B, H), f32))
    xs = (c_loc.transpose(2, 0, 1, 3, 4), n_loc.transpose(2, 0, 1, 3), m_loc.transpose(2, 0, 1), b_last.transpose(2, 0, 1))
    _, (c_prev, n_prev, m_prev) = lax.scan(step, init, xs)
    c_prev = c_prev.transpose(1, 2, 0, 3, 4)
    n_prev = n_prev.transpose(1, 2, 0, 3)
    m_prev = m_prev.transpose(1, 2, 0)
    causal = jnp.tril(jnp.ones((L, L), dtype=bool))
    d = jnp.where(causal, b[..., :, None] - b[..., None, :] + ig[..., None, :], -jnp.inf)
    inter = b + m_prev[..., None]
    m_t = jnp.maximum(inter, jnp.max(d, axis=-1))
    wts = jnp.exp(d - m_t[..., None]) * jnp.einsum('bhctd,bhcsd->bhcts', q, k)
    s_inter = jnp.exp(inter - m_t)
    num = jnp.einsum('bhcts,bhcse->bhcte', wts, v) + s_inter[..., None] * jnp.einsum('bhctd,bhcde->bhcte', q, c_prev)
    den = jnp.sum(wts, axis=-1) + s_inter * jnp.einsum('bhctd,bhcd->bhct', q, n_prev)
    h = num / jnp.maximum(jnp.abs(den), jnp.exp(-m_t))[..., None]
    return h.reshape(B, H, S, DV).transpose(0, 2, 1, 3)

def mlstm_mixer(xn, w_in, conv_w, conv_b, gate_b, head_norm, w_out):
    B, S, _ = xn.shape
    proj = xn @ w_in
    o1 = 2 * MLSTM_QK_TOT
    o2 = o1 + MLSTM_V_TOT
    o3 = o2 + D_MODEL
    qk_raw = proj[..., :o1]
    v = proj[..., o1:o2]
    o_pre = proj[..., o2:o3]
    g_pre = proj[..., o3:]
    qk = lax.conv_general_dilated(qk_raw, conv_w[:, None, :], window_strides=(1,), padding=[(CONV_W - 1, 0)],
                                  dimension_numbers=('NWC', 'WIO', 'NWC'), feature_group_count=o1)
    qk = jax.nn.silu(qk + conv_b)
    q = qk[..., :MLSTM_QK_TOT].reshape(B, S, MLSTM_HEADS, MLSTM_QK)
    k = qk[..., MLSTM_QK_TOT:].reshape(B, S, MLSTM_HEADS, MLSTM_QK)
    gates = g_pre.astype(jnp.float32) + gate_b.astype(jnp.float32)
    gates = GATE_CAP * jnp.tanh(gates / GATE_CAP)
    i_pre = gates[..., :MLSTM_HEADS]
    log_f = jax.nn.log_sigmoid(gates[..., MLSTM_HEADS:])
    h = mlstm_chunkwise(q, k, v.reshape(B, S, MLSTM_HEADS, MLSTM_V), i_pre, log_f)
    h = rmsnorm(h, head_norm.reshape(MLSTM_HEADS, MLSTM_V)).reshape(B, S, MLSTM_V_TOT)
    y = jax.nn.sigmoid(o_pre.astype(jnp.float32)) * h
    return y.astype(xn.dtype) @ w_out

def swiglu(h, wg, wu, wd):
    return (jax.nn.silu(h @ wg) * (h @ wu)) @ wd

def moe_swiglu(h, router, wg, wu, wd):
    logits = (h @ router).astype(jnp.float32)
    top_v, top_i = lax.top_k(logits, TOP_K)
    gates = jax.nn.softmax(top_v, axis=-1)
    combine = jnp.sum(jax.nn.one_hot(top_i, N_EXPERTS, dtype=jnp.float32) * gates[..., None], axis=-2)
    y = jnp.zeros(h.shape, jnp.float32)
    for e in range(N_EXPERTS):
        y = y + combine[..., e:e + 1] * swiglu(h, wg[e], wu[e], wd[e]).astype(jnp.float32)
    return y.astype(h.dtype)

def first_inputs(seed: int = 0) -> dict:
    key = jax.random.key(seed)
    ks = jax.random.split(key, 32)
    f32 = jnp.float32

    def nrm(k, shape, scale):
        return jax.random.normal(k, shape, f32) * scale

    x = nrm(ks[0], (BATCH, SEQ, D_MODEL), 1.0)
    offs = jax.random.randint(ks[1], (BATCH, 1), 0, 1024, dtype=jnp.int32)
    positions = offs + jnp.arange(SEQ, dtype=jnp.int32)[None, :]
    norm_mix = 1.0 + nrm(ks[2], (DEPTH, D_MODEL), 0.02)
    norm_ffn = 1.0 + nrm(ks[3], (DEPTH, D_MODEL), 0.02)
    final_norm = 1.0 + nrm(ks[4], (D_MODEL,), 0.02)
    mla_w_in = nrm(ks[5], (N_EVEN, D_MODEL, MLA_IN), D_MODEL ** -0.5)
    mla_q_norm = 1.0 + nrm(ks[6], (N_EVEN, MLA_Q_LORA), 0.02)
    mla_w_qb = nrm(ks[7], (N_EVEN, MLA_Q_LORA, MLA_HEADS * MLA_QK), MLA_Q_LORA ** -0.5)
    mla_kv_norm = 1.0 + nrm(ks[8], (N_EVEN, MLA_KV_LORA), 0.02)
    mla_w_kvb = nrm(ks[9], (N_EVEN, MLA_KV_LORA, MLA_HEADS * (MLA_NOPE + MLA_V)), MLA_KV_LORA ** -0.5)
    mla_w_out = nrm(ks[10], (N_EVEN, MLA_HEADS * MLA_V, D_MODEL), (MLA_HEADS * MLA_V) ** -0.5)
    mlstm_w_in = nrm(ks[11], (N_ODD, D_MODEL, MLSTM_IN), D_MODEL ** -0.5)
    mlstm_conv_w = nrm(ks[12], (N_ODD, CONV_W, 2 * MLSTM_QK_TOT), CONV_W ** -0.5)
    mlstm_conv_b = nrm(ks[13], (N_ODD, 2 * MLSTM_QK_TOT), 0.02)
    i_bias = nrm(ks[14], (N_ODD, MLSTM_HEADS), 0.1)
    f_bias = jnp.linspace(3.0, 6.0, MLSTM_HEADS, dtype=f32)[None, :] + nrm(ks[15], (N_ODD, MLSTM_HEADS), 0.1)
    mlstm_gate_b = jnp.concatenate([i_bias, f_bias], axis=-1)
    mlstm_head_norm = 1.0 + nrm(ks[16], (N_ODD, MLSTM_V_TOT), 0.02)
    mlstm_w_out = nrm(ks[17], (N_ODD, MLSTM_V_TOT, D_MODEL), MLSTM_V_TOT ** -0.5)
    ffn_w_gate = nrm(ks[18], (N_EVEN, D_MODEL, D_FF), D_MODEL ** -0.5)
    ffn_w_up = nrm(ks[19], (N_EVEN, D_MODEL, D_FF), D_MODEL ** -0.5)
    ffn_w_down = nrm(ks[20], (N_EVEN, D_FF, D_MODEL), D_FF ** -0.5)
    moe_router = nrm(ks[21], (N_ODD, D_MODEL, N_EXPERTS), D_MODEL ** -0.5)
    moe_w_gate = nrm(ks[22], (N_ODD, N_EXPERTS, D_MODEL, D_FF), D_MODEL ** -0.5)
    moe_w_up = nrm(ks[23], (N_ODD, N_EXPERTS, D_MODEL, D_FF), D_MODEL ** -0.5)
    moe_w_down = nrm(ks[24], (N_ODD, N_EXPERTS, D_FF, D_MODEL), D_FF ** -0.5)
    return {'x': x, 'positions': positions, 'norm_mix': norm_mix, 'norm_ffn': norm_ffn, 'final_norm': final_norm,
            'mla_w_in': mla_w_in, 'mla_q_norm': mla_q_norm, 'mla_w_qb': mla_w_qb, 'mla_kv_norm': mla_kv_norm,
            'mla_w_kvb': mla_w_kvb, 'mla_w_out': mla_w_out, 'mlstm_w_in': mlstm_w_in, 'mlstm_conv_w': mlstm_conv_w,
            'mlstm_conv_b': mlstm_conv_b, 'mlstm_gate_b': mlstm_gate_b, 'mlstm_head_norm': mlstm_head_norm,
            'mlstm_w_out': mlstm_w_out, 'ffn_w_gate': ffn_w_gate, 'ffn_w_up': ffn_w_up, 'ffn_w_down': ffn_w_down,
            'moe_router': moe_router, 'moe_w_gate': moe_w_gate, 'moe_w_up': moe_w_up, 'moe_w_down': moe_w_down}

def first_block(x, positions, norm_mix, norm_ffn, final_norm, mla_w_in, mla_q_norm, mla_w_qb, mla_kv_norm,
              mla_w_kvb, mla_w_out, mlstm_w_in, mlstm_conv_w, mlstm_conv_b, mlstm_gate_b, mlstm_head_norm,
              mlstm_w_out, ffn_w_gate, ffn_w_up, ffn_w_down, moe_router, moe_w_gate, moe_w_up, moe_w_down):
    cos, sin = rope_tables(positions)
    for layer in range(DEPTH):
        j = layer // 2
        h = rmsnorm(x, norm_mix[layer])
        if layer % 2 == 0:
            y = mla_mixer(h, cos, sin, mla_w_in[j], mla_q_norm[j], mla_w_qb[j], mla_kv_norm[j], mla_w_kvb[j], mla_w_out[j])
        else:
            y = mlstm_mixer(h, mlstm_w_in[j], mlstm_conv_w[j], mlstm_conv_b[j], mlstm_gate_b[j], mlstm_head_norm[j], mlstm_w_out[j])
        x = x + y.astype(x.dtype)
        h = rmsnorm(x, norm_ffn[layer])
        if layer % 2 == 0:
            y = swiglu(h, ffn_w_gate[j], ffn_w_up[j], ffn_w_down[j])
        else:
            y = moe_swiglu(h, moe_router[j], moe_w_gate[j], moe_w_up[j], moe_w_down[j])
        x = x + y.astype(x.dtype)
    return rmsnorm(x, final_norm)


GRID_W = 64
HEAD_DIM = 64
ATT_Q_HEADS = 8
ATT_KV_HEADS = 2
ATT_Q_W = ATT_Q_HEADS * HEAD_DIM
ATT_KV_W = ATT_KV_HEADS * HEAD_DIM
HY_WIDTH = 512
HY_ORDER = 2
HY_BANDS = 16
HY_EMB = 1 + 2 * HY_BANDS
HY_FFN = 64
HY_FAST_DECAY = 0.3
HY_SLOW_DECAY = 1.5
HY_TARGET = 1e-2
GLA_HEADS = 4
GLA_DK = 64
GLA_DV = 128
GLA_RANK = 16
GLA_NORMALIZER = 16.0
GLA_CHUNK = 64
GLA_K_W = GLA_HEADS * GLA_DK
GLA_V_W = GLA_HEADS * GLA_DV
MEM_LEN = 256
X_HEADS = 4
X_HEAD_DIM = D_MODEL // X_HEADS
D_FF_2 = 4 * D_MODEL
N_BRANCH = 3
IN_SPLITS = (ATT_Q_W, ATT_KV_W, ATT_KV_W, 3 * HY_WIDTH, GLA_K_W, GLA_K_W, GLA_V_W, GLA_V_W,
             2 * GLA_RANK, N_BRANCH * D_MODEL)
N_IN = ATT_Q_W + 2 * ATT_KV_W + 3 * HY_WIDTH + 2 * GLA_K_W + 2 * GLA_V_W + 2 * GLA_RANK + N_BRANCH * D_MODEL


F32 = jnp.float32

def rmsnorm_2(x, g):
    xf = x.astype(F32)
    y = xf * lax.rsqrt(jnp.mean(xf * xf, axis=-1, keepdims=True) + EPS)
    return (y * g.astype(F32)).astype(x.dtype)

def split_cols(u, sizes):
    idx = [int(i) for i in np.cumsum(sizes)[:-1]]
    return jnp.split(u, idx, axis=-1)

def axial_rope_angles(L):
    rows = L // GRID_W
    r, c = jnp.meshgrid(jnp.arange(rows), jnp.arange(GRID_W), indexing="ij")
    n_freq = HEAD_DIM // 4
    inv = ROPE_THETA ** (-jnp.arange(n_freq, dtype=F32) / n_freq)
    pos = jnp.stack([r.reshape(-1), c.reshape(-1)], axis=1).astype(F32)
    ang = pos[:, :, None] * inv
    return jnp.cos(ang), jnp.sin(ang)

def apply_rope_2(x, cos, sin):
    xs = x.reshape(x.shape[:-1] + (2, 2, HEAD_DIM // 4)).astype(F32)
    x1, x2 = xs[..., 0, :], xs[..., 1, :]
    out = jnp.stack([x1 * cos - x2 * sin, x1 * sin + x2 * cos], axis=-2)
    return out.reshape(x.shape).astype(x.dtype)

def attention_mixer(q, k, v, qn, kn, cos, sin):
    B, L, _ = q.shape
    G = ATT_Q_HEADS // ATT_KV_HEADS
    q = rmsnorm_2(q.reshape(B, L, ATT_Q_HEADS, HEAD_DIM), qn).transpose(0, 2, 1, 3)
    k = rmsnorm_2(k.reshape(B, L, ATT_KV_HEADS, HEAD_DIM), kn).transpose(0, 2, 1, 3)
    v = v.reshape(B, L, ATT_KV_HEADS, HEAD_DIM).transpose(0, 2, 1, 3)
    q = apply_rope_2(q, cos, sin).reshape(B, ATT_KV_HEADS, G, L, HEAD_DIM)
    k = apply_rope_2(k, cos, sin)
    nb = L // Q_BLOCK
    qb = jnp.moveaxis(q.reshape(B, ATT_KV_HEADS, G, nb, Q_BLOCK, HEAD_DIM), 3, 0)
    scale = HEAD_DIM ** -0.5

    def block(qblk):
        s = jnp.einsum("bkgqd,bktd->bkgqt", qblk, k).astype(F32) * scale
        p = jax.nn.softmax(s, axis=-1).astype(v.dtype)
        return jnp.einsum("bkgqt,bktd->bkgqd", p, v)

    o = lax.map(block, qb)
    o = jnp.moveaxis(o, 0, 3).reshape(B, ATT_Q_HEADS, L, HEAD_DIM)
    return o.transpose(0, 2, 1, 3).reshape(B, L, ATT_Q_W)

def short_conv(u, w):
    up = jnp.pad(u, ((0, 0), (1, 1), (0, 0)))
    return up[:, :-2] * w[0] + up[:, 1:-1] * w[1] + up[:, 2:] * w[2]

def hyena_pos_features(L):
    t = jnp.arange(L, dtype=F32)
    t_norm = t / max(L - 1, 1)
    w = 2.0 * math.pi * t / L
    f = jnp.linspace(1e-4, HY_BANDS - 1, HY_BANDS, dtype=F32)
    fw = w[:, None] * f
    z = jnp.concatenate([t_norm[:, None], jnp.cos(fw), -jnp.sin(fw)], axis=-1)
    deltas = jnp.abs(jnp.linspace(math.log(HY_TARGET) / HY_FAST_DECAY,
                                  math.log(HY_TARGET) / HY_SLOW_DECAY, HY_WIDTH, dtype=F32))
    window = jnp.exp(-t_norm[:, None] * deltas)
    return z, window

def hyena_filter_spectra(z, window, w1, b1, w2, b2, w3, b3, freq):
    L = z.shape[0]
    c = lambda a: a.astype(F32)
    h = jnp.sin(c(freq[0]) * (z @ c(w1) + c(b1)))
    h = jnp.sin(c(freq[1]) * (h @ c(w2) + c(b2)))
    h = (h @ c(w3) + c(b3)).reshape(L, HY_ORDER, 2, HY_WIDTH) * window[:, None, None, :]
    fwd, bwd = h[:, :, 0], h[:, :, 1]
    f = jnp.concatenate([fwd, jnp.zeros((1, HY_ORDER, HY_WIDTH), F32), bwd[1:][::-1]], axis=0)
    f = f / (jnp.sum(jnp.abs(f), axis=0, keepdims=True) + EPS)
    return jnp.fft.rfft(f, axis=0)

def long_conv(u, spec, skip):
    L = u.shape[1]
    uf = u.astype(F32)
    y = jnp.fft.irfft(jnp.fft.rfft(uf, n=2 * L, axis=1) * spec, n=2 * L, axis=1)[:, :L]
    return (y + uf * skip.astype(F32)).astype(u.dtype)

def hyena_mixer(u, conv_w, spec, skip):
    u = short_conv(u, conv_w)
    v, x1, x2 = jnp.split(u, 3, axis=-1)
    z = x1 * long_conv(v, spec[:, 0], skip[0])
    return x2 * long_conv(z, spec[:, 1], skip[1])

def gla_scan(q, k, v, g, include_diag):
    B, H, L, dk = q.shape
    dv = v.shape[-1]
    C = GLA_CHUNK
    N = L // C
    q, k, g = (a.reshape(B, H, N, C, dk) for a in (q, k, g))
    v = v.reshape(B, H, N, C, dv)
    b = jnp.cumsum(g, axis=3)
    b_last = b[:, :, :, -1:, :]
    q_dec = q * jnp.exp(b)
    a = jnp.einsum("bhncd,bhnsd->bhncs", q_dec, k * jnp.exp(-b))
    mask = jnp.tril(jnp.ones((C, C), dtype=bool), k=0 if include_diag else -1)
    o = jnp.einsum("bhncs,bhnse->bhnce", jnp.where(mask, a, 0.0), v)
    d_state = jnp.einsum("bhncd,bhnce->bhnde", k * jnp.exp(b_last - b), v)
    decay = jnp.exp(b_last[:, :, :, 0, :])

    def step(S, inp):
        dec, ds = inp
        return dec[..., None] * S + ds, S

    _, s_prev = lax.scan(step, jnp.zeros((B, H, dk, dv), F32),
                         (jnp.moveaxis(decay, 2, 0), jnp.moveaxis(d_state, 2, 0)))
    s_prev = jnp.moveaxis(s_prev, 0, 2)
    o = o + jnp.einsum("bhncd,bhnde->bhnce", q_dec, s_prev)
    return o.reshape(B, H, L, dv)

def gla_mixer(q, k, v, og, lr, w_lr, b_lr, onorm):
    B, L, _ = q.shape
    heads = lambda a, d: a.astype(F32).reshape(B, L, GLA_HEADS, d).transpose(0, 2, 1, 3)
    q = heads(q, GLA_DK) * (GLA_DK ** -0.5)
    k = heads(k, GLA_DK)
    v = heads(v, GLA_DV)
    logit = jnp.einsum("btsr,srd->btsd", lr.astype(F32).reshape(B, L, 2, GLA_RANK),
                       w_lr.astype(F32)) + b_lr.astype(F32)
    g = jax.nn.log_sigmoid(logit) / GLA_NORMALIZER
    g_f = heads(g[:, :, 0], GLA_DK)
    g_b = heads(g[:, :, 1], GLA_DK)
    fl = lambda a: jnp.flip(a, axis=2)
    o_f = gla_scan(q, k, v, g_f, True)
    o_b = fl(gla_scan(fl(q), fl(k), fl(v), fl(g_b), False))
    o = (o_f + o_b).transpose(0, 2, 1, 3)
    o = rmsnorm_2(o, onorm) * jax.nn.silu(og.astype(F32).reshape(B, L, GLA_HEADS, GLA_DV))
    return o.reshape(B, L, GLA_V_W).astype(og.dtype)

def memory_cross_attention(hn, mn, wq, wk, wv, wo, qn, kn):
    B, L, _ = hn.shape
    M = mn.shape[1]
    q = rmsnorm_2((hn @ wq).reshape(B, L, X_HEADS, X_HEAD_DIM), qn)
    k = rmsnorm_2((mn @ wk).reshape(B, M, X_HEADS, X_HEAD_DIM), kn)
    v = (mn @ wv).reshape(B, M, X_HEADS, X_HEAD_DIM)
    s = jnp.einsum("blhd,bmhd->bhlm", q, k).astype(F32) * (X_HEAD_DIM ** -0.5)
    p = jax.nn.softmax(s, axis=-1).astype(v.dtype)
    o = jnp.einsum("bhlm,bmhd->blhd", p, v).reshape(B, L, D_MODEL)
    return o @ wo

def second_inputs(seed: int = 0) -> dict:
    key = jax.random.key(seed)
    ks = iter(jax.random.split(key, 40))

    def nrm(shape, s):
        return jax.random.normal(next(ks), shape, F32) * s

    def gain(shape):
        return 1.0 + nrm(shape, 0.02)

    Ld = DEPTH
    return {
        "x": nrm((BATCH, SEQ, D_MODEL), 1.0),
        "mem": nrm((BATCH, MEM_LEN, D_MODEL), 1.0),
        "ln_mix": gain((Ld, D_MODEL)),
        "w_in": nrm((Ld, D_MODEL, N_IN), D_MODEL ** -0.5),
        "attn_qnorm": gain((Ld, HEAD_DIM)),
        "attn_knorm": gain((Ld, HEAD_DIM)),
        "hy_conv": nrm((Ld, 3, 3 * HY_WIDTH), 3 ** -0.5),
        "hy_w1": nrm((Ld, HY_EMB, HY_FFN), HY_EMB ** -0.5),
        "hy_b1": nrm((Ld, HY_FFN), 0.1),
        "hy_w2": nrm((Ld, HY_FFN, HY_FFN), HY_FFN ** -0.5),
        "hy_b2": nrm((Ld, HY_FFN), 0.1),
        "hy_w3": nrm((Ld, HY_FFN, HY_ORDER * 2 * HY_WIDTH), HY_FFN ** -0.5),
        "hy_b3": nrm((Ld, HY_ORDER * 2 * HY_WIDTH), 0.1),
        "hy_freq": 1.0 + nrm((Ld, 2, HY_FFN), 0.1),
        "hy_skip": nrm((Ld, HY_ORDER, HY_WIDTH), 0.5),
        "gla_w_lr": nrm((Ld, 2, GLA_RANK, GLA_K_W), GLA_RANK ** -0.5),
        "gla_b_lr": nrm((Ld, 2, GLA_K_W), 0.1),
        "gla_onorm": gain((Ld, GLA_DV)),
        "w_br_attn": nrm((Ld, ATT_Q_W, D_MODEL), ATT_Q_W ** -0.5),
        "w_br_hyena": nrm((Ld, HY_WIDTH, D_MODEL), HY_WIDTH ** -0.5),
        "w_br_gla": nrm((Ld, GLA_V_W, D_MODEL), GLA_V_W ** -0.5),
        "w_out": nrm((Ld, D_MODEL, D_MODEL), D_MODEL ** -0.5),
        "ln_x": gain((Ld, D_MODEL)),
        "ln_mem": gain((Ld, D_MODEL)),
        "x_wq": nrm((Ld, D_MODEL, D_MODEL), D_MODEL ** -0.5),
        "x_wk": nrm((Ld, D_MODEL, D_MODEL), D_MODEL ** -0.5),
        "x_wv": nrm((Ld, D_MODEL, D_MODEL), D_MODEL ** -0.5),
        "x_wo": nrm((Ld, D_MODEL, D_MODEL), D_MODEL ** -0.5),
        "x_qnorm": gain((Ld, X_HEAD_DIM)),
        "x_knorm": gain((Ld, X_HEAD_DIM)),
        "ln_mlp": gain((Ld, D_MODEL)),
        "mlp_w1": nrm((Ld, D_MODEL, D_FF_2), D_MODEL ** -0.5),
        "mlp_w2": nrm((Ld, D_FF_2, D_MODEL), D_FF_2 ** -0.5),
    }

def second_block(x, mem, ln_mix, w_in, attn_qnorm, attn_knorm, hy_conv, hy_w1, hy_b1, hy_w2, hy_b2,
              hy_w3, hy_b3, hy_freq, hy_skip, gla_w_lr, gla_b_lr, gla_onorm, w_br_attn, w_br_hyena,
              w_br_gla, w_out, ln_x, ln_mem, x_wq, x_wk, x_wv, x_wo, x_qnorm, x_knorm, ln_mlp,
              mlp_w1, mlp_w2):
    B, L, _ = x.shape
    cos, sin = axial_rope_angles(L)
    z_pos, window = hyena_pos_features(L)
    h = x
    for i in range(DEPTH):
        hn = rmsnorm_2(h, ln_mix[i])
        (aq, ak, av, hy, gq, gk, gv, go, glr, gates) = split_cols(hn @ w_in[i], IN_SPLITS)
        y_a = attention_mixer(aq, ak, av, attn_qnorm[i], attn_knorm[i], cos, sin) @ w_br_attn[i]
        spec = hyena_filter_spectra(z_pos, window, hy_w1[i], hy_b1[i], hy_w2[i], hy_b2[i],
                                    hy_w3[i], hy_b3[i], hy_freq[i])
        y_b = hyena_mixer(hy, hy_conv[i], spec, hy_skip[i]) @ w_br_hyena[i]
        y_c = gla_mixer(gq, gk, gv, go, glr, gla_w_lr[i], gla_b_lr[i], gla_onorm[i]) @ w_br_gla[i]
        gate = jax.nn.sigmoid(gates.reshape(B, L, N_BRANCH, D_MODEL))
        mixed = gate[:, :, 0] * y_a + gate[:, :, 1] * y_b + gate[:, :, 2] * y_c
        h = h + mixed @ w_out[i]
        h = h + memory_cross_attention(rmsnorm_2(h, ln_x[i]), rmsnorm_2(mem, ln_mem[i]),
                                       x_wq[i], x_wk[i], x_wv[i], x_wo[i], x_qnorm[i], x_knorm[i])
        hn = rmsnorm_2(h, ln_mlp[i])
        h = h + jnp.square(jax.nn.relu(hn @ mlp_w1[i])) @ mlp_w2[i]
    return h


def setup_inputs(seed=0):
    out = dict(first_inputs(seed))
    for name, value in second_inputs(seed + 1).items():
        if name != "x":
            out[name + "_2"] = value
    return out


def reference(
    x, positions, norm_mix, norm_ffn, final_norm, mla_w_in, mla_q_norm, mla_w_qb, mla_kv_norm,
    mla_w_kvb, mla_w_out, mlstm_w_in, mlstm_conv_w, mlstm_conv_b, mlstm_gate_b, mlstm_head_norm,
    mlstm_w_out, ffn_w_gate, ffn_w_up, ffn_w_down, moe_router, moe_w_gate, moe_w_up, moe_w_down,
    mem_2, ln_mix_2, w_in_2, attn_qnorm_2, attn_knorm_2, hy_conv_2, hy_w1_2, hy_b1_2, hy_w2_2,
    hy_b2_2, hy_w3_2, hy_b3_2, hy_freq_2, hy_skip_2, gla_w_lr_2, gla_b_lr_2, gla_onorm_2,
    w_br_attn_2, w_br_hyena_2, w_br_gla_2, w_out_2, ln_x_2, ln_mem_2, x_wq_2, x_wk_2, x_wv_2,
    x_wo_2, x_qnorm_2, x_knorm_2, ln_mlp_2, mlp_w1_2, mlp_w2_2,
):
    x = first_block(
        x, positions, norm_mix, norm_ffn, final_norm, mla_w_in, mla_q_norm, mla_w_qb,
        mla_kv_norm, mla_w_kvb, mla_w_out, mlstm_w_in, mlstm_conv_w, mlstm_conv_b, mlstm_gate_b,
        mlstm_head_norm, mlstm_w_out, ffn_w_gate, ffn_w_up, ffn_w_down, moe_router, moe_w_gate,
        moe_w_up, moe_w_down,
    )
    return second_block(
        x, mem_2, ln_mix_2, w_in_2, attn_qnorm_2, attn_knorm_2, hy_conv_2, hy_w1_2, hy_b1_2,
        hy_w2_2, hy_b2_2, hy_w3_2, hy_b3_2, hy_freq_2, hy_skip_2, gla_w_lr_2, gla_b_lr_2,
        gla_onorm_2, w_br_attn_2, w_br_hyena_2, w_br_gla_2, w_out_2, ln_x_2, ln_mem_2, x_wq_2,
        x_wk_2, x_wv_2, x_wo_2, x_qnorm_2, x_knorm_2, ln_mlp_2, mlp_w1_2, mlp_w2_2,
    )


_drawn_inputs = setup_inputs


def setup_inputs(seed=0):
    import zlib

    import numpy as np

    out = dict(_drawn_inputs(seed))
    spreads = {}
    factors = {'ln_mix_2': 2.943,
     'attn_qnorm_2': 8.0,
     'attn_knorm_2': 8.0,
     'hy_b1_2': 4.5,
     'hy_b2_2': 3.09,
     'hy_b3_2': 2.774,
     'hy_freq_2': 7.449,
     'gla_b_lr_2': 2.712,
     'gla_onorm_2': 6.929,
     'ln_x_2': 8.0,
     'ln_mem_2': 8.0,
     'x_qnorm_2': 8.0,
     'x_knorm_2': 8.0,
     'ln_mlp_2': 3.54}
    for name, (base, spread) in spreads.items():
        noise = np.random.default_rng([zlib.crc32(name.encode()), seed]).standard_normal(out[name].shape)
        drawn = base * np.exp(spread * noise) if base else spread * noise
        out[name] = jnp.asarray(drawn.astype(out[name].dtype))
    for name, factor in factors.items():
        out[name] = (out[name] * factor).astype(out[name].dtype)
    return out
```

```python
import math
from contextlib import ExitStack, contextmanager

import numpy as np
import concourse.bass as bass
from concourse import mybir

F32 = mybir.dt.float32
BF16 = mybir.dt.bfloat16
I32 = mybir.dt.int32
U32 = mybir.dt.uint32
ALU = mybir.AluOpType
ACT = mybir.ActivationFunctionType
AX = mybir.AxisListType

P = 128
T = 256
TT = T // P
D = 1024
KD = D // P
EPS = 1e-6
NSLOT = 8
UNIT = 256
NEG = -1e30


def constants():
    c = {}
    eye = np.eye(P, dtype=np.float32)
    c["eye"] = eye
    i = np.arange(P)
    c["blocks64"] = (i[:, None] // 64 == i[None, :] // 64).astype(np.float32)
    def rotation(half):
        r = np.zeros((P, P), np.float32)
        for j in range(P):
            if j % (2 * half) < half:
                r[j + half, j] = -1.0
            else:
                r[j - half, j] = 1.0
        return r
    c["rot32"] = rotation(32)
    c["rot16"] = rotation(16)
    for g in range(2):
        e = np.zeros((P, P), np.float32)
        e[64 * g + i % 64, i] = 1.0
        c[f"twice{g}"] = e
    c["causal_add"] = np.where(i[None, :] <= i[:, None], 0.0, NEG).astype(np.float32)
    t = np.arange(T)
    c["keep_st"] = np.stack([(i[:, None] + P * k <= t[None, :]) for k in range(TT)], 1).astype(np.float32).reshape(P, -1)
    same = i[:, None] // 64 == i[None, :] // 64
    c["gla_keep"] = np.stack([same & (i[:, None] <= i[None, :]), same & (i[:, None] > i[None, :])], 1).astype(np.float32).reshape(P, -1)
    c["chunk_start"] = np.tile((t % 64 != 0).astype(np.float32)[None, :], (P, 4))
    sel = np.zeros((8, 8, P), np.float32)
    for h in range(8):
        sel[h, h, :] = 1.0
    c["row_select"] = sel.reshape(8, -1)
    c["inv_freq"] = (1.0 / (10000.0 ** (np.arange(0, 64, 2, dtype=np.float32) / np.float32(64))))[i % 32].astype(np.float32)[:, None]
    d = i % 64
    inv = (10000.0 ** (-np.arange(16, dtype=np.float32) / np.float32(16))).astype(np.float32)
    pos = np.stack([t // 64, t % 64]).astype(np.float32)
    ang = (pos[d // 32] * inv[d % 16][:, None]).astype(np.float32)
    c["axial_cos"] = np.cos(ang).astype(np.float32)
    c["axial_sin"] = np.sin(ang).astype(np.float32)
    tf = np.arange(T, dtype=np.float32)
    tn = tf / (T - 1)
    w = 2.0 * math.pi * tf / T
    f = np.linspace(1e-4, 15, 16, dtype=np.float32)
    fw = (w[:, None] * f).astype(np.float32)
    c["hy_pos"] = np.ascontiguousarray(np.concatenate([tn[:, None], np.cos(fw), -np.sin(fw)], -1).astype(np.float32).T)
    deltas = np.abs(np.linspace(math.log(1e-2) / 0.3, math.log(1e-2) / 1.5, 512, dtype=np.float32))
    win = np.exp(-tn[:, None] * deltas).astype(np.float32)
    c["hy_window"] = np.ascontiguousarray(win.reshape(TT, P, 512).transpose(1, 0, 2)).reshape(P, -1)
    k = np.arange(T)
    a = np.pi * ((2 * k[None, :] + 1) * np.arange(T)[:, None] % 1024) / 512.0
    cs = np.stack([np.cos(a), np.sin(a)])
    c["dft"] = np.ascontiguousarray(cs.reshape(2, TT, P, T).transpose(2, 1, 0, 3)).astype(np.float32).reshape(P, -1)
    c["idft"] = np.ascontiguousarray((cs / T).transpose(0, 2, 1).reshape(2, TT, P, T).transpose(2, 0, 1, 3)).astype(np.float32).reshape(P, -1)
    c["gla_order"] = np.zeros((1, 1), np.float32)
    del c["gla_order"]
    return c


CONST = constants()


def program(nc, A, out, dbg=None, stop=None):
    ctx = ExitStack()
    SEM0 = 120
    engines = list(nc.engines.keys())

    @contextmanager
    def stage(*names):
        sems = [nc.alloc_semaphore(name=f"{n}_{nc.next_id()}", num=SEM0 + k) for k, n in enumerate(names)]
        with nc.Block() as block:
            yield (block, *sems)
        nc.multi_engine_barrier(engines, sems_to_clear=range(SEM0, SEM0 + len(names)))
        for s in sems:
            nc.release_semaphore(s)

    def sb(c, name, shape, dt=F32):
        return c.enter_context(nc.sbuf_tensor(f"{name}_{nc.next_id()}", shape, dt))

    class Steps:
        def __init__(self, engine, sem):
            self.engine, self.sem, self.n = engine, sem, 0

        def did(self, inst):
            self.n += 1
            inst.then_inc(self.sem, 1)
            return self.n

        def settle(self, n=None):
            self.engine.wait_ge(self.sem, self.n if n is None else n)

    with ctx:
        ctx.enter_context(nc.allow_non_contiguous_dma(reason="small vectors"))
        ps = ctx.enter_context(nc.psum_tensor("ps", [P, 8, 512], F32))
        slots = sb(ctx, "slots", [P, NSLOT, 2048])
        res = sb(ctx, "res", [P, KD, T])
        hn = sb(ctx, "hn", [P, KD, T])
        K = {}
        for name, arr in CONST.items():
            K[name] = sb(ctx, name, list(arr.shape))
        ones = sb(ctx, "ones", [P, P])
        zeros = sb(ctx, "zeros", [P, 512], BF16)
        eye = K["eye"]

        def bank(b):
            return ps[:, b, :]

        def load(pairs):
            with stage("landed") as (block, landed):
                @block.sync
                def _(sp):
                    for dst, src in pairs[0::2]:
                        sp.dma_start(dst, src).then_inc(landed, 16)
                    sp.wait_ge(landed, 16 * len(pairs))

                @block.scalar
                def _(act):
                    for dst, src in pairs[1::2]:
                        act.dma_start(dst, src).then_inc(landed, 16)

        def linear(units):
            n = len(units)
            NB = 8
            by = {e: [j for j, u in enumerate(units) if u[3] == e] for e in ("act", "dve")}
            with stage(*[f"landed{s}" for s in range(NSLOT)], "products_done", "act_emptied", "dve_emptied") as (block, *sems):
                landed, (products_done, act_emptied, dve_emptied) = sems[:NSLOT], sems[NSLOT:]

                def slab(j):
                    w = units[j][1]
                    kt, cols = max(1, w.shape[0] // P), w.shape[1]
                    rows = min(P, w.shape[0])
                    return slots[0:rows, j % NSLOT, 0:kt * cols].rearrange("p (k n) -> p k n", k=kt)

                def fetch(q, j):
                    w = units[j][1]
                    if j >= NSLOT:
                        q.wait_ge(products_done, j - NSLOT + 1)
                    q.dma_start(slab(j), w.rearrange("(k p) n -> p k n", p=min(P, w.shape[0]))).then_inc(landed[j % NSLOT], 16)

                @block.sync
                def _(sp):
                    for j in range(n):
                        fetch(sp, j)

                @block.tensor
                def _(pe):
                    for j, (src, w, kind, _, _) in enumerate(units):
                        if j >= NB:
                            e = units[j - NB][3]
                            pe.wait_ge(act_emptied if e == "act" else dve_emptied, by[e].index(j - NB) + 1)
                        pe.wait_ge(landed[j % NSLOT], 16 * (j // NSLOT + 1))
                        ws, b = slab(j), bank(j % NB)
                        kt, cols = ws.shape[1], ws.shape[2]
                        if kind == "fm":
                            for m in range(0, cols, P):
                                mc = min(P, cols - m)
                                for k in range(kt):
                                    mm = pe.matmul(b[0:mc, m // P * T:(m // P + 1) * T], ws[:, k, m:m + mc], src[:, k, :],
                                                   start=(k == 0), stop=(k == kt - 1))
                        else:
                            for m in range(TT):
                                for k in range(kt):
                                    mm = pe.matmul(b[:, m * cols:(m + 1) * cols], src[:, k, m * P:(m + 1) * P], ws[:, k, :],
                                                   start=(k == 0), stop=(k == kt - 1))
                        mm.then_inc(products_done, 1)

                def empty(engine, e, sem):
                    for i, j in enumerate(by[e]):
                        engine.wait_ge(products_done, j + 1)
                        units[j][4](engine, bank(j % NB)).then_inc(sem, 1)

                @block.scalar
                def _(act):
                    empty(act, "act", act_emptied)

                @block.vector
                def _(dve):
                    empty(dve, "dve", dve_emptied)

        def copy_to(dst):
            rows, size = dst.shape[0], int(np.prod(dst.shape[1:]))
            def f(engine, b):
                src = b[0:rows, 0:size]
                if len(dst.shape) == 3:
                    src = src.rearrange("p (a n) -> p a n", a=dst.shape[1])
                if engine is nc.scalar or "calar" in type(engine).__name__ or "Activation" in str(engine.engine):
                    return nc.scalar.activation(dst, src, ACT.Copy)
                return nc.vector.tensor_copy(dst, src)
            return f

        def add_to(dst):
            def f(engine, b):
                src = b.rearrange("p (a n) -> p a n", a=dst.shape[1])
                return nc.vector.tensor_tensor(dst, dst, src, ALU.add)
            return f

        def fm_units(src, w, dst, first="act"):
            order = ["act", "dve"] if first == "act" else ["dve", "act"]
            u = []
            for i, c in enumerate(range(0, w.shape[1], UNIT)):
                cols = min(UNIT, w.shape[1] - c)
                d = dst[:, c // P:(c + cols) // P, :] if cols >= P else dst[0:cols, c // P, :]
                u.append((src, w[:, c:c + cols], "fm", order[i % 2], copy_to(d)))
            return u

        def residual_units(src, w):
            return [(src, w[:, c:c + UNIT], "fm", "dve", add_to(res[:, c // P:c // P + 2, :])) for c in range(0, D, UNIT)]

        def rmsnorm(parts):
            with ExitStack() as c, stage("squared", "summed", "shifted", "rooted", "inverted", "scaled") as \
                    (block, squared, summed, shifted, rooted, inverted, scaled):
                sq, ms, rs = [], [], []
                for i, (src, groups, mat, width, gain, dst) in enumerate(parts):
                    sq.append(slots[:, i, 0:src.shape[1] * T].rearrange("p (k n) -> p k n", n=T))
                    ms.append(slots[:, 4 + i, 0:len(groups) * T].rearrange("p (k n) -> p k n", n=T))
                    rs.append(ms[i])
                nb = 0
                area = []
                for part in parts:
                    g = len(part[1])
                    area.append(ps[:, nb:nb + (g + 1) // 2, :].rearrange("p b n -> p (b n)"))
                    nb += (g + 1) // 2

                @block.scalar
                def _(act):
                    for i, (src, groups, mat, width, gain, dst) in enumerate(parts):
                        act.activation(sq[i], src, ACT.Square).then_inc(squared, 1)
                    for i in range(len(parts)):
                        act.wait_ge(shifted, i + 1)
                        act.activation(ms[i], ms[i], ACT.Sqrt).then_inc(rooted, 1)

                @block.tensor
                def _(pe):
                    for i, (src, groups, mat, width, gain, dst) in enumerate(parts):
                        pe.wait_ge(squared, i + 1)
                        for g, tiles in enumerate(groups):
                            for k in tiles:
                                mm = pe.matmul(area[i][:, g * T:(g + 1) * T], mat[:, :], sq[i][:, k, :],
                                               start=(k == tiles[0]), stop=(k == tiles[-1]))
                        mm.then_inc(summed, 1)

                @block.vector
                def _(dve):
                    for i, (src, groups, mat, width, gain, dst) in enumerate(parts):
                        g = len(groups)
                        dve.wait_ge(summed, i + 1)
                        dve.tensor_scalar(flat(ms[i]), area[i][:, 0:g * T], 1.0 / width, EPS,
                                          ALU.mult, ALU.add).then_inc(shifted, 1)
                    done = 0
                    for i, (src, groups, mat, width, gain, dst) in enumerate(parts):
                        dve.wait_ge(rooted, i + 1)
                        dve.reciprocal(rs[i], ms[i]).then_inc(inverted, 1)
                        dve.wait_ge(inverted, i + 1)
                        for g, tiles in enumerate(groups):
                            for k in tiles:
                                dve.scalar_tensor_tensor(out=dst[:, k, :], in0=src[:, k, :], scalar=gain(k), in1=rs[i][:, g, :],
                                                         op0=ALU.mult, op1=ALU.mult).then_inc(scaled, 1)

        def norm_model(src, gain, dst):
            rmsnorm([(src[:, :, :], [list(range(KD))], ones, D, lambda k: gain[:, k:k + 1], dst)])

        def transposes(items):
            with stage("turned", "act_out", "dve_out") as (block, turned, act_out, dve_out):
                @block.tensor
                def _(pe):
                    for g, (srcs, dst) in enumerate(items):
                        if g >= 8:
                            pe.wait_ge(act_out if g % 2 == 0 else dve_out, (g - 8) // 2 + 1)
                        for src, col in srcs:
                            k, m = src.shape[0], src.shape[1]
                            mm = pe.transpose(bank(g % 8)[0:m, col:col + k], src, eye[0:k, 0:k])
                        mm.then_inc(turned, 1)

                def outs(g):
                    dst = items[g][1]
                    return dst, bank(g % 8)[0:dst.shape[0], 0:dst.shape[1]]

                @block.scalar
                def _(act):
                    for g in range(0, len(items), 2):
                        act.wait_ge(turned, g + 1)
                        dst, b = outs(g)
                        act.activation(dst, b, ACT.Copy).then_inc(act_out, 1)

                @block.vector
                def _(dve):
                    for g in range(1, len(items), 2):
                        dve.wait_ge(turned, g + 1)
                        dst, b = outs(g)
                        dve.tensor_copy(dst, b).then_inc(dve_out, 1)

        def flat(x):
            return x.rearrange("p a n -> p (a n)")

        def rotate(src, n, rot, cos, sin):
            with ExitStack() as c, stage("swapped", "sine_part", "cos_part", "turned") as (block, swapped, sine_part, cos_part, turned):
                t1 = slots[:, 7, 0:n * T].rearrange("p (k n) -> p k n", n=T)
                @block.tensor
                def _(pe):
                    for k in range(n):
                        pe.matmul(bank(k)[:, 0:T], rot[:, :], src[:, k, :], start=True, stop=True).then_inc(swapped, 1)
                @block.vector
                def _(dve):
                    for k in range(n):
                        dve.wait_ge(swapped, k + 1)
                        dve.tensor_tensor(t1[:, k, :], bank(k)[:, 0:T], sin, ALU.mult).then_inc(sine_part, 1)
                    for k in range(n):
                        dve.tensor_tensor(src[:, k, :], src[:, k, :], cos, ALU.mult).then_inc(cos_part, 1)
                    for k in range(n):
                        dve.wait_ge(sine_part, k + 1)
                        dve.wait_ge(cos_part, k + 1)
                        dve.tensor_tensor(src[:, k, :], src[:, k, :], t1[:, k, :], ALU.add).then_inc(turned, 1)

        def spread(pairs):
            with stage("made", "out") as (block, made, outed):
                @block.tensor
                def _(pe):
                    for i, (m, src, dst) in enumerate(pairs):
                        pe.matmul(bank(i)[:, 0:T], m, src, start=True, stop=True).then_inc(made, 1)
                @block.vector
                def _(dve):
                    for i, (m, src, dst) in enumerate(pairs):
                        dve.wait_ge(made, i + 1)
                        dve.tensor_copy(dst, bank(i)[:, 0:T]).then_inc(outed, 1)

        def attention(heads, scale, causal):
            U = [(h, q) for h in range(len(heads)) for q in range(TT)]
            with ExitStack() as c, stage("scored", "masked", "topped", "biased", "expd", "inverted", "weighted", "turned",
                                         "keys_first", "mixed", "out") as \
                    (block, scored, masked, topped, biased, expd, inverted, weighted, turned, keys_first, mixed, outed):
                work = slots[:, 6, :]
                s = work[:, 0:2 * T].rearrange("p (b n) -> p b n", b=2)
                pr = work[:, 2 * T:5 * T].rearrange("p (b n) -> p b n", b=3)
                pt = work[:, 5 * T:7 * T].rearrange("p (b k n) -> p b k n", b=2, k=TT)
                top = work[:, 7 * T:7 * T + 4].rearrange("p (b n) -> p b n", b=2)
                sm = work[:, 7 * T + 4:7 * T + 8].rearrange("p (b n) -> p b n", b=2)

                def keys(q):
                    return P * (q + 1) if causal else T

                @block.tensor
                def _(pe):
                    for i in range(len(U) + 2):
                        if i < len(U):
                            h, q = U[i]
                            if i >= 3:
                                pe.wait_ge(masked if causal else topped, i - 2)
                                if not causal:
                                    pe.wait_ge(expd, i - 2)
                            pairs = heads[h][0]
                            for n, (qq, kk) in enumerate(pairs):
                                mm = pe.matmul(bank(i % 3)[:, 0:keys(q)], qq[:, q * P:(q + 1) * P], kk[:, 0:keys(q)],
                                               start=(n == 0), stop=(n == len(pairs) - 1))
                            mm.then_inc(scored, 1)
                        if 0 <= i - 1 < len(U):
                            j = i - 1
                            h, q = U[j]
                            pe.wait_ge(weighted, j + 1)
                            if j >= 2:
                                pe.wait_ge(keys_first, j - 1)
                            for kt in range(keys(q) // P):
                                mm = pe.transpose(bank(3 + j % 2)[:, kt * P:(kt + 1) * P], pr[:, j % 3, kt * P:(kt + 1) * P], eye[:, :])
                            mm.then_inc(turned, 1)
                        if i - 2 >= 0:
                            j = i - 2
                            h, q = U[j]
                            _, v, base, dst = heads[h]
                            dv = dst.shape[0]
                            pe.wait_ge(keys_first, j + 1)
                            if j >= 2:
                                pe.wait_ge(outed, j - 1)
                            nk = keys(q) // P
                            for m in range(dst.shape[1]):
                                for kt in range(nk):
                                    mm = pe.matmul(bank(5 + j % 2)[base:base + dv, m * P:(m + 1) * P], v(kt, m), pt[:, j % 2, kt, :],
                                                   start=(kt == 0), stop=(kt == nk - 1))
                            mm.then_inc(mixed, 1)

                @block.vector
                def _(dve):
                    def finish(j):
                        dve.wait_ge(expd, j + 1)
                        dve.reciprocal(sm[:, j % 2, 1:2], sm[:, j % 2, 0:1]).then_inc(inverted, 1)
                        dve.wait_ge(inverted, j + 1)
                        n = keys(U[j][1])
                        dve.tensor_scalar(pr[:, j % 3, 0:n], pr[:, j % 3, 0:n], sm[:, j % 2, 1:2], None, ALU.mult).then_inc(weighted, 1)

                    for j, (h, q) in enumerate(U):
                        n = keys(q)
                        dve.wait_ge(scored, j + 1)
                        src = bank(j % 3)[:, 0:n]
                        if causal:
                            if j >= 2:
                                dve.wait_ge(expd, j - 1)
                            if q:
                                dve.tensor_copy(s[:, j % 2, 0:P], src[:, 0:P])
                            dve.tensor_tensor(s[:, j % 2, q * P:n], src[:, q * P:n], K["causal_add"][:, :], ALU.add).then_inc(masked, 1)
                            dve.wait_ge(masked, j + 1)
                            src = s[:, j % 2, 0:n]
                        if j >= 2:
                            dve.wait_ge(expd, j - 1)
                        dve.tensor_reduce(top[:, j % 2, 0:1], src, AX.X, ALU.max).then_inc(topped, 1)
                        dve.wait_ge(topped, j + 1)
                        dve.tensor_scalar(top[:, j % 2, 1:2], top[:, j % 2, 0:1], -scale, None, ALU.mult).then_inc(biased, 1)
                        if j >= 1:
                            finish(j - 1)
                    finish(len(U) - 1)

                @block.scalar
                def _(act):
                    def out(j):
                        h, q = U[j]
                        _, v, base, dst = heads[h]
                        dv = dst.shape[0]
                        act.wait_ge(mixed, j + 1)
                        nm = dst.shape[1]
                        act.activation(dst[:, :, q * P:(q + 1) * P], bank(5 + j % 2)[base:base + dv, 0:nm * P].rearrange("p (m n) -> p m n", m=nm),
                                       ACT.Copy).then_inc(outed, 1)

                    def turn(j):
                        n = keys(U[j][1])
                        act.wait_ge(turned, j + 1)
                        if j >= 2:
                            act.wait_ge(mixed, j - 1)
                        act.activation(flat(pt[:, j % 2, 0:n // P, :]), bank(3 + j % 2)[:, 0:n], ACT.Copy).then_inc(keys_first, 1)

                    for j, (h, q) in enumerate(U):
                        n = keys(q)
                        act.wait_ge(biased, j + 1)
                        if j >= 3:
                            act.wait_ge(turned, j - 2)
                        if j >= 2:
                            act.wait_ge(weighted, j - 1)
                        src = s[:, j % 2, 0:n] if causal else bank(j % 3)[:, 0:n]
                        act.activation(pr[:, j % 3, 0:n], src, ACT.Exp, bias=top[:, j % 2, 1:2], scale=scale,
                                       accum_out=sm[:, j % 2, 0:1]).then_inc(expd, 1)
                        if j >= 1:
                            turn(j - 1)
                        if j >= 2:
                            out(j - 2)
                    turn(len(U) - 1)
                    out(len(U) - 2)
                    out(len(U) - 1)

        CH = 256
        def mlp(src, gate, up, down, nchunk, outer=1, weight=None):
            G = gate is not None
            gate_banks = (4, 6)
            with ExitStack() as c, stage("gate_in0", "gate_in1", "up_in0", "up_in1", "down_in0", "down_in1", "cleared",
                                         "hidden_done", "activated", "hidden", "down_done", "weighted", "added") as \
                    (block, g0, g1, u0, u1, d0, d1, cleared, hidden_done, activated, hidden, down_done, weighted, added):
                gate_in, up_in, down_in = (g0, g1), (u0, u1), (d0, d1)
                sg = sb(c, "activated", [P, 2, 2, T])
                wsg = sb(c, "weighted", [P, 2, 2, T]) if weight else sg
                hid = sb(c, "hidden", [P, 2, 2, T])
                gs = [slots[:, b, :].rearrange("p (k n) -> p k n", k=KD) for b in (0, 1)]
                us = [slots[:, 2 + b, :].rearrange("p (k n) -> p k n", k=KD) for b in (0, 1)]
                ds = [slots[:, 4 + b, :].rearrange("p (k n) -> p k n", k=2) for b in (0, 1)]
                half = nchunk // 2
                total = outer * nchunk

                def loops(engine, body):
                    if outer == 1:
                        with engine.Fori(0, half) as i:
                            body(0, i, i)
                    else:
                        with engine.Fori(0, outer) as e:
                            with engine.Fori(0, half) as i:
                                body(e, i, e * half + i)

                @block.sync
                def _(sp):
                    def fetch(e, i, n, guard):
                        for b in (0, 1):
                            c = i * 2 + b
                            if guard:
                                sp.wait_ge(hidden_done, 2 * n + b - 1)
                            if G:
                                sp.dma_start(gs[b], gate(e, c)).then_inc(gate_in[b], 16)
                            sp.dma_start(us[b], up(e, c)).then_inc(up_in[b], 16)
                            if guard:
                                sp.wait_ge(down_done, 2 * n + b - 1)
                            sp.dma_start(ds[b], down(e, c)).then_inc(down_in[b], 16)
                    fetch(0, 0, 0, False)
                    if outer == 1:
                        with sp.Fori(1, half) as i:
                            fetch(0, i, i, True)
                    else:
                        with sp.Fori(1, half) as i:
                            fetch(0, i, i, True)
                        with sp.Fori(1, outer) as e:
                            with sp.Fori(0, half) as i:
                                fetch(e, i, e * half + i, True)

                @block.tensor
                def _(pe):
                    def first(b, n, c):
                        gb = gate_banks[b]
                        if G:
                            pe.wait_ge(gate_in[b], 16 * n + 16)
                            for m in range(2):
                                for k in range(KD):
                                    pe.matmul(bank(gb)[:, m * T:(m + 1) * T], gs[b][:, k, m * P:(m + 1) * P], src[:, k, :],
                                              start=(k == 0), stop=(k == KD - 1))
                        pe.wait_ge(up_in[b], 16 * n + 16)
                        for m in range(2):
                            for k in range(KD):
                                mm = pe.matmul(bank(gb + 1)[:, m * T:(m + 1) * T], us[b][:, k, m * P:(m + 1) * P], src[:, k, :],
                                               start=(k == 0), stop=(k == KD - 1))
                        mm.then_inc(hidden_done, 1)

                    def second(b, n):
                        pe.wait_ge(down_in[b], 16 * n + 16)
                        pe.wait_ge(hidden, 2 * n + b + 1)
                        for m in range(KD):
                            for k in range(2):
                                mm = pe.matmul(bank(m // 2)[:, m % 2 * T:(m % 2 + 1) * T], ds[b][:, k, m * P:(m + 1) * P],
                                               hid[:, b, k, :], start=False, stop=False, skip_group_check=True)
                        mm.then_inc(down_done, 1)

                    for b in range(4):
                        mm = pe.matmul(bank(b), zeros[:, 0:P], zeros[:, :], start=True, stop=True)
                    first(0, 0, 0)
                    with pe.Fori(0, total // 2 - 1) as n:
                        first(1, n, None)
                        second(0, n)
                        first(0, n + 1, None)
                        second(1, n)
                    last = total // 2 - 1
                    first(1, last, None)
                    second(0, last)
                    second(1, last)

                @block.scalar
                def _(act):
                    def body(e, i, n):
                        for b in (0, 1):
                            gb = gate_banks[b]
                            act.wait_ge(hidden_done, 2 * n + b + 1)
                            act.wait_ge(hidden, 2 * n + b + 1 - 2) if isinstance(n, int) and n > 0 else None
                            if G:
                                act.activation(flat(sg[:, b]), bank(gb), ACT.Silu).then_inc(activated, 1)
                            else:
                                act.activation(flat(sg[:, b]), bank(gb + 1), ACT.Relu).then_inc(activated, 1)
                    loops(act, body)

                @block.vector
                def _(dve):
                    def body(e, i, n):
                        for b in (0, 1):
                            dve.wait_ge(activated, 2 * n + b + 1)
                            if weight:
                                for m in range(2):
                                    dve.tensor_tensor(wsg[:, b, m, :], sg[:, b, m, :], weight(e), ALU.mult).then_inc(weighted, 1)
                                dve.wait_ge(weighted, 4 * n + 2 * b + 2)
                            dve.tensor_tensor(flat(hid[:, b]), bank(gate_banks[b] + 1), flat(wsg[:, b]), ALU.mult).then_inc(hidden, 1)
                    loops(dve, body)
                    dve.wait_ge(down_done, total)
                    for b in range(4):
                        dve.tensor_tensor(res[:, 2 * b:2 * b + 2, :], res[:, 2 * b:2 * b + 2, :],
                                          bank(b).rearrange("p (a n) -> p a n", a=2), ALU.add).then_inc(added, 1)

        def dump(name, ap):
            if dbg is None or name not in dbg:
                return
            with stage("saved") as (block, saved):
                @block.sync
                def _(sp):
                    sp.dma_start(dbg[name], ap).then_inc(saved, 16)
                    sp.wait_ge(saved, 16)

        def column(ap):
            return ap.rearrange("(k p) -> p k", p=P)

        with stage("set") as (block, set_):
            @block.gpsimd
            def _(pool):
                pool.memset(ones[:, :], 1.0).then_inc(set_, 1)
                pool.memset(zeros[:, :], 0.0).then_inc(set_, 1)
        load([(K[n][:, :], A["c_" + n]) for n in CONST])

        G = {}
        def vec(c, name, ap, n):
            G[name] = sb(c, name, [P, n])
            return (G[name][:, :], column(ap))

        with ExitStack() as c:
            x_tm = sb(c, "x_tm", [P, TT, D])
            load([(x_tm[:, :, :], A["x"][0].rearrange("(t p) d -> p t d", p=P))])
            transposes([([(x_tm[:, t, k * P:(k + 1) * P], kk * T + t * P) for kk, k in enumerate((2 * g, 2 * g + 1)) for t in range(TT)],
                         flat(res[:, 2 * g:2 * g + 2, :])) for g in range(KD // 2)])
        load([vec(ctx, "norm_mix0", A["norm_mix"][0], KD), vec(ctx, "norm_mix1", A["norm_mix"][1], KD),
              vec(ctx, "norm_ffn0", A["norm_ffn"][0], KD), vec(ctx, "norm_ffn1", A["norm_ffn"][1], KD),
              vec(ctx, "final_norm", A["final_norm"], KD)])
        dump("x", res[:, :, :])

        with ExitStack() as c:
            cos = sb(c, "cos", [P, T])
            sin = sb(c, "sin", [P, T])
            load([vec(c, "q_norm", A["mla_q_norm"][0], 2), vec(c, "kv_norm", A["mla_kv_norm"][0], 1)])
            with ExitStack() as c2:
                pos = sb(c2, "pos", [P, T], I32)
                load([(pos[:, :], A["positions"][0].partition_broadcast(P))])
                ang, nn, rr = sb(c2, "ang", [P, 2, T]), sb(c2, "turns", [P, 2, T]), sb(c2, "reduced", [P, 2, T])
                posf = sb(c2, "posf", [P, T])
                with stage("step", "sined") as (block, step, sined):
                    @block.vector
                    def _(dve):
                        st = Steps(dve, step)
                        st.did(dve.tensor_copy(posf[:, :], pos[:, :])); st.settle()
                        st.did(dve.tensor_scalar(ang[:, 1, :], posf[:, :], K["inv_freq"][:, 0:1], None, ALU.mult)); st.settle()
                        st.did(dve.tensor_scalar(ang[:, 0, :], ang[:, 1, :], math.pi / 2, None, ALU.add)); st.settle()
                        reduce_angle(dve, st, flat(ang[:, :, :]), flat(nn[:, :, :]), flat(rr[:, :, :]))
                    @block.scalar
                    def _(act):
                        act.wait_ge(step, 3 + REDUCE_STEPS)
                        act.activation(cos[:, :], rr[:, 0, :], ACT.Sin).then_inc(sined, 1)
                        act.activation(sin[:, :], rr[:, 1, :], ACT.Sin).then_inc(sined, 1)
            norm_model(res, G["norm_mix0"], hn)
            with ExitStack() as c1:
                lat = sb(c1, "latents", [P, 4, T])
                w = A["mla_w_in"][0]
                linear([(hn, w[:, 0:256], "fm", "act", copy_to(lat[:, 0:2, :])),
                        (hn, w[:, 256:384], "fm", "dve", copy_to(lat[:, 2, :])),
                        (hn, w[:, 384:448], "fm", "act", copy_to(lat[0:64, 3, :]))])
                rmsnorm([(lat[:, 0:2, :], [[0, 1]], ones, 256, lambda k: G["q_norm"][:, k:k + 1], lat[:, 0:2, :]),
                         (lat[:, 2:3, :], [[0]], ones, 128, lambda k: G["kv_norm"][:, 0:1], lat[:, 2:3, :])])
                qn = sb(c1, "q_nope", [P, 8, T])
                qr = sb(c1, "q_rope", [P, 4, T])
                kn = sb(c1, "k_nope", [P, 8, T])
                kr = sb(c1, "k_rope", [P, 1, T])
                vv = sb(c1, "v", [P, TT, 8 * P])
                spread([(K["twice0"][0:64, :], lat[0:64, 3, :], kr[:, 0, :])])
                wq, wkv = A["mla_w_qb"][0], A["mla_w_kvb"][0]
                un = []
                for h in range(8):
                    un.append((lat[:, 0:2, :], wq[:, h * 192:h * 192 + 128], "fm", ("act", "dve")[h % 2], copy_to(qn[:, h, :])))
                for h in range(8):
                    lo = h % 2 * 64
                    un.append((lat[:, 0:2, :], wq[:, h * 192 + 128:h * 192 + 192], "fm", "dve", copy_to(qr[lo:lo + 64, h // 2, :])))
                for h in range(8):
                    un.append((lat[:, 2:3, :], wkv[:, h * 256:h * 256 + 128], "fm", ("act", "dve")[h % 2], copy_to(kn[:, h, :])))
                for h in range(8):
                    un.append((lat[:, 2:3, :], wkv[:, h * 256 + 128:h * 256 + 256], "tm", ("act", "dve")[h % 2],
                               copy_to(vv[:, :, h * P:(h + 1) * P])))
                linear(un)
                rotate(qr, 4, K["rot32"], cos[:, :], sin[:, :])
                rotate(kr, 1, K["rot32"], cos[:, :], sin[:, :])
                o = sb(c1, "o", [P, 8, T])
                hd = []
                for h in range(8):
                    lo = h % 2 * 64
                    hd.append(([(qn[:, h, :], kn[:, h, :]), (qr[lo:lo + 64, h // 2, :], kr[lo:lo + 64, 0, :])],
                               (lambda kt, m, h=h: vv[:, kt, h * P:(h + 1) * P]), 0, o[:, h:h + 1, :]))
                attention(hd, 192 ** -0.5, True)
                linear(residual_units(o, A["mla_w_out"][0]))
        dump("mla", res[:, :, :])

        def rows(w):
            return w.rearrange("(k p) n -> p k n", p=P)

        norm_model(res, G["norm_ffn0"], hn)
        wg, wu, wd = A["ffn_w_gate"][0], A["ffn_w_up"][0], A["ffn_w_down"][0]
        mlp(hn, lambda e, c: rows(wg)[:, :, bass.ds(c * CH, CH)], lambda e, c: rows(wu)[:, :, bass.ds(c * CH, CH)],
            lambda e, c: rows(wd)[:, bass.ds(c * 2, 2), :], 3584 // CH)
        dump("ffn", res[:, :, :])
        if stop == "ffn":
            return
        norm_model(res, G["norm_mix1"], hn)
        with ExitStack() as c:
            NH = 8
            w = A["mlstm_w_in"][0]
            load([vec(c, "head_norm", A["mlstm_head_norm"][0], 8), vec(c, "conv_b", A["mlstm_conv_b"][0], 8)])
            conv_w = sb(c, "conv_w", [P, 4, 8])
            gate_b = sb(c, "gate_b", [8, 2])
            load([(conv_w[:, j, :], column(A["mlstm_conv_w"][0][j])) for j in range(4)]
                 + [(gate_b[:, :], A["mlstm_gate_b"][0].rearrange("(a p) -> p a", p=8))])
            og = sb(c, "out_gate", [P, 8, T])
            v = sb(c, "v", [P, TT, D])
            raw = sb(c, "qk_raw", [P, 8, 3 + T])
            qk = sb(c, "qk", [P, 8, T])
            gi = sb(c, "gi", [8, T])
            gf = sb(c, "gf", [8, T])
            hh = sb(c, "h", [P, 8, T])
            with stage("padded") as (block, padded):
                @block.gpsimd
                def _(pool):
                    pool.memset(raw[:, :, 0:3], 0.0).then_inc(padded, 1)
            un = []
            for k in range(4):
                un.append((hn, w[:, k * 256:(k + 1) * 256], "fm", ("act", "dve")[k % 2], copy_to(raw[:, 2 * k:2 * k + 2, 3:3 + T])))
            for k in range(4):
                un.append((hn, w[:, 1024 + k * 256:1024 + (k + 1) * 256], "tm", "dve", copy_to(v[:, :, k * 256:(k + 1) * 256])))
            for k in range(4):
                def gate_out(engine, b, k=k):
                    return nc.scalar.activation(flat(og[:, 2 * k:2 * k + 2, :]), b, ACT.Sigmoid)
                un.append((hn, w[:, 2048 + k * 256:2048 + (k + 1) * 256], "fm", "act", gate_out))
            un.append((hn, w[:, 3072:3080], "fm", "dve", copy_to(gi[:, :])))
            un.append((hn, w[:, 3080:3088], "fm", "dve", copy_to(gf[:, :])))
            linear(un)
            one8 = sb(c, "one8", [8, T])
            bb = sb(c, "bias15", [8, 2])
            B_neg, u, M, em = (sb(c, n, [8, T]) for n in ("B_neg", "u", "M", "em"))
            with stage("conv_step", "convolved", "smooth", "step", "bias_ready", "tanhed", "forget", "last_scan", "floor") as \
                    (block, conv_step, convolved, smooth, step, bias_ready, tanhed, forget, last_scan, floor):
                @block.vector
                def _(dve):
                    st = Steps(dve, step)
                    dve.tensor_scalar(bb[:, :], gate_b[:, :], 1.0 / 15.0, None, ALU.mult).then_inc(bias_ready, 1)
                    st.did(dve.memset(one8[:, :], 1.0))
                    cs = Steps(dve, conv_step)
                    for j in range(4):
                        for k in range(8):
                            src, acc = raw[:, k, j:j + T], qk[:, k, :]
                            if j == 0:
                                cs.did(dve.tensor_scalar(acc, src, conv_w[:, 0, k:k + 1], None, ALU.mult))
                            else:
                                cs.settle(8 * (j - 1) + k + 1)
                                inst = dve.scalar_tensor_tensor(out=acc, in0=src, scalar=conv_w[:, j, k:k + 1], in1=acc, op0=ALU.mult, op1=ALU.add)
                                if j == 3:
                                    inst.then_inc(convolved, 1)
                                else:
                                    cs.did(inst)
                    dve.wait_ge(forget, 2)
                    st.settle()
                    st.did(dve.tensor_tensor_scan(B_neg[:, :], one8[:, :], gf[:, :], 0.0, ALU.mult, ALU.add)); st.settle()
                    st.did(dve.scalar_tensor_tensor(out=u[:, :], in0=gi[:, :], scalar=15.0, in1=B_neg[:, :], op0=ALU.mult, op1=ALU.add)); st.settle()
                    st.did(dve.tensor_tensor_scan(M[:, :], one8[:, :], u[:, :], 0.0, ALU.mult, ALU.max)); st.settle()
                    dve.tensor_tensor(em[:, :], B_neg[:, :], M[:, :], ALU.subtract).then_inc(last_scan, 1)

                @block.scalar
                def _(act):
                    act.wait_ge(bias_ready, 1)
                    act.activation(gf[:, :], gf[:, :], ACT.Tanh, bias=bb[:, 1:2], scale=1.0 / 15.0).then_inc(tanhed, 1)
                    act.activation(gi[:, :], gi[:, :], ACT.Tanh, bias=bb[:, 0:1], scale=1.0 / 15.0).then_inc(tanhed, 1)
                    act.wait_ge(tanhed, 2)
                    act.activation(gf[:, :], gf[:, :], ACT.Exp, scale=-15.0).then_inc(forget, 1)
                    act.wait_ge(forget, 1)
                    act.activation(gf[:, :], gf[:, :], ACT.Ln, bias=1.0).then_inc(forget, 1)
                    act.wait_ge(last_scan, 1)
                    act.activation(em[:, :], em[:, :], ACT.Exp).then_inc(floor, 1)
                    for k in range(8):
                        act.wait_ge(convolved, k + 1)
                        act.activation(qk[:, k, :], qk[:, k, :], ACT.Silu, bias=G["conv_b"][:, k:k + 1]).then_inc(smooth, 1)
            Mb = sb(c, "M_all", [P, 8, T])
            Eb = sb(c, "floor_all", [P, 8, T])
            uT = sb(c, "u_col", [P, TT, 8])
            sel = K["row_select"][:, :].rearrange("p (h n) -> p h n", h=8)
            spread([(sel[:, h, :], M[:, :], Mb[:, h, :]) for h in range(8)])
            spread([(sel[:, h, :], em[:, :], Eb[:, h, :]) for h in range(8)])
            transposes([([(u[:, t * P:(t + 1) * P], 0)], uT[:, t, :]) for t in range(TT)])
            W3 = T + P
            gt = sb(c, "decay", [P, 8, W3])
            dn = sb(c, "divisor", [P, 8, T])
            keep = K["keep_st"][:, 0:P]
            with stage("margin", "decayed", "kept", "scored", "weighted", "summed", "absolute", "bounded", "inverted", "normed") as \
                    (block, margin, decayed, kept, scored, weighted, summed, absolute, bounded, inverted, normed):
                @block.tensor
                def _(pe):
                    for h in range(NH):
                        lo = h % 2 * 64
                        q_, k_ = qk[lo:lo + 64, h // 2, :], qk[lo:lo + 64, 4 + h // 2, :]
                        pe.matmul(bank(h)[:, 0:T], k_[:, 0:P], q_, start=True, stop=True)
                        pe.matmul(bank(h)[:, T:W3], k_[:, P:T], q_[:, P:T], start=True, stop=True).then_inc(scored, 1)
                    for h in range(NH):
                        pe.wait_ge(weighted, h + 1)
                        for dst, lhs in ((bank(h)[:, 0:T], lambda kt: v[:, kt, h * P:(h + 1) * P]), (bank(h)[:, T:2 * T], lambda kt: ones[:, :])):
                            pe.matmul(dst, lhs(0), gt[:, h, 0:T], start=True, stop=True)
                            mm = pe.matmul(dst[:, P:T], lhs(1), gt[:, h, T:W3], start=False, stop=True, skip_group_check=True)
                        mm.then_inc(summed, 1)

                @block.vector
                def _(dve):
                    for h in range(NH):
                        dve.tensor_scalar(gt[:, h, 0:T], Mb[:, h, :], uT[:, 0, h:h + 1], 0.0, ALU.subtract, ALU.max).then_inc(margin, 1)
                        dve.tensor_scalar(gt[:, h, T:W3], Mb[:, h, P:T], uT[:, 1, h:h + 1], 0.0, ALU.subtract, ALU.max).then_inc(margin, 1)
                    for h in range(NH):
                        dve.wait_ge(decayed, h + 1)
                        dve.tensor_tensor(gt[:, h, 0:P], gt[:, h, 0:P], keep, ALU.mult).then_inc(kept, 1)
                        dve.tensor_tensor(gt[:, h, T:W3], gt[:, h, T:W3], keep, ALU.mult).then_inc(kept, 1)
                        dve.wait_ge(scored, h + 1)
                        dve.wait_ge(kept, 2 * h + 2)
                        dve.scalar_tensor_tensor(out=gt[:, h, :], in0=bank(h)[:, 0:W3], scalar=64 ** -0.5, in1=gt[:, h, :],
                                                 op0=ALU.mult, op1=ALU.mult).then_inc(weighted, 1)
                    for h in range(NH):
                        dve.wait_ge(absolute, h + 1)
                        dve.tensor_tensor(dn[:, h, :], dn[:, h, :], Eb[:, h, :], ALU.max).then_inc(bounded, 1)
                        dve.wait_ge(bounded, h + 1)
                        dve.reciprocal(dn[:, h, :], dn[:, h, :]).then_inc(inverted, 1)
                        dve.wait_ge(inverted, h + 1)
                        dve.tensor_tensor(hh[:, h, :], bank(h)[:, 0:T], dn[:, h, :], ALU.mult).then_inc(normed, 1)

                @block.scalar
                def _(act):
                    for h in range(NH):
                        act.wait_ge(margin, 2 * h + 2)
                        act.activation(gt[:, h, :], gt[:, h, :], ACT.Exp, scale=-1.0).then_inc(decayed, 1)
                    for h in range(NH):
                        act.wait_ge(summed, h + 1)
                        act.activation(dn[:, h, :], bank(h)[:, T:2 * T], ACT.Abs).then_inc(absolute, 1)
            rmsnorm([(hh[:, :, :], [[k] for k in range(8)], ones, 128, lambda k: G["head_norm"][:, k:k + 1], hh)])
            with stage("gated") as (block, gated):
                @block.vector
                def _(dve):
                    dve.tensor_tensor(flat(hh[:, :, :]), flat(hh[:, :, :]), flat(og[:, :, :]), ALU.mult).then_inc(gated, 1)
            linear(residual_units(hh, A["mlstm_w_out"][0]))
        dump("mlstm", res[:, :, :])
        if stop == "mlstm":
            return

        norm_model(res, G["norm_ffn1"], hn)
        NE = 8
        with ExitStack() as c:
            CB = sb(c, "expert_weights", [P, NE, T])
            with ExitStack() as c1:
                lg = sb(c1, "logits", [P, TT, NE])
                linear([(hn, A["moe_router"][0], "tm", "act", copy_to(lg[:, :, :]))])
                top, idx, idf = sb(c1, "top", [P, TT, 8]), sb(c1, "index", [P, TT, 8], U32), sb(c1, "indexf", [P, TT, 8])
                number, oh, gg = sb(c1, "number", [P, NE]), sb(c1, "chosen", [P, 2, TT, NE]), sb(c1, "shares", [P, TT, 4])
                cw = sb(c1, "combine", [P, TT, NE])
                with stage("numbered", "step", "differed", "expd") as (block, numbered, step, differed, expd):
                    @block.gpsimd
                    def _(pool):
                        pool.iota(number[:, :], [[1, NE]], base=0, channel_multiplier=0, allow_small_or_imprecise_dtypes=True).then_inc(numbered, 1)

                    @block.vector
                    def _(dve):
                        st = Steps(dve, step)
                        for t in range(TT):
                            st.did(dve.max(out=top[:, t, :], in_=lg[:, t, :])); st.settle()
                            st.did(dve.max_index(out=idx[:, t, :], in_max=top[:, t, :], in_values=lg[:, t, :])); st.settle()
                        st.did(dve.tensor_copy(idf[:, :, :], idx[:, :, :])); st.settle()
                        for t in range(TT):
                            dve.tensor_tensor(gg[:, t, 0:1], top[:, t, 1:2], top[:, t, 0:1], ALU.subtract).then_inc(differed, 1)
                        dve.wait_ge(numbered, 1)
                        for t in range(TT):
                            for j in range(2):
                                st.did(dve.tensor_scalar(oh[:, j, t, :], number[:, :], idf[:, t, j:j + 1], None, ALU.is_equal))
                        dve.wait_ge(expd, 1)
                        st.did(dve.tensor_scalar(gg[:, :, 2:3], gg[:, :, 1:2], 1.0, None, ALU.add)); st.settle()
                        st.did(dve.reciprocal(gg[:, :, 2:3], gg[:, :, 2:3])); st.settle()
                        st.did(dve.tensor_tensor(gg[:, :, 3:4], gg[:, :, 2:3], gg[:, :, 1:2], ALU.mult)); st.settle()
                        for t in range(TT):
                            st.did(dve.tensor_scalar(cw[:, t, :], oh[:, 0, t, :], gg[:, t, 2:3], None, ALU.mult)); st.settle()
                            st.did(dve.scalar_tensor_tensor(out=cw[:, t, :], in0=oh[:, 1, t, :], scalar=gg[:, t, 3:4], in1=cw[:, t, :],
                                                            op0=ALU.mult, op1=ALU.add))

                    @block.scalar
                    def _(act):
                        act.wait_ge(differed, 2)
                        act.activation(gg[:, :, 1:2], gg[:, :, 0:1], ACT.Exp).then_inc(expd, 1)
                cwT = sb(c1, "combine_t", [NE, T])
                transposes([([(cw[:, t, :], t * P) for t in range(TT)], cwT[:, :])])
                spread([(K["row_select"][:, e * P:(e + 1) * P], cwT[:, :], CB[:, e, :]) for e in range(NE)])
            eg, eu = (A[n][0].rearrange("e (k p) n -> p e k n", p=P) for n in ("moe_w_gate", "moe_w_up"))
            ed = A["moe_w_down"][0].rearrange("e (k p) n -> p e k n", p=P)

            def expert(w, e):
                return w[:, bass.ds(e, 1)].rearrange("p e k n -> p (e k) n")
            mlp(hn, lambda e, c: expert(eg, e)[:, :, bass.ds(c * CH, CH)], lambda e, c: expert(eu, e)[:, :, bass.ds(c * CH, CH)],
                lambda e, c: expert(ed, e)[:, bass.ds(c * 2, 2), :], 3584 // CH, outer=NE,
                weight=lambda e: CB[:, bass.ds(e, 1), :].rearrange("p e n -> p (e n)"))
        dump("moe", res[:, :, :])
        norm_model(res, G["final_norm"], res)
        dump("block1", res[:, :, :])
        if stop == "block1":
            return

        memT = sb(ctx, "memory", [P, KD, T])
        with ExitStack() as c:
            m_tm = sb(c, "m_tm", [P, TT, D])
            load([(m_tm[:, :, :], A["mem_2"][0].rearrange("(t p) d -> p t d", p=P))])
            transposes([([(m_tm[:, t, k * P:(k + 1) * P], kk * T + t * P) for kk, k in enumerate((2 * g, 2 * g + 1)) for t in range(TT)],
                         flat(memT[:, 2 * g:2 * g + 2, :])) for g in range(KD // 2)])

        def layer(L):
            def of(name):
                ap = A[name][bass.ds(L, 1)]
                n = len(ap.shape)
                return ap.rearrange({2: "a k -> (a k)", 3: "a k n -> (a k) n", 4: "a b k n -> (a b) k n"}[n])

            with ExitStack() as c:
                w_in = of("w_in_2")
                for n, name, k in (("ln_mix", "ln_mix_2", 8), ("onorm", "gla_onorm_2", 1)):
                    G[n] = sb(c, n, [P, k])
                qg, kg = sb(c, "q_gain", [P, 1]), sb(c, "k_gain", [P, 1])
                hconv = sb(c, "hy_conv", [P, 3, 12])
                skip = sb(c, "skip", [P, 2, 4])
                w1, w2, w3 = sb(c, "hy_w1", [33, 64]), sb(c, "hy_w2", [64, 64]), sb(c, "hy_w3", [65, 2048])
                hb, hf = sb(c, "hy_b", [64, 2]), sb(c, "hy_freq", [64, 2])
                wlr = sb(c, "w_lr", [32, 2, 256])
                blr = sb(c, "b_lr", [P, 2, 2])
                with stage("cleared") as (block, cleared):
                    @block.gpsimd
                    def _(pool):
                        pool.memset(wlr[:, :, :], 0.0).then_inc(cleared, 1)
                load([(G["ln_mix"][:, :], column(of("ln_mix_2"))), (G["onorm"][:, :], column(of("gla_onorm_2"))),
                      *[(g[o:o + 64, :], of(n).rearrange("(p a) -> p a", a=1)) for g, n in ((qg, "attn_qnorm_2"), (kg, "attn_knorm_2")) for o in (0, 64)],
                      *[(hconv[:, j, :], column(of("hy_conv_2")[j])) for j in range(3)],
                      *[(skip[:, j, :], column(of("hy_skip_2")[j])) for j in range(2)],
                      (w1[:, :], of("hy_w1_2")), (w2[:, :], of("hy_w2_2")), (w3[0:64, :], of("hy_w3_2")),
                      (w3[64:65, :], of("hy_b3_2").rearrange("(a n) -> a n", a=1)),
                      (hb[:, 0:1], of("hy_b1_2").rearrange("(p a) -> p a", a=1)), (hb[:, 1:2], of("hy_b2_2").rearrange("(p a) -> p a", a=1)),
                      *[(hf[:, j:j + 1], of("hy_freq_2")[j].rearrange("(p a) -> p a", a=1)) for j in range(2)],
                      *[(wlr[16 * d:16 * d + 16, d, :], of("gla_w_lr_2")[d]) for d in range(2)],
                      *[(blr[:, d, :], column(of("gla_b_lr_2")[d])) for d in range(2)]])

                norm_model(res, G["ln_mix"], hn)
                gates = sb(c, "gates", [P, 24, T])
                oa, oh_, og = (sb(c, n, [P, 4, T]) for n in ("o_attn", "o_hyena", "o_gla"))
                with ExitStack() as c1:
                    hc = sb(c1, "hy_convolved", [P, 12, T])
                    with ExitStack() as c2:
                        hy = sb(c2, "hy", [P, 12, T + 2])
                        gq, gk = sb(c2, "gq", [P, 2, T]), sb(c2, "gk", [P, 2, T])
                        gv = sb(c2, "gv", [P, TT, 512])
                        lr = sb(c2, "lr", [32, T])
                        with ExitStack() as c3:
                            aq, ak, av = sb(c3, "aq", [P, 4, T]), sb(c3, "ak", [P, 1, T]), sb(c3, "av", [P, TT, P])
                            with stage("padded") as (block, padded):
                                @block.gpsimd
                                def _(pool):
                                    pool.memset(hy[:, :, 0:1], 0.0).then_inc(padded, 1)
                                    pool.memset(hy[:, :, T + 1:T + 2], 0.0).then_inc(padded, 1)
                            un = []

                            def add(kind, lo, hi, dst, step=UNIT):
                                for n, x in enumerate(range(lo, hi, step)):
                                    un.append((hn, w_in[:, x:min(x + step, hi)], kind, ("act", "dve")[len(un) % 2], copy_to(dst(n))))
                            add("fm", 0, 512, lambda n: aq[:, 2 * n:2 * n + 2, :])
                            add("fm", 512, 640, lambda n: ak[:, 0, :])
                            add("tm", 640, 768, lambda n: av[:, :, :])
                            add("fm", 768, 2304, lambda n: hy[:, 2 * n:2 * n + 2, 1:T + 1])
                            add("fm", 2304, 2560, lambda n: gq[:, :, :])
                            add("fm", 2560, 2816, lambda n: gk[:, :, :])
                            add("tm", 2816, 3328, lambda n: gv[:, :, n * 256:(n + 1) * 256])
                            for n in range(2):
                                def silu_out(engine, b, n=n):
                                    return nc.scalar.activation(flat(og[:, 2 * n:2 * n + 2, :]), b, ACT.Silu)
                                un.append((hn, w_in[:, 3328 + n * 256:3584 + n * 256], "fm", "act", silu_out))
                            add("fm", 3840, 3872, lambda n: lr[:, :])
                            for n in range(12):
                                def sigmoid_out(engine, b, n=n):
                                    return nc.scalar.activation(flat(gates[:, 2 * n:2 * n + 2, :]), b, ACT.Sigmoid)
                                un.append((hn, w_in[:, 3872 + n * 256:4128 + n * 256], "fm", "act", sigmoid_out))
                            linear(un)

                            rmsnorm([(aq[:, :, :], [[k] for k in range(4)], K["blocks64"], 64, lambda k: qg[:, 0:1], aq),
                                     (ak[:, :, :], [[0]], K["blocks64"], 64, lambda k: kg[:, 0:1], ak)])
                            rotate(aq, 4, K["rot16"], K["axial_cos"][:, :], K["axial_sin"][:, :])
                            rotate(ak, 1, K["rot16"], K["axial_cos"][:, :], K["axial_sin"][:, :])
                            kk = sb(c3, "k_twice", [P, 2, T])
                            spread([(K["twice0"][:, :], ak[:, 0, :], kk[:, 0, :]), (K["twice1"][:, :], ak[:, 0, :], kk[:, 1, :])])
                            hd = []
                            for h in range(8):
                                lo, g = h % 2 * 64, h // 4
                                hd.append(([(aq[lo:lo + 64, h // 2, :], kk[lo:lo + 64, g, :])],
                                           (lambda kt, m, g=g: av[:, kt, g * 64:(g + 1) * 64]), lo, oa[lo:lo + 64, h // 2:h // 2 + 1, :]))
                            attention(hd, 64 ** -0.5, False)
                        with stage("tap", "convolved") as (block, tap, convolved):
                            @block.vector
                            def _(dve):
                                st = Steps(dve, tap)
                                for j in range(3):
                                    for k in range(12):
                                        src, acc = hy[:, k, j:j + T], hc[:, k, :]
                                        if j == 0:
                                            st.did(dve.tensor_scalar(acc, src, hconv[:, 0, k:k + 1], None, ALU.mult))
                                        else:
                                            st.settle(12 * (j - 1) + k + 1)
                                            st.did(dve.scalar_tensor_tensor(out=acc, in0=src, scalar=hconv[:, j, k:k + 1], in1=acc,
                                                                            op0=ALU.mult, op1=ALU.add))
                        gla(c2, gq, gk, gv, lr, wlr, blr, og)
                    hyena(c1, hc, skip, w1, w2, w3, hb, hf, oh_)
                for i, name in ((L, None),):
                    dumpl("att", oa); dumpl("hyena", oh_); dumpl("gla", og)

                un = []
                for b, (src, wn) in enumerate(((oa, "w_br_attn_2"), (oh_, "w_br_hyena_2"), (og, "w_br_gla_2"))):
                    wb = of(wn)
                    for n in range(4):
                        def gated(engine, bk, k=8 * b + 2 * n):
                            return nc.vector.tensor_tensor(flat(gates[:, k:k + 2, :]), flat(gates[:, k:k + 2, :]), bk, ALU.mult)
                        un.append((src, wb[:, n * 256:(n + 1) * 256], "fm", "dve", gated))
                linear(un)
                with stage("two", "three") as (block, two, three):
                    @block.vector
                    def _(dve):
                        for n in range(4):
                            dve.tensor_tensor(gates[:, 2 * n:2 * n + 2, :], gates[:, 2 * n:2 * n + 2, :], gates[:, 8 + 2 * n:10 + 2 * n, :], ALU.add).then_inc(two, 1)
                        for n in range(4):
                            dve.wait_ge(two, n + 1)
                            dve.tensor_tensor(gates[:, 2 * n:2 * n + 2, :], gates[:, 2 * n:2 * n + 2, :], gates[:, 16 + 2 * n:18 + 2 * n, :], ALU.add).then_inc(three, 1)
                dumpl("mixed", gates[:, 0:8, :])
                linear(residual_units(gates[:, 0:8, :], of("w_out_2")))
            dumpl("mix", res)

            with ExitStack() as c:
                for n, name, k in (("ln_x", "ln_x_2", 8), ("ln_mem", "ln_mem_2", 8), ("x_qnorm", "x_qnorm_2", 2), ("x_knorm", "x_knorm_2", 2), ("ln_mlp", "ln_mlp_2", 8)):
                    G[n] = sb(c, n, [P, k])
                load([(G[n][:, :], column(of(n + "_2"))) for n in ("ln_x", "ln_mem", "x_qnorm", "x_knorm", "ln_mlp")])
                with ExitStack() as c1:
                    mn = sb(c1, "memory_normed", [P, KD, T])
                    rmsnorm([(res[:, :, :], [list(range(KD))], ones, D, lambda k: G["ln_x"][:, k:k + 1], hn),
                             (memT[:, :, :], [list(range(KD))], ones, D, lambda k: G["ln_mem"][:, k:k + 1], mn)])
                    q, k_, v = sb(c1, "q", [P, 8, T]), sb(c1, "k", [P, 8, T]), sb(c1, "v", [P, TT, D])
                    wv = of("x_wv_2")
                    linear(fm_units(hn, of("x_wq_2"), q) + fm_units(mn, of("x_wk_2"), k_)
                           + [(mn, wv[:, n * 256:(n + 1) * 256], "tm", ("act", "dve")[n % 2], copy_to(v[:, :, n * 256:(n + 1) * 256])) for n in range(4)])
                    pairs = [[0, 1], [2, 3], [4, 5], [6, 7]]
                    rmsnorm([(q[:, :, :], pairs, ones, 256, lambda k: G["x_qnorm"][:, k % 2:k % 2 + 1], q),
                             (k_[:, :, :], pairs, ones, 256, lambda k: G["x_knorm"][:, k % 2:k % 2 + 1], k_)])
                    hd = [([(q[:, 2 * h + j, :], k_[:, 2 * h + j, :]) for j in range(2)],
                           (lambda kt, m, h=h: v[:, kt, (2 * h + m) * P:(2 * h + m + 1) * P]), 0, hn[:, 2 * h:2 * h + 2, :]) for h in range(4)]
                    attention(hd, 256 ** -0.5, False)
                    linear(residual_units(hn, of("x_wo_2")))
                dumpl("cross", res)
                norm_model(res, G["ln_mlp"], hn)
            m1, m2 = rows(of("mlp_w1_2")), rows(of("mlp_w2_2"))
            mlp(hn, None, lambda e, c: m1[:, :, bass.ds(c * CH, CH)], lambda e, c: m2[:, bass.ds(c * 2, 2), :], 4096 // CH)

        def dumpl(name, ap):
            if dbg is None or name + "0" not in dbg:
                return
            with stage("saved") as (block, saved):
                @block.sync
                def _(sp):
                    sp.dma_start(dbg[name + "0"], ap[:, :, :]).then_inc(saved, 16)
                    sp.wait_ge(saved, 16)

        def gla(c, gq, gk, gv, lr, wlr, blr, og):
            NC, H = 4, 4
            with ExitStack() as c:
                def scratch(slot, half, *dims):
                    size = int(np.prod(dims))
                    names = "abc"[:len(dims)]
                    return slots[:, slot, half * 1024:half * 1024 + size].rearrange(
                        f"p ({' '.join(names)}) -> p {' '.join(names)}", **dict(zip(names, dims)))
                x, a, g, b = (scratch(n, 0, 4, T) for n in range(4))
                tot = sb(c, "total", [P, 4, NC])
                dec = sb(c, "chunk_decay", [P, 4, NC])
                with stage("made", "shifted", "act_step", "step", "cumulated") as (block, made, shifted, act_step, step, cumulated):
                    @block.tensor
                    def _(pe):
                        for t in range(4):
                            pe.matmul(bank(t)[:, 0:T], wlr[:, t // 2, t % 2 * P:(t % 2 + 1) * P], lr[:, :], start=True, stop=True).then_inc(made, 1)

                    @block.vector
                    def _(dve):
                        st = Steps(dve, step)
                        for t in range(4):
                            dve.wait_ge(made, t + 1)
                            dve.tensor_scalar(x[:, t, :], bank(t)[:, 0:T], blr[:, t // 2, t % 2:t % 2 + 1], None, ALU.add).then_inc(shifted, 1)
                        dve.wait_ge(shifted, 4)
                        dve.wait_ge(act_step, 1)
                        st.did(dve.tensor_scalar(flat(x[:, :, :]), flat(x[:, :, :]), 0.0, 1.0 / 16, ALU.min, ALU.mult))
                        st.settle()
                        dve.wait_ge(act_step, 3)
                        st.did(dve.scalar_tensor_tensor(out=flat(g[:, :, :]), in0=flat(a[:, :, :]), scalar=-1.0 / 16, in1=flat(x[:, :, :]),
                                                        op0=ALU.mult, op1=ALU.add))
                        st.settle()
                        st.did(dve.tensor_tensor_scan(flat(b[:, :, :]), K["chunk_start"][:, :], flat(g[:, :, :]), 0.0, ALU.mult, ALU.add))
                        st.settle()
                        ends = flat(b[:, :, :]).rearrange("p (a c n) -> p a c n", a=4, c=NC)
                        st.did(dve.tensor_copy(tot[:, :, :], ends[:, :, :, 63]))
                        st.settle()
                        back, gb = flat(b[:, 2:4, :]), flat(g[:, 2:4, :])
                        st.did(dve.tensor_tensor(back, gb, back, ALU.subtract)); st.settle()
                        for t in range(2, 4):
                            for n in range(NC):
                                dve.tensor_scalar(b[:, t, n * 64:(n + 1) * 64], b[:, t, n * 64:(n + 1) * 64], tot[:, t, n:n + 1], None, ALU.add).then_inc(cumulated, 1)

                    @block.scalar
                    def _(act):
                        act.wait_ge(shifted, 4)
                        act.activation(flat(a[:, :, :]), flat(x[:, :, :]), ACT.Abs).then_inc(act_step, 1)
                        act.wait_ge(act_step, 1)
                        act.activation(flat(a[:, :, :]), flat(a[:, :, :]), ACT.Exp, scale=-1.0).then_inc(act_step, 1)
                        act.wait_ge(act_step, 2)
                        act.activation(flat(a[:, :, :]), flat(a[:, :, :]), ACT.Ln, bias=1.0).then_inc(act_step, 1)
                qd, kd, kst = x, a, g
                with stage("e_up", "e_down", "e_rest", "rest", "made") as (block, e_up, e_down, e_rest, rest_, made):
                    ex, en = scratch(5, 0, 4, T), scratch(5, 1, 4, T)
                    @block.gpsimd
                    def _(pool):
                        for t in range(4):
                            for n in range(NC):
                                op = pool.tensor_scalar(kst[:, t, n * 64:(n + 1) * 64], b[:, t, n * 64:(n + 1) * 64], tot[:, t, n:n + 1], None, ALU.subtract)
                        op.then_inc(rest_, 1)

                    @block.scalar
                    def _(act):
                        act.activation(flat(ex[:, :, :]), flat(b[:, :, :]), ACT.Exp).then_inc(e_up, 1)
                        act.activation(flat(en[:, :, :]), flat(b[:, :, :]), ACT.Exp, scale=-1.0).then_inc(e_down, 1)
                        act.activation(flat(dec[:, :, :]), flat(tot[:, :, :]), ACT.Exp).then_inc(e_down, 1)
                        act.wait_ge(rest_, 1)
                        act.activation(flat(kst[:, :, :]), flat(kst[:, :, :]), ACT.Exp, scale=-1.0).then_inc(e_rest, 1)

                    @block.vector
                    def _(dve):
                        dve.wait_ge(e_up, 1)
                        for d in range(2):
                            dve.scalar_tensor_tensor(out=flat(qd[:, 2 * d:2 * d + 2, :]), in0=flat(gq[:, :, :]), scalar=64 ** -0.5,
                                                     in1=flat(ex[:, 2 * d:2 * d + 2, :]), op0=ALU.mult, op1=ALU.mult).then_inc(made, 1)
                        dve.wait_ge(e_down, 1)
                        for d in range(2):
                            dve.tensor_tensor(flat(kd[:, 2 * d:2 * d + 2, :]), flat(gk[:, :, :]), flat(en[:, 2 * d:2 * d + 2, :]), ALU.mult).then_inc(made, 1)
                        dve.wait_ge(e_rest, 1)
                        for d in range(2):
                            dve.tensor_tensor(flat(kst[:, 2 * d:2 * d + 2, :]), flat(gk[:, :, :]), flat(kst[:, 2 * d:2 * d + 2, :]), ALU.mult).then_inc(made, 1)
                kT = scratch(7, 0, TT, 512)
                transposes([([(kst[:, t, tt * P:(tt + 1) * P], t * P) for t in range(4)], kT[:, tt, :]) for tt in range(TT)])
                ent = scratch(4, 0, 4, NC, P)
                order = {0: [0, 1, 2, 3], 1: [3, 2, 1, 0]}
                place = {}
                for par in range(2):
                    n = 0
                    for d in range(2):
                        for ch in order[d][:3]:
                            if ch % 2 == par:
                                for p in range(2):
                                    place[d, ch, p] = (2 * par + n // 4, n % 4)
                                    n += 1
                with stage("grown", "carried") as (block, grown, carried):
                    @block.tensor
                    def _(pe):
                        for (d, ch, p), (bk, col) in place.items():
                            r = ch % 2 * 64
                            for hp in range(2):
                                h = 2 * p + hp
                                mm = pe.matmul(bank(bk)[hp * 64:hp * 64 + 64, col * P:(col + 1) * P], kT[r:r + 64, ch // 2, d * 256 + h * 64:d * 256 + h * 64 + 64],
                                               gv[r:r + 64, ch // 2, h * P:(h + 1) * P], start=True, stop=True)
                        mm.then_inc(grown, 1)

                    @block.vector
                    def _(dve):
                        dve.wait_ge(grown, 1)
                        n = 0
                        for i in range(3):
                            for d in range(2):
                                now, nxt = order[d][i], order[d][i + 1]
                                for p in range(2):
                                    t = 2 * d + p
                                    bk, col = place[d, now, p]
                                    src, dst = bank(bk)[:, col * P:(col + 1) * P], ent[:, t, nxt, :]
                                    if i == 0:
                                        dve.tensor_copy(dst, src).then_inc(carried, 1)
                                    else:
                                        dve.wait_ge(carried, n - 3)
                                        dve.scalar_tensor_tensor(out=dst, in0=ent[:, t, now, :], scalar=dec[:, t, now:now + 1], in1=src,
                                                                 op0=ALU.mult, op1=ALU.add).then_inc(carried, 1)
                                    n += 1
                o = scratch(3, 1, 4, T)
                am = scratch(7, 1, 3, 2 * P)
                U = [(h, tt) for h in range(H) for tt in range(TT)]
                with stage("scored", "masked", "summed", "out") as (block, scored, masked, summed, outed):
                    @block.tensor
                    def _(pe):
                        for i in range(len(U) + 1):
                            if i < len(U):
                                h, tt = U[i]
                                lo = h % 2 * 64
                                if i >= 3:
                                    pe.wait_ge(masked, i - 2)
                                for d in range(2):
                                    t = 2 * d + h // 2
                                    mm = pe.matmul(bank(i % 3)[:, d * P:(d + 1) * P], kd[lo:lo + 64, t, tt * P:(tt + 1) * P], qd[lo:lo + 64, t, tt * P:(tt + 1) * P],
                                                   start=True, stop=True)
                                mm.then_inc(scored, 1)
                            if i >= 1:
                                j = i - 1
                                h, tt = U[j]
                                lo = h % 2 * 64
                                pe.wait_ge(masked, j + 1)
                                if j >= 3:
                                    pe.wait_ge(outed, j - 2)
                                bk = bank(3 + j % 3)
                                for d in range(2):
                                    pe.matmul(bk[:, 0:P], gv[:, tt, h * P:(h + 1) * P], am[:, j % 3, d * P:(d + 1) * P], start=(d == 0), stop=(d == 1))
                                for d in range(2):
                                    for ch in (2 * tt, 2 * tt + 1):
                                        if ch == order[d][0]:
                                            continue
                                        cc = ch % 2 * 64
                                        mm = pe.matmul(bk[:, cc:cc + 64], ent[lo:lo + 64, 2 * d + h // 2, ch, :], qd[lo:lo + 64, 2 * d + h // 2, ch * 64:(ch + 1) * 64],
                                                       start=False, stop=True, skip_group_check=True)
                                mm.then_inc(summed, 1)

                    @block.vector
                    def _(dve):
                        for j in range(len(U)):
                            dve.wait_ge(scored, j + 1)
                            if j >= 3:
                                dve.wait_ge(summed, j - 2)
                            dve.tensor_tensor(am[:, j % 3, :], bank(j % 3)[:, 0:2 * P], K["gla_keep"][:, :], ALU.mult).then_inc(masked, 1)

                    @block.scalar
                    def _(act):
                        for j, (h, tt) in enumerate(U):
                            act.wait_ge(summed, j + 1)
                            act.activation(o[:, h, tt * P:(tt + 1) * P], bank(3 + j % 3)[:, 0:P], ACT.Copy).then_inc(outed, 1)
                rmsnorm([(o[:, :, :], [[k] for k in range(4)], ones, 128, lambda k: G["onorm"][:, 0:1], o)])
                with stage("gated") as (block, gated):
                    @block.vector
                    def _(dve):
                        dve.tensor_tensor(flat(og[:, :, :]), flat(og[:, :, :]), flat(o[:, :, :]), ALU.mult).then_inc(gated, 1)

        def hyena(c, hc, skip, w1, w2, w3, hb, hf, dst):
            dft = K["dft"][:, :].rearrange("p (t s k) -> p t s k", t=TT, s=2)
            idft = K["idft"][:, :].rearrange("p (s k t) -> p s k t", s=2, k=TT)
            with ExitStack() as c:
                F = sb(c, "spectra", [P, 2, 4, 512])
                with ExitStack() as c1:
                    h2 = sb(c1, "filter_hidden", [65, T])
                    an, tn, rr = sb(c1, "angle", [64, T]), sb(c1, "turns", [64, T]), sb(c1, "reduced", [64, T])
                    with stage("made", "step", "sined", "one") as (block, made, step, sined, one):
                        R = REDUCE_STEPS + 1
                        @block.gpsimd
                        def _(pool):
                            pool.memset(h2[64:65, :], 1.0).then_inc(one, 1)
                        @block.tensor
                        def _(pe):
                            pe.matmul(bank(0)[0:64, 0:T], w1[:, :], K["hy_pos"][:, :], start=True, stop=True).then_inc(made, 1)
                            pe.wait_ge(sined, 1)
                            pe.matmul(bank(1)[0:64, 0:T], w2[:, :], h2[0:64, :], start=True, stop=True).then_inc(made, 1)
                        @block.vector
                        def _(dve):
                            st = Steps(dve, step)
                            for j in range(2):
                                dve.wait_ge(made, j + 1)
                                st.did(dve.tensor_scalar(an[:, :], bank(j)[0:64, 0:T], hb[:, j:j + 1], hf[:, j:j + 1], ALU.add, ALU.mult)); st.settle()
                                if j:
                                    dve.wait_ge(sined, 1)
                                reduce_angle(dve, st, an[:, :], tn[:, :], rr[:, :])
                        @block.scalar
                        def _(act):
                            act.wait_ge(step, R)
                            act.activation(h2[0:64, :], rr[:, :], ACT.Sin).then_inc(sined, 1)
                            act.wait_ge(made, 2)
                            act.wait_ge(step, 2 * R)
                            act.activation(h2[0:64, :], rr[:, :], ACT.Sin).then_inc(sined, 1)
                    for o in range(2):
                        with ExitStack() as c2:
                            fb = slots[:, 0, :].rearrange("p (d t n) -> p d t n", d=2, t=TT)
                            ab = slots[:, 1, :].rearrange("p (d t n) -> p d t n", d=2, t=TT)
                            pq = slots[:, 2, :].rearrange("p (d t n) -> p d t n", d=2, t=TT)
                            sc = slots[:, 3, 0:512]
                            win = K["hy_window"][:, :].rearrange("p (t n) -> p t n", t=TT)
                            with stage("made", "windowed", "lag0", "absd", "mixed", "summed", "step", "transformed", "out") as \
                                    (block, made, windowed, lag0, absd, mixed, summed, step, transformed, outed):
                                @block.tensor
                                def _(pe):
                                    for d in range(2):
                                        for t in range(TT):
                                            pe.matmul(bank(2 * d + t), h2[:, t * P:(t + 1) * P], w3[:, (2 * o + d) * 512:(2 * o + d + 1) * 512], start=True, stop=True).then_inc(made, 1)
                                    pe.wait_ge(absd, 2)
                                    for n in range(4):
                                        mm = pe.matmul(bank(4), ones[:, :], ab[:, n // 2, n % 2, :], start=(n == 0), stop=(n == 3))
                                    mm.then_inc(summed, 1)
                                    pe.wait_ge(mixed, 2)
                                    for s in range(2):
                                        for k in range(2):
                                            for t in range(TT):
                                                mm = pe.matmul(bank(2 * s + k), dft[:, t, s, k * P:(k + 1) * P], pq[:, s, t, :], start=(t == 0), stop=(t == TT - 1))
                                            mm.then_inc(transformed, 1)
                                @block.vector
                                def _(dve):
                                    for d in range(2):
                                        for t in range(TT):
                                            dve.wait_ge(made, 2 * d + t + 1)
                                            dve.tensor_tensor(fb[:, d, t, :], bank(2 * d + t), win[:, t, :], ALU.mult).then_inc(windowed, 1)
                                    dve.wait_ge(windowed, 3)
                                    dve.memset(fb[0:1, 1, 0, :], 0.0).then_inc(lag0, 1)
                                    dve.wait_ge(lag0, 1)
                                    dve.wait_ge(windowed, 4)
                                    for s, op in enumerate((ALU.add, ALU.subtract)):
                                        dve.tensor_tensor(flat(pq[:, s]), flat(fb[:, 0]), flat(fb[:, 1]), op).then_inc(mixed, 1)
                                    dve.wait_ge(summed, 1)
                                    st = Steps(dve, step)
                                    st.did(dve.tensor_scalar(sc[:, :], bank(4), EPS, None, ALU.add)); st.settle()
                                    st.did(dve.reciprocal(sc[:, :], sc[:, :])); st.settle()
                                    for n in range(4):
                                        dve.wait_ge(transformed, n + 1)
                                        dve.tensor_tensor(F[:, o, n, :], bank(n), sc[:, :], ALU.mult).then_inc(outed, 1)
                                @block.scalar
                                def _(act):
                                    act.wait_ge(windowed, 4)
                                    act.wait_ge(lag0, 1)
                                    for d in range(2):
                                        act.activation(flat(ab[:, d]), flat(fb[:, d]), ACT.Abs).then_inc(absd, 1)
                u = sb(c, "tokens", [P, TT, 512])
                y = slots[:, 0, :].rearrange("p (a n) -> p a n", a=4)
                t2 = slots[:, 1, :].rearrange("p (a n) -> p a n", a=4)
                z = sb(c, "z", [P, 4, T])
                src = [hc[:, 0:4, :], z[:, :, :]]
                for o in range(2):
                    transposes([([(src[o][:, k, t * P:(t + 1) * P], k * P) for k in range(4)], u[:, t, :]) for t in range(TT)])
                    res_ = z if o == 0 else dst
                    with stage("transformed", "first", "second", "product", "back", "skipped", "out") as \
                            (block, transformed, first_, second_, product, back, skipped, outed):
                        @block.tensor
                        def _(pe):
                            for n in range(4):
                                for t in range(TT):
                                    mm = pe.matmul(bank(n), dft[:, t, n // 2, n % 2 * P:(n % 2 + 1) * P], u[:, t, :], start=(t == 0), stop=(t == TT - 1))
                                mm.then_inc(transformed, 1)
                            pe.wait_ge(product, 4)
                            for m in range(4):
                                for n in range(4):
                                    mm = pe.matmul(bank(4 + m)[:, 0:T], y[:, n, m * P:(m + 1) * P], idft[:, n // 2, n % 2, :], start=(n == 0), stop=(n == 3))
                                mm.then_inc(back, 1)
                        @block.vector
                        def _(dve):
                            dve.wait_ge(transformed, 4)
                            for k in range(2):
                                Ak, Bk, Fc, Fs = bank(k), bank(2 + k), F[:, o, k, :], F[:, o, 2 + k, :]
                                dve.tensor_tensor(y[:, k, :], Ak, Fc, ALU.mult).then_inc(first_, 1)
                                dve.tensor_tensor(y[:, 2 + k, :], Ak, Fs, ALU.mult).then_inc(first_, 1)
                                dve.tensor_tensor(t2[:, k, :], Bk, Fs, ALU.mult).then_inc(second_, 1)
                                dve.tensor_tensor(t2[:, 2 + k, :], Bk, Fc, ALU.mult).then_inc(second_, 1)
                            for m in range(4):
                                dve.wait_ge(back, m + 1)
                                dve.scalar_tensor_tensor(out=res_[:, m, :], in0=src[o][:, m, :], scalar=skip[:, o, m:m + 1], in1=bank(4 + m)[:, 0:T],
                                                         op0=ALU.mult, op1=ALU.add).then_inc(skipped, 1)
                            for m in range(4):
                                dve.wait_ge(skipped, m + 1)
                                dve.tensor_tensor(res_[:, m, :], res_[:, m, :], hc[:, 4 * (o + 1) + m, :], ALU.mult).then_inc(outed, 1)
                        @block.gpsimd
                        def _(pool):
                            for k in range(2):
                                pool.wait_ge(first_, 2 * k + 2)
                                pool.wait_ge(second_, 2 * k + 2)
                                pool.tensor_tensor(y[:, k, :], y[:, k, :], t2[:, k, :], ALU.subtract).then_inc(product, 1)
                                pool.tensor_tensor(y[:, 2 + k, :], y[:, 2 + k, :], t2[:, 2 + k, :], ALU.add).then_inc(product, 1)

        with nc.Fori(0, 1 if stop == "layer" else 2) as L:
            layer(L)
        if stop == "layer":
            dump("mlp0", res[:, :, :])
            return

        with ExitStack() as c:
            y = sb(c, "y", [P, TT, D])
            transposes([([(res[:, 4 * g + k, t * P:(t + 1) * P], k * P) for k in range(4)], y[:, t, g * 512:(g + 1) * 512]) for t in range(TT) for g in range(2)])
            with stage("stored") as (block, stored):
                @block.sync
                def _(sp):
                    sp.dma_start(out[0].rearrange("(t p) d -> p t d", p=P), y[:, :, :]).then_inc(stored, 16)
                    sp.wait_ge(stored, 16)


REDUCE_STEPS = 6


def reduce_angle(dve, st, ang, turns, out):
    magic = 1.5 * 2.0 ** 23
    two_pi = 2 * math.pi
    c1 = float(np.float32(6.28125))
    c2 = float(np.float32(two_pi - c1))
    c2 = float(np.float32(np.round(c2 * 2 ** 20) / 2 ** 20))
    c3 = two_pi - c1 - c2
    st.did(dve.tensor_scalar(turns, ang, 1.0 / two_pi, magic, ALU.mult, ALU.add)); st.settle()
    st.did(dve.tensor_scalar(turns, turns, magic, None, ALU.subtract)); st.settle()
    st.did(dve.scalar_tensor_tensor(out=out, in0=turns, scalar=-c1, in1=ang, op0=ALU.mult, op1=ALU.add)); st.settle()
    st.did(dve.scalar_tensor_tensor(out=out, in0=turns, scalar=-c2, in1=out, op0=ALU.mult, op1=ALU.add)); st.settle()
    st.did(dve.scalar_tensor_tensor(out=out, in0=turns, scalar=-c3, in1=out, op0=ALU.mult, op1=ALU.add)); st.settle()
    st.did(dve.tensor_scalar(out, out, 3.1415925, -3.1415925, ALU.min, ALU.max)); st.settle()


def kernel(**inputs):
    import concourse.bacc as bacc
    from concourse.bass_utils import run_bass_kernel_spmd

    nc = bacc.Bacc("TRN2", target_bir_lowering=False, num_devices=1)
    arrays, A = {}, {}
    for name, a in list(inputs.items()) + [("c_" + n, a) for n, a in CONST.items()]:
        a = np.ascontiguousarray(a)
        arrays[f"in_{name}_dram"] = a
        A[name] = nc.dram_tensor(f"in_{name}_dram", a.shape, mybir.dt.from_np(a.dtype), kind="ExternalInput").ap()
    out = nc.dram_tensor("out_0_dram", (1, T, D), F32, kind="ExternalOutput").ap()
    program(nc, A, out)
    r = run_bass_kernel_spmd(nc, [arrays], core_ids=[0])
    return r.results[0]["out_0_dram"]
```

```python
import math
from contextlib import ExitStack, contextmanager

import numpy as np
import concourse.bass as bass
from concourse import mybir

F32 = mybir.dt.float32
BF16 = mybir.dt.bfloat16
F32R = mybir.dt.float32r
I32 = mybir.dt.int32
U32 = mybir.dt.uint32
ALU = mybir.AluOpType
ACT = mybir.ActivationFunctionType
AX = mybir.AxisListType

P = 128
T = 256
TT = T // P
D = 1024
KD = D // P
EPS = 1e-6
NSLOT = 6
CAP = P
NE = 8
NJOB = NE + 4
UNIT = 256
NEG = -1e30


def constants():
    c = {}
    eye = np.eye(P, dtype=np.float32)
    c["eye"] = eye
    i = np.arange(P)
    c["blocks64"] = (i[:, None] // 64 == i[None, :] // 64).astype(np.float32)
    def rotation(half):
        r = np.zeros((P, P), np.float32)
        for j in range(P):
            if j % (2 * half) < half:
                r[j + half, j] = -1.0
            else:
                r[j - half, j] = 1.0
        return r
    c["rot32"] = rotation(32)
    c["rot16"] = rotation(16)
    for g in range(2):
        e = np.zeros((P, P), np.float32)
        e[64 * g + i % 64, i] = 1.0
        c[f"twice{g}"] = e
    c["causal_add"] = np.where(i[None, :] <= i[:, None], 0.0, NEG).astype(np.float32)
    t = np.arange(T)
    c["keep_st"] = (i[:, None] <= i[None, :]).astype(np.float32)
    same = i[:, None] // 64 == i[None, :] // 64
    c["gla_keep"] = np.stack([same & (i[:, None] <= i[None, :]), same & (i[:, None] > i[None, :])], 1).astype(np.float32).reshape(P, -1)
    c["chunk_start"] = np.tile((t % 64 != 0).astype(np.float32)[None, :], (P, 4))
    sel = np.zeros((NJOB, NJOB, P), np.float32)
    sel[np.arange(NJOB), np.arange(NJOB), :] = 1.0
    c["row_select"] = sel.reshape(NJOB, -1)
    c["earlier"] = (i[:, None] < i[None, :]).astype(np.float32)
    c["inv_freq"] = (1.0 / (10000.0 ** (np.arange(0, 64, 2, dtype=np.float32) / np.float32(64))))[i % 32].astype(np.float32)[:, None]
    d = i % 64
    inv = (10000.0 ** (-np.arange(16, dtype=np.float32) / np.float32(16))).astype(np.float32)
    pos = np.stack([t // 64, t % 64]).astype(np.float32)
    ang = (pos[d // 32] * inv[d % 16][:, None]).astype(np.float32)
    c["axial_cos"] = np.cos(ang).astype(np.float32)
    c["axial_sin"] = np.sin(ang).astype(np.float32)
    tf = np.arange(T, dtype=np.float32)
    tn = tf / (T - 1)
    w = 2.0 * math.pi * tf / T
    f = np.linspace(1e-4, 15, 16, dtype=np.float32)
    fw = (w[:, None] * f).astype(np.float32)
    c["hy_pos"] = np.ascontiguousarray(np.concatenate([tn[:, None], np.cos(fw), -np.sin(fw)], -1).astype(np.float32).T)
    deltas = np.abs(np.linspace(math.log(1e-2) / 0.3, math.log(1e-2) / 1.5, 512, dtype=np.float32))
    win = np.exp(-tn[:, None] * deltas).astype(np.float32)
    c["hy_window"] = np.ascontiguousarray(win.reshape(TT, P, 512).transpose(1, 0, 2)).reshape(P, -1)
    k = np.arange(T)
    a = np.pi * ((2 * k[None, :] + 1) * np.arange(T)[:, None] % 1024) / 512.0
    cs = np.stack([np.cos(a), np.sin(a)])
    c["dft"] = np.ascontiguousarray(cs.reshape(2, TT, P, T).transpose(2, 1, 0, 3)).astype(np.float32).reshape(P, -1)
    c["idft"] = np.ascontiguousarray((cs / T).transpose(0, 2, 1).reshape(2, TT, P, T).transpose(2, 0, 1, 3)).astype(np.float32).reshape(P, -1)
    return c


CONST = constants()


def program(nc, A, out, dbg=None, stop=None):
    ctx = ExitStack()
    SEM0 = 120
    engines = list(nc.engines.keys())

    @contextmanager
    def stage(*names):
        sems = [nc.alloc_semaphore(name=f"{n}_{nc.next_id()}", num=SEM0 + k) for k, n in enumerate(names)]
        with nc.Block() as block:
            yield (block, *sems)
        nc.multi_engine_barrier(engines, sems_to_clear=range(SEM0, SEM0 + len(names)))
        for s in sems:
            nc.release_semaphore(s)

    def sb(c, name, shape, dt=F32):
        return c.enter_context(nc.sbuf_tensor(f"{name}_{nc.next_id()}", shape, dt))

    class Steps:
        def __init__(self, engine, sem):
            self.engine, self.sem, self.n = engine, sem, 0

        def did(self, inst):
            self.n += 1
            inst.then_inc(self.sem, 1)
            return self.n

        def settle(self, n=None):
            self.engine.wait_ge(self.sem, self.n if n is None else n)

    with ctx:
        ctx.enter_context(nc.allow_non_contiguous_dma(reason="small vectors"))
        ps = ctx.enter_context(nc.psum_tensor("ps", [P, 8, 512], F32))
        slots = sb(ctx, "slots", [P, NSLOT, 2048])
        w_hi = sb(ctx, "w_hi", [P, 2, 2048], F32R)
        w_lo = sb(ctx, "w_lo", [P, 2, 2048], F32R)
        res = sb(ctx, "res", [P, KD, T])
        hn = sb(ctx, "hn", [P, KD, T])
        K = {}
        ALWAYS = ("eye", "blocks64", "rot32", "rot16", "twice0", "twice1", "causal_add", "keep_st", "gla_keep", "inv_freq")
        for name in ALWAYS:
            K[name] = sb(ctx, name, list(CONST[name].shape))

        def constant(c, *names):
            for name in names:
                K[name] = sb(c, name, list(CONST[name].shape))
            return [(K[n][:, :], A["c_" + n]) for n in names]
        ones = sb(ctx, "ones", [P, P])
        zeros = sb(ctx, "zeros", [P, 512], BF16)
        eye = K["eye"]

        def bank(b):
            return ps[:, b, :]

        def load(pairs):
            with stage("landed") as (block, landed):
                @block.sync
                def _(sp):
                    for dst, src in pairs[0::2]:
                        sp.dma_start(dst, src).then_inc(landed, 16)
                    sp.wait_ge(landed, 16 * len(pairs))

                @block.scalar
                def _(act):
                    for dst, src in pairs[1::2]:
                        act.dma_start(dst, src).then_inc(landed, 16)

        def split_source(c, srcs, name):
            pairs = []
            for s in srcs:
                pairs.append((sb(c, name + "_hi", list(s.shape), F32R), sb(c, name + "_lo", list(s.shape), F32R)))
            return pairs

        def linear(units):
            n = len(units)
            NB = 8
            by = {e: [j for j, u in enumerate(units) if u[3] == e] for e in ("act", "dve")}
            srcs, index = [], []
            for u in units:
                if not any(u[0] is s for s in srcs):
                    srcs.append(u[0])
                index.append(next(i for i, s in enumerate(srcs) if s is u[0]))
            with ExitStack() as c, stage(*[f"landed{s}" for s in range(NSLOT)], "products_done", "act_emptied", "dve_emptied",
                                         "src_hi_done", "src_lo_done", "hi_done", "lo_done") as (block, *sems):
                landed, (products_done, act_emptied, dve_emptied, src_hi_done, src_lo_done, hi_done, lo_done) = sems[:NSLOT], sems[NSLOT:]
                pairs = split_source(c, srcs, "x")
                whole = [s[:, :, :] for s in srcs]

                def shape(j):
                    w = units[j][1]
                    return min(P, w.shape[0]), max(1, w.shape[0] // P), w.shape[1]

                def view(tensor, k, j):
                    rows, kt, cols = shape(j)
                    return tensor[0:rows, k, 0:kt * cols].rearrange("p (k n) -> p k n", k=kt)

                @block.sync
                def _(sp):
                    for j in range(n):
                        if j >= NSLOT:
                            sp.wait_ge(lo_done, j - NSLOT + 1)
                            if shape(j - NSLOT)[2] < P:
                                sp.wait_ge(products_done, j - NSLOT + 1)
                        sp.dma_start(view(slots, j % NSLOT, j), units[j][1].rearrange("(k p) n -> p k n", p=shape(j)[0])).then_inc(landed[j % NSLOT], 16)

                @block.tensor
                def _(pe):
                    for j, (src, w, kind, _, _) in enumerate(units):
                        if j >= NB:
                            e = units[j - NB][3]
                            pe.wait_ge(act_emptied if e == "act" else dve_emptied, by[e].index(j - NB) + 1)
                        if index[j] not in index[:j]:
                            pe.wait_ge(src_lo_done, index[j] + 1)
                        pe.wait_ge(lo_done, j + 1)
                        wh, wl, b = view(w_hi, j % 2, j), view(w_lo, j % 2, j), bank(j % NB)
                        xh, xl = pairs[index[j]]
                        rows, kt, cols = shape(j)
                        three = ((wh, xh), (wh, xl), (wl, xh))
                        if kind == "fm":
                            for m in range(0, cols, P):
                                mc = min(P, cols - m)
                                for k in range(kt):
                                    for i, (ww, xx) in enumerate(three):
                                        if mc == P:
                                            mm = pe.matmul(b[:, m // P * T:(m // P + 1) * T], ww[:, k, m:m + P], xx[0:rows, k, :],
                                                           start=(k == 0 and i == 0), stop=(k == kt - 1 and i == 2))
                                    if mc < P:
                                        mm = pe.matmul(b[0:mc, 0:T], view(slots, j % NSLOT, j)[:, k, m:m + mc], src[:, k, :],
                                                       start=(k == 0), stop=(k == kt - 1))
                        else:
                            for m in range(TT):
                                for k in range(kt):
                                    for i, (ww, xx) in enumerate(three):
                                        mm = pe.matmul(b[:, m * cols:(m + 1) * cols], xx[0:rows, k, m * P:(m + 1) * P], ww[:, k, :],
                                                       start=(k == 0 and i == 0), stop=(k == kt - 1 and i == 2))
                        mm.then_inc(products_done, 1)

                def split(engine, j, e):
                    if e == "act":
                        engine.wait_ge(landed[j % NSLOT], 16 * (j // NSLOT + 1))
                        if j >= 2:
                            engine.wait_ge(products_done, j - 1)
                        engine.activation(view(w_hi, j % 2, j), view(slots, j % NSLOT, j), ACT.Copy).then_inc(hi_done, 1)
                    else:
                        engine.wait_ge(hi_done, j + 1)
                        engine.tensor_tensor(view(w_lo, j % 2, j), view(slots, j % NSLOT, j), view(w_hi, j % 2, j).bitcast(F32), ALU.subtract).then_inc(lo_done, 1)

                def run(engine, e, emptied, first):
                    done = 0
                    for j in range(n + 1):
                        if j < n:
                            if index[j] not in index[:j]:
                                first(index[j])
                            split(engine, j, e)
                        if j >= 1 and units[j - 1][3] == e:
                            engine.wait_ge(products_done, j)
                            units[j - 1][4](engine, bank((j - 1) % NB)).then_inc(emptied, 1)

                @block.scalar
                def _(act):
                    run(act, "act", act_emptied,
                        lambda i: act.activation(pairs[i][0][:, :, :], whole[i], ACT.Copy).then_inc(src_hi_done, 1))

                @block.vector
                def _(dve):
                    def lo(i):
                        dve.wait_ge(src_hi_done, i + 1)
                        dve.tensor_tensor(pairs[i][1][:, :, :], whole[i], pairs[i][0][:, :, :].bitcast(F32), ALU.subtract).then_inc(src_lo_done, 1)
                    run(dve, "dve", dve_emptied, lo)

        def copy_to(dst):
            rows, size = dst.shape[0], int(np.prod(dst.shape[1:]))
            def f(engine, b):
                src = b[0:rows, 0:size]
                if len(dst.shape) == 3:
                    src = src.rearrange("p (a n) -> p a n", a=dst.shape[1])
                if engine is nc.scalar or "calar" in type(engine).__name__ or "Activation" in str(engine.engine):
                    return nc.scalar.activation(dst, src, ACT.Copy)
                return nc.vector.tensor_copy(dst, src)
            return f

        def add_to(dst):
            def f(engine, b):
                src = b.rearrange("p (a n) -> p a n", a=dst.shape[1])
                return nc.vector.tensor_tensor(dst, dst, src, ALU.add)
            return f

        def fm_units(src, w, dst, first="act"):
            order = ["act", "dve"] if first == "act" else ["dve", "act"]
            u = []
            for i, c in enumerate(range(0, w.shape[1], UNIT)):
                cols = min(UNIT, w.shape[1] - c)
                d = dst[:, c // P:(c + cols) // P, :] if cols >= P else dst[0:cols, c // P, :]
                u.append((src, w[:, c:c + cols], "fm", order[i % 2], copy_to(d)))
            return u

        def residual_units(src, w):
            return [(src, w[:, c:c + UNIT], "fm", "dve", add_to(res[:, c // P:c // P + 2, :])) for c in range(0, D, UNIT)]

        def rmsnorm(parts):
            with ExitStack() as c, stage("squared", "summed", "shifted", "rooted", "inverted", "scaled") as \
                    (block, squared, summed, shifted, rooted, inverted, scaled):
                sq, ms, rs = [], [], []
                for i, (src, groups, mat, width, gain, dst) in enumerate(parts):
                    sq.append(slots[:, i, 0:src.shape[1] * T].rearrange("p (k n) -> p k n", n=T))
                    ms.append(slots[:, 4 + i, 0:len(groups) * T].rearrange("p (k n) -> p k n", n=T))
                    rs.append(ms[i])
                nb = 0
                area = []
                for part in parts:
                    g = len(part[1])
                    area.append(ps[:, nb:nb + (g + 1) // 2, :].rearrange("p b n -> p (b n)"))
                    nb += (g + 1) // 2

                @block.scalar
                def _(act):
                    for i, (src, groups, mat, width, gain, dst) in enumerate(parts):
                        act.activation(sq[i], src, ACT.Square).then_inc(squared, 1)
                    for i in range(len(parts)):
                        act.wait_ge(shifted, i + 1)
                        act.activation(ms[i], ms[i], ACT.Sqrt).then_inc(rooted, 1)

                @block.tensor
                def _(pe):
                    for i, (src, groups, mat, width, gain, dst) in enumerate(parts):
                        pe.wait_ge(squared, i + 1)
                        for g, tiles in enumerate(groups):
                            for k in tiles:
                                mm = pe.matmul(area[i][:, g * T:(g + 1) * T], mat[:, :], sq[i][:, k, :],
                                               start=(k == tiles[0]), stop=(k == tiles[-1]))
                        mm.then_inc(summed, 1)

                @block.vector
                def _(dve):
                    for i, (src, groups, mat, width, gain, dst) in enumerate(parts):
                        g = len(groups)
                        dve.wait_ge(summed, i + 1)
                        dve.tensor_scalar(flat(ms[i]), area[i][:, 0:g * T], 1.0 / width, EPS,
                                          ALU.mult, ALU.add).then_inc(shifted, 1)
                    done = 0
                    for i, (src, groups, mat, width, gain, dst) in enumerate(parts):
                        dve.wait_ge(rooted, i + 1)
                        dve.reciprocal(rs[i], ms[i]).then_inc(inverted, 1)
                        dve.wait_ge(inverted, i + 1)
                        for g, tiles in enumerate(groups):
                            for k in tiles:
                                dve.scalar_tensor_tensor(out=dst[:, k, :], in0=src[:, k, :], scalar=gain(k), in1=rs[i][:, g, :],
                                                         op0=ALU.mult, op1=ALU.mult).then_inc(scaled, 1)

        def norm_model(src, gain, dst):
            rmsnorm([(src[:, :, :], [list(range(KD))], ones, D, lambda k: gain[:, k:k + 1], dst)])

        def transposes(items):
            with stage("turned", "act_out", "dve_out") as (block, turned, act_out, dve_out):
                @block.tensor
                def _(pe):
                    for g, (srcs, dst) in enumerate(items):
                        if g >= 8:
                            pe.wait_ge(act_out if g % 2 == 0 else dve_out, (g - 8) // 2 + 1)
                        for src, col in srcs:
                            k, m = src.shape[0], src.shape[1]
                            mm = pe.transpose(bank(g % 8)[0:m, col:col + k], src, eye[0:k, 0:k])
                        mm.then_inc(turned, 1)

                def outs(g):
                    dst = items[g][1]
                    return dst, bank(g % 8)[0:dst.shape[0], 0:dst.shape[1]]

                @block.scalar
                def _(act):
                    for g in range(0, len(items), 2):
                        act.wait_ge(turned, g + 1)
                        dst, b = outs(g)
                        act.activation(dst, b, ACT.Copy).then_inc(act_out, 1)

                @block.vector
                def _(dve):
                    for g in range(1, len(items), 2):
                        dve.wait_ge(turned, g + 1)
                        dst, b = outs(g)
                        dve.tensor_copy(dst, b).then_inc(dve_out, 1)

        def flat(x):
            return x.rearrange("p a n -> p (a n)")

        def rotate(src, n, rot, cos, sin):
            with ExitStack() as c, stage("swapped", "sine_part", "cos_part", "turned") as (block, swapped, sine_part, cos_part, turned):
                t1 = slots[:, 5, 0:n * T].rearrange("p (k n) -> p k n", n=T)
                @block.tensor
                def _(pe):
                    for k in range(n):
                        pe.matmul(bank(k)[:, 0:T], rot[:, :], src[:, k, :], start=True, stop=True).then_inc(swapped, 1)
                @block.vector
                def _(dve):
                    for k in range(n):
                        dve.wait_ge(swapped, k + 1)
                        dve.tensor_tensor(t1[:, k, :], bank(k)[:, 0:T], sin, ALU.mult).then_inc(sine_part, 1)
                    for k in range(n):
                        dve.tensor_tensor(src[:, k, :], src[:, k, :], cos, ALU.mult).then_inc(cos_part, 1)
                    for k in range(n):
                        dve.wait_ge(sine_part, k + 1)
                        dve.wait_ge(cos_part, k + 1)
                        dve.tensor_tensor(src[:, k, :], src[:, k, :], t1[:, k, :], ALU.add).then_inc(turned, 1)

        def spread(pairs):
            with stage("made", "out") as (block, made, outed):
                @block.tensor
                def _(pe):
                    for i, (m, src, dst) in enumerate(pairs):
                        pe.matmul(bank(i)[:, 0:T], m, src, start=True, stop=True).then_inc(made, 1)
                @block.vector
                def _(dve):
                    for i, (m, src, dst) in enumerate(pairs):
                        dve.wait_ge(made, i + 1)
                        dve.tensor_copy(dst, bank(i)[:, 0:T]).then_inc(outed, 1)

        def attention(heads, scale, causal):
            U = [(h, q) for h in range(len(heads)) for q in range(TT)]
            with ExitStack() as c, stage("scored", "masked", "topped", "biased", "expd", "inverted", "weighted", "turned",
                                         "keys_first", "mixed", "out") as \
                    (block, scored, masked, topped, biased, expd, inverted, weighted, turned, keys_first, mixed, outed):
                work = slots[:, 5, :]
                s = work[:, 0:2 * T].rearrange("p (b n) -> p b n", b=2)
                pr = work[:, 2 * T:5 * T].rearrange("p (b n) -> p b n", b=3)
                pt = work[:, 5 * T:7 * T].rearrange("p (b k n) -> p b k n", b=2, k=TT)
                top = work[:, 7 * T:7 * T + 4].rearrange("p (b n) -> p b n", b=2)
                sm = work[:, 7 * T + 4:7 * T + 8].rearrange("p (b n) -> p b n", b=2)

                def keys(q):
                    return P * (q + 1) if causal else T

                @block.tensor
                def _(pe):
                    for i in range(len(U) + 2):
                        if i < len(U):
                            h, q = U[i]
                            if i >= 3:
                                pe.wait_ge(masked if causal else topped, i - 2)
                                if not causal:
                                    pe.wait_ge(expd, i - 2)
                            pairs = heads[h][0]
                            for n, (qq, kk) in enumerate(pairs):
                                mm = pe.matmul(bank(i % 3)[:, 0:keys(q)], qq[:, q * P:(q + 1) * P], kk[:, 0:keys(q)],
                                               start=(n == 0), stop=(n == len(pairs) - 1))
                            mm.then_inc(scored, 1)
                        if 0 <= i - 1 < len(U):
                            j = i - 1
                            h, q = U[j]
                            pe.wait_ge(weighted, j + 1)
                            if j >= 2:
                                pe.wait_ge(keys_first, j - 1)
                            for kt in range(keys(q) // P):
                                mm = pe.transpose(bank(3 + j % 2)[:, kt * P:(kt + 1) * P], pr[:, j % 3, kt * P:(kt + 1) * P], eye[:, :])
                            mm.then_inc(turned, 1)
                        if i - 2 >= 0:
                            j = i - 2
                            h, q = U[j]
                            _, v, base, dst = heads[h]
                            dv = dst.shape[0]
                            pe.wait_ge(keys_first, j + 1)
                            if j >= 2:
                                pe.wait_ge(outed, j - 1)
                            nk = keys(q) // P
                            for m in range(dst.shape[1]):
                                for kt in range(nk):
                                    mm = pe.matmul(bank(5 + j % 2)[base:base + dv, m * P:(m + 1) * P], v(kt, m), pt[:, j % 2, kt, :],
                                                   start=(kt == 0), stop=(kt == nk - 1))
                            mm.then_inc(mixed, 1)

                @block.vector
                def _(dve):
                    def finish(j):
                        dve.wait_ge(expd, j + 1)
                        dve.reciprocal(sm[:, j % 2, 1:2], sm[:, j % 2, 0:1]).then_inc(inverted, 1)
                        dve.wait_ge(inverted, j + 1)
                        n = keys(U[j][1])
                        dve.tensor_scalar(pr[:, j % 3, 0:n], pr[:, j % 3, 0:n], sm[:, j % 2, 1:2], None, ALU.mult).then_inc(weighted, 1)

                    for j, (h, q) in enumerate(U):
                        n = keys(q)
                        dve.wait_ge(scored, j + 1)
                        src = bank(j % 3)[:, 0:n]
                        if causal:
                            if j >= 2:
                                dve.wait_ge(expd, j - 1)
                            if q:
                                dve.tensor_copy(s[:, j % 2, 0:P], src[:, 0:P])
                            dve.tensor_tensor(s[:, j % 2, q * P:n], src[:, q * P:n], K["causal_add"][:, :], ALU.add).then_inc(masked, 1)
                            dve.wait_ge(masked, j + 1)
                            src = s[:, j % 2, 0:n]
                        if j >= 2:
                            dve.wait_ge(expd, j - 1)
                        dve.tensor_reduce(top[:, j % 2, 0:1], src, AX.X, ALU.max).then_inc(topped, 1)
                        dve.wait_ge(topped, j + 1)
                        dve.tensor_scalar(top[:, j % 2, 1:2], top[:, j % 2, 0:1], -scale, None, ALU.mult).then_inc(biased, 1)
                        if j >= 1:
                            finish(j - 1)
                    finish(len(U) - 1)

                @block.scalar
                def _(act):
                    def out(j):
                        h, q = U[j]
                        _, v, base, dst = heads[h]
                        dv = dst.shape[0]
                        act.wait_ge(mixed, j + 1)
                        nm = dst.shape[1]
                        act.activation(dst[:, :, q * P:(q + 1) * P], bank(5 + j % 2)[base:base + dv, 0:nm * P].rearrange("p (m n) -> p m n", m=nm),
                                       ACT.Copy).then_inc(outed, 1)

                    def turn(j):
                        n = keys(U[j][1])
                        act.wait_ge(turned, j + 1)
                        if j >= 2:
                            act.wait_ge(mixed, j - 1)
                        act.activation(flat(pt[:, j % 2, 0:n // P, :]), bank(3 + j % 2)[:, 0:n], ACT.Copy).then_inc(keys_first, 1)

                    for j, (h, q) in enumerate(U):
                        n = keys(q)
                        act.wait_ge(biased, j + 1)
                        if j >= 3:
                            act.wait_ge(turned, j - 2)
                        if j >= 2:
                            act.wait_ge(weighted, j - 1)
                        src = s[:, j % 2, 0:n] if causal else bank(j % 3)[:, 0:n]
                        act.activation(pr[:, j % 3, 0:n], src, ACT.Exp, bias=top[:, j % 2, 1:2], scale=scale,
                                       accum_out=sm[:, j % 2, 0:1]).then_inc(expd, 1)
                        if j >= 1:
                            turn(j - 1)
                        if j >= 2:
                            out(j - 2)
                    turn(len(U) - 1)
                    out(len(U) - 2)
                    out(len(U) - 1)

        def mlp(src, gate, up, down, width, routed=None):
            G = gate is not None
            NT = 1 if routed else TT
            W = 256 if G else 512
            ND = W // 256
            NCH = width // W
            SL = 2 + ND
            NS = 6 if G else 4
            R = 3 if routed else 2
            KH = KD // 2
            PAIRS = NCH // 2
            SLABS = NCH * SL
            with ExitStack() as outer_scope:
                y = sb(outer_scope, "y", [P, NT, D])
                with ExitStack() as c, stage(*[f"landed{s}" for s in range(NS)], "pair_free", "hi_done", "lo_done",
                                             "src_hi_done", "src_lo_done", "activated", "hidden", "turned", "turned_hi", "turned_lo",
                                             "act_out", "dve_out", "chosen", "shared", "gathered", "scattered", "added") as (block, *sems):
                    landed = sems[:NS]
                    (pair_free, hi_done, lo_done, src_hi_done, src_lo_done, activated, hidden, turned, turned_hi, turned_lo,
                     act_out, dve_out, chosen, shared, gathered, scattered, added) = sems[NS:]
                    xh, xl = sb(c, "x_hi", [P, KD, NT * P], F32R), sb(c, "x_lo", [P, KD, NT * P], F32R)
                    his = [w_hi[:, b, :] for b in range(2)]
                    los = [w_lo[:, b, :] for b in range(2)]
                    if R == 3:
                        his.append(sb(c, "w_hi3", [P, 2048], F32R)[:, :])
                        los.append(sb(c, "w_lo3", [P, 2048], F32R)[:, :])
                    sg, hid = sb(c, "activated", [P, NT, W]), sb(c, "hidden", [P, NT, W])
                    hth, htl = sb(c, "hidden_hi", [P, NT, W], F32R), sb(c, "hidden_lo", [P, NT, W], F32R)
                    if routed:
                        RJ, RB, CB, htm_hi, htm_lo, jobs, row_number, col_number = routed
                        sel = sb(c, "select", [P, TT, CAP], F32R)
                        back = sb(c, "select_back", [P, T])

                    def y_bank(tt, h):
                        return bank(2 * tt + h)

                    def first_bank(tt, parity):
                        return bank(4 + parity) if NT == 1 else bank(4 + tt)

                    def turn_bank(tt):
                        return bank(6 + tt)

                    def slab(a, q):
                        return 2 * SL * a + q

                    def passes(engine, body):
                        if routed:
                            n = engine.value_load(jobs[0:1, NJOB:NJOB + 1], min_val=NE, max_val=NJOB - 1)
                            with engine.Fori(0, n) as j:
                                body(j)
                        else:
                            body(0)

                    def walk(j, engine, first, down_, turn, between=None):
                        a0 = j * PAIRS
                        first(a0, 0, 0, 0, None)

                        def pair(i, before):
                            a = a0 + i
                            first(a, 2, 2 * i + 1, 1, before)
                            down_(a, 4, 2 * i, 0)
                            first(a, 2 + SL, 2 * i + 2, 0, (a, 1, a, 3))
                            down_(a, 4 + SL, 2 * i + 1, 1)
                        pair(0, (a0, 0, a0, 1))
                        with engine.Fori(1, PAIRS - 1) as i:
                            pair(i, (a0 + i, 0, a0 + i - 1, 3 + SL))
                        a = a0 + PAIRS - 1
                        first(a, 2, NCH - 1, 1, (a, 0, a - 1, 3 + SL))
                        down_(a, 4, NCH - 2, 0)
                        turn(a, 1, a, 3)
                        if between:
                            between()
                        down_(a, 4 + ND, NCH - 1, 1)

                    @block.sync
                    def _(sp):
                        def body(j):
                            e = sp.value_load(jobs[0:1, bass.ds(j, 1)], min_val=0, max_val=NE - 1) if routed else None

                            def own(w):
                                return w[:, bass.ds(e, 1)].rearrange("p e k n -> p (e k) n") if routed else w
                            gw, uw, dw = own(gate) if G else None, own(up), own(down)

                            def first(a, q, chunk, parity, prev):
                                for h in range(2):
                                    slot, k0 = (q + h) % NS, h * KH
                                    t = slots[:, slot, :].rearrange("p (k n) -> p k n", k=KH)
                                    sp.wait_ge(lo_done, slab(a, q + h) + 1)
                                    if G:
                                        sp.dma_start(t[:, :, 0:W], gw[:, k0:k0 + KH, bass.ds(chunk * W, W)]).then_inc(landed[slot], 16)
                                        sp.dma_start(t[:, :, W:2 * W], uw[:, k0:k0 + KH, bass.ds(chunk * W, W)]).then_inc(landed[slot], 16)
                                    else:
                                        for kk in (0, 2):
                                            sp.dma_start(t[:, kk:kk + 2, :], uw[:, k0 + kk:k0 + kk + 2, bass.ds(chunk * W, W)]).then_inc(landed[slot], 16)

                            def down_(a, q, chunk, parity):
                                for d in range(ND):
                                    slot = (q + d) % NS
                                    sp.wait_ge(lo_done, slab(a, q + d) + 1)
                                    for kk in range(2):
                                        sp.dma_start(slots[:, slot, kk * D:(kk + 1) * D],
                                                     dw[:, bass.ds(chunk * (W // P) + 2 * d + kk, 1), :].rearrange("p k n -> p (k n)")).then_inc(landed[slot], 16)
                            walk(j, sp, first, down_, lambda *_: None)
                        passes(sp, body)

                    @block.tensor
                    def _(pe):
                        pe.matmul(y_bank(0, 0), zeros[:, 0:P], zeros[:, :], start=True, stop=True).then_inc(pair_free, R)

                        def gather(half):
                            for k in range(4 * half, 4 * half + 4):
                                terms = [(t, part) for t in range(TT) for part in (htm_hi, htm_lo)]
                                for i, (t, part) in enumerate(terms):
                                    mm = pe.matmul(bank(2 + half)[:, k % 4 * P:(k % 4 + 1) * P], part[:, t, k * P:(k + 1) * P], sel[:, t, :],
                                                   start=(i == 0), stop=(i == len(terms) - 1))
                            mm.then_inc(gathered, 1)

                        def body(j):
                            for tt in range(NT):
                                for h in range(2):
                                    pe.matmul(y_bank(tt, h), zeros[:, 0:P], zeros[:, :], start=True, stop=True)

                            def turn(a, parity, *_):
                                pe.wait_ge(hidden, NT * (2 * a + parity) + NT)
                                for tt in range(NT):
                                    for w in range(W // P):
                                        mm = pe.transpose(turn_bank(tt)[:, w * P:(w + 1) * P], hid[:, tt, w * P:(w + 1) * P], eye[:, :])
                                    mm.then_inc(turned, 1)

                            def first(a, q, chunk, parity, prev):
                                if prev is None:
                                    pe.wait_ge(src_lo_done, 2 * j + 2)
                                elif NT == 2:
                                    pe.wait_ge(hidden, NT * (2 * prev[0] + prev[1]) + NT)
                                for h in range(2):
                                    pe.wait_ge(lo_done, slab(a, q + h) + 1 + NS)
                                    wh, wl = (x[(q + h) % R].rearrange("p (k n) -> p k n", k=KH) for x in (his, los))
                                    for tt in range(NT):
                                        for k in range(KH):
                                            for i, (xx, ww) in enumerate(((xh, wh), (xh, wl), (xl, wh))):
                                                mm = pe.matmul(first_bank(tt, parity), xx[:, h * KH + k, tt * P:(tt + 1) * P], ww[:, k, :],
                                                               start=(h == 0 and k == 0 and i == 0), stop=(h == 1 and k == KH - 1 and i == 2))
                                    mm.then_inc(pair_free, 1)
                                    if h == 0 and prev is not None:
                                        turn(*prev)

                            def down_(a, q, chunk, parity):
                                pe.wait_ge(turned_lo, NT * (2 * a + parity) + NT)
                                for d in range(ND):
                                    pe.wait_ge(lo_done, slab(a, q + d) + 1 + NS)
                                    wh, wl = (x[(q + d) % R].rearrange("p (k n) -> p k n", k=2) for x in (his, los))
                                    for tt in range(NT):
                                        for kk in range(2):
                                            f = (2 * d + kk) * P
                                            for xx, ww in ((hth, wh), (hth, wl), (htl, wh)):
                                                for h in range(2):
                                                    mm = pe.matmul(y_bank(tt, h), xx[:, tt, f:f + P], ww[:, kk, h * 512:(h + 1) * 512],
                                                                   start=False, stop=False, skip_group_check=True)
                                    mm.then_inc(pair_free, 1)

                            def next_source():
                                pe.wait_ge(chosen, j + 2)
                                gather(0)
                            walk(j, pe, first, down_, turn, next_source if routed else None)
                            if routed:
                                gather(1)
                                pe.wait_ge(act_out, j + 1)
                                pe.wait_ge(dve_out, j + 1)
                                pe.wait_ge(shared, j + 1)
                                for g in range(4):
                                    if g < 2:
                                        pe.wait_ge(src_lo_done, 2 * j + g + 3)
                                    else:
                                        pe.wait_ge(added, 4 * j + g - 1)
                                    for m in range(2):
                                        f = (2 * g + m) * P
                                        mm = pe.matmul(bank(2 + g % 2)[:, m * T:(m + 1) * T], y[:, 0, f:f + P], back[:, :], start=True, stop=True)
                                    mm.then_inc(scattered, 1)

                        if routed:
                            pe.wait_ge(chosen, 1)
                            gather(0)
                            gather(1)
                        passes(pe, body)

                    @block.scalar
                    def _(act):
                        def source(n):
                            for g in range(2):
                                if routed:
                                    act.wait_ge(gathered, 2 * n + g + 1)
                                    act.activation(flat(xh[:, 4 * g:4 * g + 4, :]), bank(2 + g), ACT.Copy).then_inc(src_hi_done, 1)
                                else:
                                    act.activation(xh[:, 4 * g:4 * g + 4, :], src[:, 4 * g:4 * g + 4, :], ACT.Copy).then_inc(src_hi_done, 1)

                        def body(j):
                            def hi(a, q):
                                act.wait_ge(landed[q % NS], 32 * (a * (2 * SL // NS) + q // NS + 1))
                                act.wait_ge(pair_free, slab(a, q) + 1)
                                act.activation(his[q % R], slots[:, q % NS, :], ACT.Copy).then_inc(hi_done, 1)

                            def activate(a, parity, a1, q1):
                                act.wait_ge(pair_free, slab(a1, q1) + 1 + R)
                                for tt in range(NT):
                                    act.activation(sg[:, tt, :], first_bank(tt, parity)[:, 0:W], ACT.Silu if G else ACT.Relu).then_inc(activated, 1)

                            def turned_out(a, parity):
                                for tt in range(NT):
                                    act.wait_ge(turned, NT * (2 * a + parity) + tt + 1)
                                    act.activation(hth[:, tt, :], turn_bank(tt)[:, 0:W], ACT.Copy).then_inc(turned_hi, 1)

                            def first(a, q, chunk, parity, prev):
                                hi(a, q)
                                if prev:
                                    activate(*prev)
                                hi(a, q + 1)
                                if prev:
                                    turned_out(*prev[:2])

                            def down_(a, q, chunk, parity):
                                for d in range(ND):
                                    hi(a, q + d)

                            def turn(a, parity, a1, q1):
                                activate(a, parity, a1, q1)
                                turned_out(a, parity)
                            walk(j, act, first, down_, turn)
                            act.wait_ge(pair_free, SLABS * (j + 1) + R)
                            for tt in range(NT):
                                op = act.activation(y[:, tt, 0:512], y_bank(tt, 0), ACT.Copy)
                            op.then_inc(act_out, 1)
                            if routed:
                                source(j + 1)
                        source(0)
                        passes(act, body)

                    @block.vector
                    def _(dve):
                        def choose(n):
                            for t in range(TT):
                                op = dve.tensor_scalar(sel[:, t, :], row_number[:, :], RJ[:, t, bass.ds(n, 1)], None, ALU.is_equal)
                            op.then_inc(chosen, 1)

                        def source(n):
                            for g in range(2):
                                dve.wait_ge(src_hi_done, 2 * n + g + 1)
                                own = bank(2 + g) if routed else flat(src[:, 4 * g:4 * g + 4, :])
                                dve.tensor_tensor(flat(xl[:, 4 * g:4 * g + 4, :]), own, flat(xh[:, 4 * g:4 * g + 4, :]).bitcast(F32), ALU.subtract).then_inc(src_lo_done, 1)

                        def body(j):
                            def lo(a, q):
                                dve.wait_ge(hi_done, slab(a, q) + 1)
                                dve.tensor_tensor(los[q % R], slots[:, q % NS, :], his[q % R].bitcast(F32), ALU.subtract).then_inc(lo_done, 1)

                            def activate(a, parity):
                                for tt in range(NT):
                                    dve.wait_ge(activated, NT * (2 * a + parity) + tt + 1)
                                    b = first_bank(tt, parity)
                                    dve.tensor_tensor(hid[:, tt, :], b[:, W:2 * W] if G else b[:, 0:W], sg[:, tt, :], ALU.mult).then_inc(hidden, 1)

                            def turned_out(a, parity):
                                for tt in range(NT):
                                    dve.wait_ge(turned_hi, NT * (2 * a + parity) + tt + 1)
                                    dve.tensor_tensor(htl[:, tt, :], turn_bank(tt)[:, 0:W], hth[:, tt, :].bitcast(F32), ALU.subtract).then_inc(turned_lo, 1)

                            def first(a, q, chunk, parity, prev):
                                lo(a, q)
                                if prev:
                                    activate(*prev[:2])
                                lo(a, q + 1)
                                if prev:
                                    turned_out(*prev[:2])

                            def down_(a, q, chunk, parity):
                                for d in range(ND):
                                    lo(a, q + d)

                            def turn(a, parity, a1, q1):
                                activate(a, parity)
                                turned_out(a, parity)

                            if routed:
                                dve.wait_ge(gathered, 2 * j + 2)
                                choose(j + 1)
                                dve.scalar_tensor_tensor(out=back[:, :], in0=RB[:, bass.ds(j, 1), :].rearrange("p a n -> p (a n)"), scalar=col_number[:, 0:1],
                                                         in1=CB[:, bass.ds(j, 1), :].rearrange("p a n -> p (a n)"),
                                                         op0=ALU.is_equal, op1=ALU.mult).then_inc(shared, 1)
                            walk(j, dve, first, down_, turn)
                            dve.wait_ge(pair_free, SLABS * (j + 1) + R)
                            for tt in range(NT):
                                op = dve.tensor_copy(y[:, tt, 512:1024], y_bank(tt, 1))
                            op.then_inc(dve_out, 1)
                            if routed:
                                source(j + 1)
                                for g in range(4):
                                    dve.wait_ge(scattered, 4 * j + g + 1)
                                    dve.tensor_tensor(flat(res[:, 2 * g:2 * g + 2, :]), flat(res[:, 2 * g:2 * g + 2, :]), bank(2 + g % 2), ALU.add).then_inc(added, 1)

                        (dve.memset(hid[:, 0, 0:1], 0.0)).then_inc(lo_done, NS)
                        if routed:
                            choose(0)
                        source(0)
                        passes(dve, body)
                if not routed:
                    with stage("turned", "added") as (block, turned, added):
                        @block.tensor
                        def _(pe):
                            for g in range(KD // 2):
                                for k in range(2):
                                    for t in range(TT):
                                        f = (2 * g + k) * P
                                        mm = pe.transpose(bank(g)[:, k * T + t * P:k * T + (t + 1) * P], y[:, t, f:f + P], eye[:, :])
                                mm.then_inc(turned, 1)

                        @block.vector
                        def _(dve):
                            for g in range(KD // 2):
                                dve.wait_ge(turned, g + 1)
                                dve.tensor_tensor(flat(res[:, 2 * g:2 * g + 2, :]), flat(res[:, 2 * g:2 * g + 2, :]), bank(g), ALU.add).then_inc(added, 1)

        def dump(name, ap):
            if dbg is None or name not in dbg:
                return
            with stage("saved") as (block, saved):
                @block.sync
                def _(sp):
                    sp.dma_start(dbg[name], ap).then_inc(saved, 16)
                    sp.wait_ge(saved, 16)

        def column(ap):
            return ap.rearrange("(k p) -> p k", p=P)

        with stage("set") as (block, set_):
            @block.gpsimd
            def _(pool):
                pool.memset(ones[:, :], 1.0).then_inc(set_, 1)
                pool.memset(zeros[:, :], 0.0).then_inc(set_, 1)
        load([(K[n][:, :], A["c_" + n]) for n in ALWAYS])

        G = {}
        def vec(c, name, ap, n):
            G[name] = sb(c, name, [P, n])
            return (G[name][:, :], column(ap))

        with ExitStack() as c:
            x_tm = sb(c, "x_tm", [P, TT, D])
            load([(x_tm[:, :, :], A["x"][0].rearrange("(t p) d -> p t d", p=P))])
            transposes([([(x_tm[:, t, k * P:(k + 1) * P], kk * T + t * P) for kk, k in enumerate((2 * g, 2 * g + 1)) for t in range(TT)],
                         flat(res[:, 2 * g:2 * g + 2, :])) for g in range(KD // 2)])
        load([vec(ctx, "norm_mix0", A["norm_mix"][0], KD), vec(ctx, "norm_mix1", A["norm_mix"][1], KD),
              vec(ctx, "norm_ffn0", A["norm_ffn"][0], KD), vec(ctx, "norm_ffn1", A["norm_ffn"][1], KD),
              vec(ctx, "final_norm", A["final_norm"], KD)])
        dump("x", res[:, :, :])

        with ExitStack() as c:
            cos = sb(c, "cos", [P, T])
            sin = sb(c, "sin", [P, T])
            load([vec(c, "q_norm", A["mla_q_norm"][0], 2), vec(c, "kv_norm", A["mla_kv_norm"][0], 1)])
            with ExitStack() as c2:
                pos = sb(c2, "pos", [P, T], I32)
                load([(pos[:, :], A["positions"][0].partition_broadcast(P))])
                ang, nn, rr = sb(c2, "ang", [P, 2, T]), sb(c2, "turns", [P, 2, T]), sb(c2, "reduced", [P, 2, T])
                posf = sb(c2, "posf", [P, T])
                with stage("step", "sined") as (block, step, sined):
                    @block.vector
                    def _(dve):
                        st = Steps(dve, step)
                        st.did(dve.tensor_copy(posf[:, :], pos[:, :])); st.settle()
                        st.did(dve.tensor_scalar(ang[:, 1, :], posf[:, :], K["inv_freq"][:, 0:1], None, ALU.mult)); st.settle()
                        st.did(dve.tensor_scalar(ang[:, 0, :], ang[:, 1, :], math.pi / 2, None, ALU.add)); st.settle()
                        reduce_angle(dve, st, flat(ang[:, :, :]), flat(nn[:, :, :]), flat(rr[:, :, :]))
                    @block.scalar
                    def _(act):
                        act.wait_ge(step, 3 + REDUCE_STEPS)
                        act.activation(cos[:, :], rr[:, 0, :], ACT.Sin).then_inc(sined, 1)
                        act.activation(sin[:, :], rr[:, 1, :], ACT.Sin).then_inc(sined, 1)
            norm_model(res, G["norm_mix0"], hn)
            with ExitStack() as c1:
                lat = sb(c1, "latents", [P, 4, T])
                w = A["mla_w_in"][0]
                linear([(hn, w[:, 0:256], "fm", "act", copy_to(lat[:, 0:2, :])),
                        (hn, w[:, 256:384], "fm", "dve", copy_to(lat[:, 2, :])),
                        (hn, w[:, 384:448], "fm", "act", copy_to(lat[0:64, 3, :]))])
                rmsnorm([(lat[:, 0:2, :], [[0, 1]], ones, 256, lambda k: G["q_norm"][:, k:k + 1], lat[:, 0:2, :]),
                         (lat[:, 2:3, :], [[0]], ones, 128, lambda k: G["kv_norm"][:, 0:1], lat[:, 2:3, :])])
                qn = sb(c1, "q_nope", [P, 8, T])
                qr = sb(c1, "q_rope", [P, 4, T])
                kn = sb(c1, "k_nope", [P, 8, T])
                kr = sb(c1, "k_rope", [P, 1, T])
                vv = sb(c1, "v", [P, TT, 8 * P])
                spread([(K["twice0"][0:64, :], lat[0:64, 3, :], kr[:, 0, :])])
                wq, wkv = A["mla_w_qb"][0], A["mla_w_kvb"][0]
                un = []
                lat_q, lat_kv = lat[:, 0:2, :], lat[:, 2:3, :]
                for h in range(8):
                    un.append((lat_q, wq[:, h * 192:h * 192 + 128], "fm", ("act", "dve")[h % 2], copy_to(qn[:, h, :])))
                for h in range(8):
                    lo = h % 2 * 64
                    un.append((lat_q, wq[:, h * 192 + 128:h * 192 + 192], "fm", "dve", copy_to(qr[lo:lo + 64, h // 2, :])))
                for h in range(8):
                    un.append((lat_kv, wkv[:, h * 256:h * 256 + 128], "fm", ("act", "dve")[h % 2], copy_to(kn[:, h, :])))
                for h in range(8):
                    un.append((lat_kv, wkv[:, h * 256 + 128:h * 256 + 256], "tm", ("act", "dve")[h % 2],
                               copy_to(vv[:, :, h * P:(h + 1) * P])))
                linear(un)
                rotate(qr, 4, K["rot32"], cos[:, :], sin[:, :])
                rotate(kr, 1, K["rot32"], cos[:, :], sin[:, :])
                o = sb(c1, "o", [P, 8, T])
                hd = []
                for h in range(8):
                    lo = h % 2 * 64
                    hd.append(([(qn[:, h, :], kn[:, h, :]), (qr[lo:lo + 64, h // 2, :], kr[lo:lo + 64, 0, :])],
                               (lambda kt, m, h=h: vv[:, kt, h * P:(h + 1) * P]), 0, o[:, h:h + 1, :]))
                attention(hd, 192 ** -0.5, True)
                linear(residual_units(o, A["mla_w_out"][0]))
        dump("mla", res[:, :, :])

        def rows(w):
            return w.rearrange("(k p) n -> p k n", p=P)

        norm_model(res, G["norm_ffn0"], hn)
        wg, wu, wd = A["ffn_w_gate"][0], A["ffn_w_up"][0], A["ffn_w_down"][0]
        mlp(hn, rows(wg), rows(wu), rows(wd), 3584)
        dump("ffn", res[:, :, :])
        if stop == "ffn":
            return
        norm_model(res, G["norm_mix1"], hn)
        with ExitStack() as c:
            NH = 8
            w = A["mlstm_w_in"][0]
            load(constant(c, "row_select"))
            load([vec(c, "head_norm", A["mlstm_head_norm"][0], 8), vec(c, "conv_b", A["mlstm_conv_b"][0], 8)])
            conv_w = sb(c, "conv_w", [P, 4, 8])
            gate_b = sb(c, "gate_b", [8, 2])
            load([(conv_w[:, j, :], column(A["mlstm_conv_w"][0][j])) for j in range(4)]
                 + [(gate_b[:, :], A["mlstm_gate_b"][0].rearrange("(a p) -> p a", p=8))])
            og = sb(c, "out_gate", [P, 8, T])
            v = sb(c, "v", [P, TT, D])
            raw = sb(c, "qk_raw", [P, 8, 3 + T])
            qk = sb(c, "qk", [P, 8, T])
            gi = sb(c, "gi", [8, T])
            gf = sb(c, "gf", [8, T])
            hh = sb(c, "h", [P, 8, T])
            with stage("padded") as (block, padded):
                @block.gpsimd
                def _(pool):
                    pool.memset(raw[:, :, 0:3], 0.0).then_inc(padded, 1)
            un = []
            for k in range(4):
                un.append((hn, w[:, k * 256:(k + 1) * 256], "fm", ("act", "dve")[k % 2], copy_to(raw[:, 2 * k:2 * k + 2, 3:3 + T])))
            for k in range(4):
                un.append((hn, w[:, 1024 + k * 256:1024 + (k + 1) * 256], "tm", "dve", copy_to(v[:, :, k * 256:(k + 1) * 256])))
            for k in range(4):
                def gate_out(engine, b, k=k):
                    return nc.scalar.activation(flat(og[:, 2 * k:2 * k + 2, :]), b, ACT.Sigmoid)
                un.append((hn, w[:, 2048 + k * 256:2048 + (k + 1) * 256], "fm", "act", gate_out))
            un.append((hn, w[:, 3072:3080], "fm", "dve", copy_to(gi[:, :])))
            un.append((hn, w[:, 3080:3088], "fm", "dve", copy_to(gf[:, :])))
            linear(un)
            one8 = sb(c, "one8", [8, T])
            bb = sb(c, "bias15", [8, 2])
            B_neg, u, M, em = (sb(c, n, [8, T]) for n in ("B_neg", "u", "M", "em"))
            with stage("conv_step", "convolved", "smooth", "step", "bias_ready", "tanhed", "forget", "last_scan", "floor") as \
                    (block, conv_step, convolved, smooth, step, bias_ready, tanhed, forget, last_scan, floor):
                @block.vector
                def _(dve):
                    st = Steps(dve, step)
                    dve.tensor_scalar(bb[:, :], gate_b[:, :], 1.0 / 15.0, None, ALU.mult).then_inc(bias_ready, 1)
                    st.did(dve.memset(one8[:, :], 1.0))
                    cs = Steps(dve, conv_step)
                    for j in range(4):
                        for k in range(8):
                            src, acc = raw[:, k, j:j + T], qk[:, k, :]
                            if j == 0:
                                cs.did(dve.tensor_scalar(acc, src, conv_w[:, 0, k:k + 1], None, ALU.mult))
                            else:
                                cs.settle(8 * (j - 1) + k + 1)
                                inst = dve.scalar_tensor_tensor(out=acc, in0=src, scalar=conv_w[:, j, k:k + 1], in1=acc, op0=ALU.mult, op1=ALU.add)
                                if j == 3:
                                    inst.then_inc(convolved, 1)
                                else:
                                    cs.did(inst)
                    dve.wait_ge(forget, 2)
                    st.settle()
                    st.did(dve.tensor_tensor_scan(B_neg[:, :], one8[:, :], gf[:, :], 0.0, ALU.mult, ALU.add)); st.settle()
                    st.did(dve.scalar_tensor_tensor(out=u[:, :], in0=gi[:, :], scalar=15.0, in1=B_neg[:, :], op0=ALU.mult, op1=ALU.add)); st.settle()
                    st.did(dve.tensor_tensor_scan(M[:, :], one8[:, :], u[:, :], 0.0, ALU.mult, ALU.max)); st.settle()
                    dve.tensor_tensor(em[:, :], B_neg[:, :], M[:, :], ALU.subtract).then_inc(last_scan, 1)

                @block.scalar
                def _(act):
                    act.wait_ge(bias_ready, 1)
                    act.activation(gf[:, :], gf[:, :], ACT.Tanh, bias=bb[:, 1:2], scale=1.0 / 15.0).then_inc(tanhed, 1)
                    act.activation(gi[:, :], gi[:, :], ACT.Tanh, bias=bb[:, 0:1], scale=1.0 / 15.0).then_inc(tanhed, 1)
                    act.wait_ge(tanhed, 2)
                    act.activation(gf[:, :], gf[:, :], ACT.Exp, scale=-15.0).then_inc(forget, 1)
                    act.wait_ge(forget, 1)
                    act.activation(gf[:, :], gf[:, :], ACT.Ln, bias=1.0).then_inc(forget, 1)
                    act.wait_ge(last_scan, 1)
                    act.activation(em[:, :], em[:, :], ACT.Exp).then_inc(floor, 1)
                    for k in range(8):
                        act.wait_ge(convolved, k + 1)
                        act.activation(qk[:, k, :], qk[:, k, :], ACT.Silu, bias=G["conv_b"][:, k:k + 1]).then_inc(smooth, 1)
            Mb, Eb, dn = (slots[:, n, :].rearrange("p (h n) -> p h n", h=8) for n in range(3))
            uT = sb(c, "u_col", [P, TT, 8])
            sel = K["row_select"][0:8, 0:8 * P].rearrange("p (h n) -> p h n", h=8)
            spread([(sel[:, h, :], M[:, :], Mb[:, h, :]) for h in range(8)])
            spread([(sel[:, h, :], em[:, :], Eb[:, h, :]) for h in range(8)])
            transposes([([(u[:, t * P:(t + 1) * P], 0)], uT[:, t, :]) for t in range(TT)])
            W3 = T + P
            gt = flat(slots[:, 3:5, :])[:, 0:8 * W3].rearrange("p (h n) -> p h n", h=8)
            keep = K["keep_st"][:, 0:P]
            with stage("margin", "decayed", "kept", "scored", "weighted", "summed", "absolute", "bounded", "inverted", "normed") as \
                    (block, margin, decayed, kept, scored, weighted, summed, absolute, bounded, inverted, normed):
                @block.tensor
                def _(pe):
                    for h in range(NH):
                        lo = h % 2 * 64
                        q_, k_ = qk[lo:lo + 64, h // 2, :], qk[lo:lo + 64, 4 + h // 2, :]
                        pe.matmul(bank(h)[:, 0:T], k_[:, 0:P], q_, start=True, stop=True)
                        pe.matmul(bank(h)[:, T:W3], k_[:, P:T], q_[:, P:T], start=True, stop=True).then_inc(scored, 1)
                    for h in range(NH):
                        pe.wait_ge(weighted, h + 1)
                        for dst, lhs in ((bank(h)[:, 0:T], lambda kt: v[:, kt, h * P:(h + 1) * P]), (bank(h)[:, T:2 * T], lambda kt: ones[:, :])):
                            pe.matmul(dst, lhs(0), gt[:, h, 0:T], start=True, stop=True)
                            mm = pe.matmul(dst[:, P:T], lhs(1), gt[:, h, T:W3], start=False, stop=True, skip_group_check=True)
                        mm.then_inc(summed, 1)

                @block.vector
                def _(dve):
                    for h in range(NH):
                        dve.tensor_scalar(gt[:, h, 0:T], Mb[:, h, :], uT[:, 0, h:h + 1], 0.0, ALU.subtract, ALU.max).then_inc(margin, 1)
                        dve.tensor_scalar(gt[:, h, T:W3], Mb[:, h, P:T], uT[:, 1, h:h + 1], 0.0, ALU.subtract, ALU.max).then_inc(margin, 1)
                    for h in range(NH):
                        dve.wait_ge(decayed, h + 1)
                        dve.tensor_tensor(gt[:, h, 0:P], gt[:, h, 0:P], keep, ALU.mult).then_inc(kept, 1)
                        dve.tensor_tensor(gt[:, h, T:W3], gt[:, h, T:W3], keep, ALU.mult).then_inc(kept, 1)
                        dve.wait_ge(scored, h + 1)
                        dve.wait_ge(kept, 2 * h + 2)
                        dve.scalar_tensor_tensor(out=gt[:, h, :], in0=bank(h)[:, 0:W3], scalar=64 ** -0.5, in1=gt[:, h, :],
                                                 op0=ALU.mult, op1=ALU.mult).then_inc(weighted, 1)
                    for h in range(NH):
                        dve.wait_ge(absolute, h + 1)
                        dve.tensor_tensor(dn[:, h, :], dn[:, h, :], Eb[:, h, :], ALU.max).then_inc(bounded, 1)
                        dve.wait_ge(bounded, h + 1)
                        dve.reciprocal(dn[:, h, :], dn[:, h, :]).then_inc(inverted, 1)
                        dve.wait_ge(inverted, h + 1)
                        dve.tensor_tensor(hh[:, h, :], bank(h)[:, 0:T], dn[:, h, :], ALU.mult).then_inc(normed, 1)

                @block.scalar
                def _(act):
                    for h in range(NH):
                        act.wait_ge(margin, 2 * h + 2)
                        act.activation(gt[:, h, :], gt[:, h, :], ACT.Exp, scale=-1.0).then_inc(decayed, 1)
                    for h in range(NH):
                        act.wait_ge(summed, h + 1)
                        act.activation(dn[:, h, :], bank(h)[:, T:2 * T], ACT.Abs).then_inc(absolute, 1)
            rmsnorm([(hh[:, :, :], [[k] for k in range(8)], ones, 128, lambda k: G["head_norm"][:, k:k + 1], hh)])
            with stage("gated") as (block, gated):
                @block.vector
                def _(dve):
                    dve.tensor_tensor(flat(hh[:, :, :]), flat(hh[:, :, :]), flat(og[:, :, :]), ALU.mult).then_inc(gated, 1)
            linear(residual_units(hh, A["mlstm_w_out"][0]))
        dump("mlstm", res[:, :, :])
        if stop == "mlstm":
            return

        norm_model(res, G["norm_ffn1"], hn)
        with ExitStack() as c:
            RJ = sb(c, "rank_by_pass", [P, TT, NJOB])
            RB = sb(c, "rank_rows", [P, NJOB, T])
            CB = sb(c, "share_rows", [P, NJOB, T])
            jobs = sb(c, "passes", [1, NJOB + 1], I32)
            row_number, col_number = sb(c, "row_number", [P, CAP]), sb(c, "col_number", [P, 1])
            htm_hi, htm_lo = sb(c, "h_hi", [P, TT, D], F32R), sb(c, "h_lo", [P, TT, D], F32R)
            with ExitStack() as c1:
                htm = slots[:, 0, :].rearrange("p (t d) -> p t d", t=TT)
                lg = sb(c1, "logits", [P, TT, NE])
                load(constant(c1, "row_select", "earlier"))
                linear([(hn, A["moe_router"][0], "tm", "act", copy_to(lg[:, :, :]))])
                transposes([([(hn[:, 4 * g + k, t * P:(t + 1) * P], k * P) for k in range(4)], htm[:, t, g * 512:(g + 1) * 512]) for t in range(TT) for g in range(2)])
                with stage("hi", "lo") as (block, hi, lo):
                    @block.scalar
                    def _(act):
                        act.activation(htm_hi[:, :, :], htm, ACT.Copy).then_inc(hi, 1)

                    @block.vector
                    def _(dve):
                        dve.wait_ge(hi, 1)
                        dve.tensor_tensor(flat(htm_lo[:, :, :]), flat(htm), flat(htm_hi[:, :, :]).bitcast(F32), ALU.subtract).then_inc(lo, 1)
                top, idx, idf = sb(c1, "top", [P, TT, 8]), sb(c1, "index", [P, TT, 8], U32), sb(c1, "indexf", [P, TT, 8])
                number, oh, gg = sb(c1, "number", [P, NE]), sb(c1, "chosen", [P, 2, TT, NE]), sb(c1, "shares", [P, TT, 4])
                CJ, member = sb(c1, "share_by_pass", [P, TT, NJOB]), sb(c1, "member", [P, TT, NE])
                over, before, pick = sb(c1, "over", [P, NE]), sb(c1, "before", [P, NE]), sb(c1, "pick", [P, NE])
                jobs_f, tmp, ones8 = sb(c1, "passes_f", [P, NJOB + 1]), sb(c1, "tmp", [P, NE]), sb(c1, "ones8", [P, NE])
                with stage("numbered", "step", "differed", "expd", "members", "ranked", "counted") as (block, numbered, step, differed, expd, members, ranked, counted):
                    @block.gpsimd
                    def _(pool):
                        pool.iota(number[:, :], [[1, NE]], base=0, channel_multiplier=0, allow_small_or_imprecise_dtypes=True).then_inc(numbered, 1)
                        pool.iota(row_number[:, :], [[1, CAP]], base=0, channel_multiplier=0, allow_small_or_imprecise_dtypes=True).then_inc(numbered, 1)
                        pool.iota(col_number[:, :], [[0, 1]], base=0, channel_multiplier=1, allow_small_or_imprecise_dtypes=True).then_inc(numbered, 1)

                    @block.tensor
                    def _(pe):
                        pe.wait_ge(members, 2)
                        before_, all_ = K["earlier"][:, :], ones[:, :]
                        pe.matmul(bank(0)[:, 0:NE], before_, member[:, 0, :], start=True, stop=True).then_inc(ranked, 1)
                        pe.matmul(bank(1)[:, 0:NE], before_, member[:, 1, :], start=True, stop=False)
                        pe.matmul(bank(1)[:, 0:NE], all_, member[:, 0, :], start=False, stop=True).then_inc(ranked, 1)
                        pe.matmul(bank(2)[:, 0:NE], all_, member[:, 0, :], start=True, stop=False)
                        pe.matmul(bank(2)[:, 0:NE], all_, member[:, 1, :], start=False, stop=True).then_inc(counted, 1)

                    @block.vector
                    def _(dve):
                        st = Steps(dve, step)

                        def do(inst):
                            st.did(inst)
                            st.settle()
                        for t in range(TT):
                            do(dve.max(out=top[:, t, :], in_=lg[:, t, :]))
                            do(dve.max_index(out=idx[:, t, :], in_max=top[:, t, :], in_values=lg[:, t, :]))
                        do(dve.tensor_copy(idf[:, :, :], idx[:, :, :]))
                        for t in range(TT):
                            dve.tensor_tensor(gg[:, t, 0:1], top[:, t, 1:2], top[:, t, 0:1], ALU.subtract).then_inc(differed, 1)
                        dve.wait_ge(numbered, 3)
                        for t in range(TT):
                            for j in range(2):
                                do(dve.tensor_scalar(oh[:, j, t, :], number[:, :], idf[:, t, j:j + 1], None, ALU.is_equal))
                            dve.tensor_tensor(member[:, t, :], oh[:, 0, t, :], oh[:, 1, t, :], ALU.add).then_inc(members, 1)
                        dve.wait_ge(expd, 1)
                        do(dve.tensor_scalar(gg[:, :, 2:3], gg[:, :, 1:2], 1.0, None, ALU.add))
                        do(dve.reciprocal(gg[:, :, 2:3], gg[:, :, 2:3]))
                        do(dve.tensor_tensor(gg[:, :, 3:4], gg[:, :, 2:3], gg[:, :, 1:2], ALU.mult))
                        do(dve.memset(RJ[:, :, :], -float(CAP)))
                        do(dve.memset(CJ[:, :, :], 0.0))
                        do(dve.memset(jobs_f[:, :], 0.0))
                        do(dve.memset(ones8[:, :], 1.0))
                        do(dve.tensor_copy(jobs_f[:, 0:NE], number[:, :]))
                        dve.wait_ge(members, 2)
                        for t in range(TT):
                            do(dve.tensor_scalar(CJ[:, t, 0:NE], oh[:, 0, t, :], gg[:, t, 2:3], None, ALU.mult))
                            do(dve.scalar_tensor_tensor(out=CJ[:, t, 0:NE], in0=oh[:, 1, t, :], scalar=gg[:, t, 3:4], in1=CJ[:, t, 0:NE],
                                                        op0=ALU.mult, op1=ALU.add))
                            dve.wait_ge(ranked, t + 1)
                            do(dve.scalar_tensor_tensor(out=RJ[:, t, 0:NE], in0=member[:, t, :], scalar=-1024.0, in1=bank(t)[:, 0:NE],
                                                        op0=ALU.mult, op1=ALU.add))
                            do(dve.tensor_scalar(RJ[:, t, 0:NE], RJ[:, t, 0:NE], 1024.0, None, ALU.add))
                        dve.wait_ge(counted, 1)
                        do(dve.tensor_scalar(over[:, :], bank(2)[:, 0:NE], float(CAP), None, ALU.is_gt))
                        do(dve.tensor_tensor_scan(before[:, :], ones8[:, :], over[:, :], 0.0, ALU.mult, ALU.add))
                        do(dve.tensor_scalar(jobs_f[:, NJOB:NJOB + 1], before[:, NE - 1:NE], float(NE), None, ALU.add))
                        do(dve.tensor_tensor(before[:, :], before[:, :], over[:, :], ALU.subtract))
                        for i in range(NJOB - NE - 1):
                            do(dve.scalar_tensor_tensor(out=pick[:, :], in0=before[:, :], scalar=float(i), in1=over[:, :], op0=ALU.is_equal, op1=ALU.mult))
                            for row, col in [(number[:, :], jobs_f[:, NE + i:NE + i + 1])] + \
                                    [(x[:, t, 0:NE], x[:, t, NE + i:NE + i + 1]) for t in range(TT) for x in (RJ, CJ)]:
                                do(dve.tensor_tensor(tmp[:, :], row, pick[:, :], ALU.mult))
                                do(dve.tensor_reduce(col, tmp[:, :], AX.X, ALU.add))
                            for t in range(TT):
                                do(dve.tensor_scalar(RJ[:, t, NE + i:NE + i + 1], RJ[:, t, NE + i:NE + i + 1], float(CAP), None, ALU.subtract))
                        do(dve.tensor_copy(jobs[:, :], jobs_f[0:1, :]))

                    @block.scalar
                    def _(act):
                        act.wait_ge(differed, 2)
                        act.activation(gg[:, :, 1:2], gg[:, :, 0:1], ACT.Exp).then_inc(expd, 1)
                rT, cT = sb(c1, "rank_t", [NJOB, T]), sb(c1, "share_t", [NJOB, T])
                transposes([([(RJ[:, t, :], t * P) for t in range(TT)], rT[:, :]), ([(CJ[:, t, :], t * P) for t in range(TT)], cT[:, :])])
                for src_, dst_ in ((rT, RB), (cT, CB)):
                    for lo_ in range(0, NJOB, 6):
                        spread([(K["row_select"][:, n * P:(n + 1) * P], src_[:, :], dst_[:, n, :]) for n in range(lo_, lo_ + 6)])
            by_row = [A[n][0].rearrange("e (k p) n -> p e k n", p=P) for n in ("moe_w_gate", "moe_w_up", "moe_w_down")]
            mlp(None, *by_row, 3584, routed=(RJ, RB, CB, htm_hi, htm_lo, jobs, row_number, col_number))
        dump("moe", res[:, :, :])
        norm_model(res, G["final_norm"], res)
        dump("block1", res[:, :, :])
        if stop == "block1":
            return

        mem_dram = nc.dram_tensor("memory_feature_major", (P, KD * T), F32).ap()
        with ExitStack() as c:
            m_tm, memT = sb(c, "m_tm", [P, TT, D]), sb(c, "memory", [P, KD, T])
            load([(m_tm[:, :, :], A["mem_2"][0].rearrange("(t p) d -> p t d", p=P))])
            transposes([([(m_tm[:, t, k * P:(k + 1) * P], kk * T + t * P) for kk, k in enumerate((2 * g, 2 * g + 1)) for t in range(TT)],
                         flat(memT[:, 2 * g:2 * g + 2, :])) for g in range(KD // 2)])
            with stage("stored") as (block, stored):
                @block.sync
                def _(sp):
                    sp.dma_start(mem_dram, flat(memT[:, :, :])).then_inc(stored, 16)
                    sp.wait_ge(stored, 16)

        def layer(L):
            def of(name):
                ap = A[name][bass.ds(L, 1)]
                n = len(ap.shape)
                return ap.rearrange({2: "a k -> (a k)", 3: "a k n -> (a k) n", 4: "a b k n -> (a b) k n"}[n])

            with ExitStack() as c:
                w_in = of("w_in_2")
                for n, name, k in (("ln_mix", "ln_mix_2", 8), ("onorm", "gla_onorm_2", 1)):
                    G[n] = sb(c, n, [P, k])
                qg, kg = sb(c, "q_gain", [P, 1]), sb(c, "k_gain", [P, 1])
                hconv = sb(c, "hy_conv", [P, 3, 12])
                skip = sb(c, "skip", [P, 2, 4])
                w1, w2 = sb(c, "hy_w1", [33, 64]), sb(c, "hy_w2", [64, 64])
                hb, hf = sb(c, "hy_b", [64, 2]), sb(c, "hy_freq", [64, 2])
                wlr = sb(c, "w_lr", [32, 2, 256])
                blr = sb(c, "b_lr", [P, 2, 2])
                with stage("cleared") as (block, cleared):
                    @block.gpsimd
                    def _(pool):
                        pool.memset(wlr[:, :, :], 0.0).then_inc(cleared, 1)
                load([(G["ln_mix"][:, :], column(of("ln_mix_2"))), (G["onorm"][:, :], column(of("gla_onorm_2"))),
                      *[(g[o:o + 64, :], of(n).rearrange("(p a) -> p a", a=1)) for g, n in ((qg, "attn_qnorm_2"), (kg, "attn_knorm_2")) for o in (0, 64)],
                      *[(hconv[:, j, :], column(of("hy_conv_2")[j])) for j in range(3)],
                      *[(skip[:, j, :], column(of("hy_skip_2")[j])) for j in range(2)],
                      (w1[:, :], of("hy_w1_2")), (w2[:, :], of("hy_w2_2")),
                      (hb[:, 0:1], of("hy_b1_2").rearrange("(p a) -> p a", a=1)), (hb[:, 1:2], of("hy_b2_2").rearrange("(p a) -> p a", a=1)),
                      *[(hf[:, j:j + 1], of("hy_freq_2")[j].rearrange("(p a) -> p a", a=1)) for j in range(2)],
                      *[(wlr[16 * d:16 * d + 16, d, :], of("gla_w_lr_2")[d]) for d in range(2)],
                      *[(blr[:, d, :], column(of("gla_b_lr_2")[d])) for d in range(2)]])

                norm_model(res, G["ln_mix"], hn)
                gates = sb(c, "gates", [P, 24, T])
                oa, oh_, og = (sb(c, n, [P, 4, T]) for n in ("o_attn", "o_hyena", "o_gla"))
                with ExitStack() as c1:
                    hc = sb(c1, "hy_convolved", [P, 12, T])
                    with ExitStack() as c2:
                        hy = sb(c2, "hy", [P, 12, T + 2])
                        gq, gk = sb(c2, "gq", [P, 2, T]), sb(c2, "gk", [P, 2, T])
                        gv = sb(c2, "gv", [P, TT, 512])
                        lr = sb(c2, "lr", [32, T])
                        with ExitStack() as c3:
                            aq, ak, av = sb(c3, "aq", [P, 4, T]), sb(c3, "ak", [P, 1, T]), sb(c3, "av", [P, TT, P])
                            with stage("padded") as (block, padded):
                                @block.gpsimd
                                def _(pool):
                                    pool.memset(hy[:, :, 0:1], 0.0).then_inc(padded, 1)
                                    pool.memset(hy[:, :, T + 1:T + 2], 0.0).then_inc(padded, 1)
                            un = []

                            def add(kind, lo, hi, dst, step=UNIT):
                                for n, x in enumerate(range(lo, hi, step)):
                                    un.append((hn, w_in[:, x:min(x + step, hi)], kind, ("act", "dve")[len(un) % 2], copy_to(dst(n))))
                            add("fm", 0, 512, lambda n: aq[:, 2 * n:2 * n + 2, :])
                            add("fm", 512, 640, lambda n: ak[:, 0, :])
                            add("tm", 640, 768, lambda n: av[:, :, :])
                            add("fm", 768, 2304, lambda n: hy[:, 2 * n:2 * n + 2, 1:T + 1])
                            add("fm", 2304, 2560, lambda n: gq[:, :, :])
                            add("fm", 2560, 2816, lambda n: gk[:, :, :])
                            add("tm", 2816, 3328, lambda n: gv[:, :, n * 256:(n + 1) * 256])
                            for n in range(2):
                                def silu_out(engine, b, n=n):
                                    return nc.scalar.activation(flat(og[:, 2 * n:2 * n + 2, :]), b, ACT.Silu)
                                un.append((hn, w_in[:, 3328 + n * 256:3584 + n * 256], "fm", "act", silu_out))
                            add("fm", 3840, 3872, lambda n: lr[:, :])
                            for n in range(12):
                                def sigmoid_out(engine, b, n=n):
                                    return nc.scalar.activation(flat(gates[:, 2 * n:2 * n + 2, :]), b, ACT.Sigmoid)
                                un.append((hn, w_in[:, 3872 + n * 256:4128 + n * 256], "fm", "act", sigmoid_out))
                            linear(un)

                            load(constant(c3, "axial_cos", "axial_sin"))
                            rmsnorm([(aq[:, :, :], [[k] for k in range(4)], K["blocks64"], 64, lambda k: qg[:, 0:1], aq),
                                     (ak[:, :, :], [[0]], K["blocks64"], 64, lambda k: kg[:, 0:1], ak)])
                            rotate(aq, 4, K["rot16"], K["axial_cos"][:, :], K["axial_sin"][:, :])
                            rotate(ak, 1, K["rot16"], K["axial_cos"][:, :], K["axial_sin"][:, :])
                            kk = sb(c3, "k_twice", [P, 2, T])
                            spread([(K["twice0"][:, :], ak[:, 0, :], kk[:, 0, :]), (K["twice1"][:, :], ak[:, 0, :], kk[:, 1, :])])
                            hd = []
                            for h in range(8):
                                lo, g = h % 2 * 64, h // 4
                                hd.append(([(aq[lo:lo + 64, h // 2, :], kk[lo:lo + 64, g, :])],
                                           (lambda kt, m, g=g: av[:, kt, g * 64:(g + 1) * 64]), lo, oa[lo:lo + 64, h // 2:h // 2 + 1, :]))
                            attention(hd, 64 ** -0.5, False)
                        with stage("tap", "convolved") as (block, tap, convolved):
                            @block.vector
                            def _(dve):
                                st = Steps(dve, tap)
                                for j in range(3):
                                    for k in range(12):
                                        src, acc = hy[:, k, j:j + T], hc[:, k, :]
                                        if j == 0:
                                            st.did(dve.tensor_scalar(acc, src, hconv[:, 0, k:k + 1], None, ALU.mult))
                                        else:
                                            st.settle(12 * (j - 1) + k + 1)
                                            st.did(dve.scalar_tensor_tensor(out=acc, in0=src, scalar=hconv[:, j, k:k + 1], in1=acc,
                                                                            op0=ALU.mult, op1=ALU.add))
                        gla(c2, gq, gk, gv, lr, wlr, blr, og)
                    hyena(c1, hc, skip, w1, w2, of("hy_w3_2"), of("hy_b3_2"), hb, hf, oh_)
                for i, name in ((L, None),):
                    dumpl("att", oa); dumpl("hyena", oh_); dumpl("gla", og)

                un = []
                for b, (src, wn) in enumerate(((oa, "w_br_attn_2"), (oh_, "w_br_hyena_2"), (og, "w_br_gla_2"))):
                    wb = of(wn)
                    for n in range(4):
                        def gated(engine, bk, k=8 * b + 2 * n):
                            return nc.vector.tensor_tensor(flat(gates[:, k:k + 2, :]), flat(gates[:, k:k + 2, :]), bk, ALU.mult)
                        un.append((src, wb[:, n * 256:(n + 1) * 256], "fm", "dve", gated))
                linear(un)
                with stage("two", "three") as (block, two, three):
                    @block.vector
                    def _(dve):
                        for n in range(4):
                            dve.tensor_tensor(gates[:, 2 * n:2 * n + 2, :], gates[:, 2 * n:2 * n + 2, :], gates[:, 8 + 2 * n:10 + 2 * n, :], ALU.add).then_inc(two, 1)
                        for n in range(4):
                            dve.wait_ge(two, n + 1)
                            dve.tensor_tensor(gates[:, 2 * n:2 * n + 2, :], gates[:, 2 * n:2 * n + 2, :], gates[:, 16 + 2 * n:18 + 2 * n, :], ALU.add).then_inc(three, 1)
                dumpl("mixed", gates[:, 0:8, :])
                linear(residual_units(gates[:, 0:8, :], of("w_out_2")))
            dumpl("mix", res)

            with ExitStack() as c:
                for n, name, k in (("ln_x", "ln_x_2", 8), ("ln_mem", "ln_mem_2", 8), ("x_qnorm", "x_qnorm_2", 2), ("x_knorm", "x_knorm_2", 2), ("ln_mlp", "ln_mlp_2", 8)):
                    G[n] = sb(c, n, [P, k])
                with ExitStack() as c1:
                    memT = sb(c1, "memory", [P, KD, T])
                    load([(flat(memT[:, :, :]), mem_dram)] + [(G[n][:, :], column(of(n + "_2"))) for n in ("ln_x", "ln_mem", "x_qnorm", "x_knorm", "ln_mlp")])
                    mn = sb(c1, "memory_normed", [P, KD, T])
                    rmsnorm([(res[:, :, :], [list(range(KD))], ones, D, lambda k: G["ln_x"][:, k:k + 1], hn),
                             (memT[:, :, :], [list(range(KD))], ones, D, lambda k: G["ln_mem"][:, k:k + 1], mn)])
                    q, k_, v = sb(c1, "q", [P, 8, T]), sb(c1, "k", [P, 8, T]), sb(c1, "v", [P, TT, D])
                    wv = of("x_wv_2")
                    linear(fm_units(hn, of("x_wq_2"), q) + fm_units(mn, of("x_wk_2"), k_)
                           + [(mn, wv[:, n * 256:(n + 1) * 256], "tm", ("act", "dve")[n % 2], copy_to(v[:, :, n * 256:(n + 1) * 256])) for n in range(4)])
                    pairs = [[0, 1], [2, 3], [4, 5], [6, 7]]
                    rmsnorm([(q[:, :, :], pairs, ones, 256, lambda k: G["x_qnorm"][:, k % 2:k % 2 + 1], q),
                             (k_[:, :, :], pairs, ones, 256, lambda k: G["x_knorm"][:, k % 2:k % 2 + 1], k_)])
                    hd = [([(q[:, 2 * h + j, :], k_[:, 2 * h + j, :]) for j in range(2)],
                           (lambda kt, m, h=h: v[:, kt, (2 * h + m) * P:(2 * h + m + 1) * P]), 0, hn[:, 2 * h:2 * h + 2, :]) for h in range(4)]
                    attention(hd, 256 ** -0.5, False)
                    linear(residual_units(hn, of("x_wo_2")))
                dumpl("cross", res)
                norm_model(res, G["ln_mlp"], hn)
            mlp(hn, None, rows(of("mlp_w1_2")), rows(of("mlp_w2_2")), 4096)

        def dumpl(name, ap):
            if dbg is None or name + "0" not in dbg:
                return
            with stage("saved") as (block, saved):
                @block.sync
                def _(sp):
                    sp.dma_start(dbg[name + "0"], ap[:, :, :]).then_inc(saved, 16)
                    sp.wait_ge(saved, 16)

        def gla(c, gq, gk, gv, lr, wlr, blr, og):
            NC, H = 4, 4
            with ExitStack() as c:
                load(constant(c, "chunk_start"))

                def scratch(slot, half, *dims):
                    size = int(np.prod(dims))
                    names = "abc"[:len(dims)]
                    return slots[:, slot, half * 1024:half * 1024 + size].rearrange(
                        f"p ({' '.join(names)}) -> p {' '.join(names)}", **dict(zip(names, dims)))
                x, a, g, b = (scratch(n, 0, 4, T) for n in range(4))
                tot = sb(c, "total", [P, 4, NC])
                dec = sb(c, "chunk_decay", [P, 4, NC])
                with stage("made", "shifted", "act_step", "step", "cumulated") as (block, made, shifted, act_step, step, cumulated):
                    @block.tensor
                    def _(pe):
                        for t in range(4):
                            pe.matmul(bank(t)[:, 0:T], wlr[:, t // 2, t % 2 * P:(t % 2 + 1) * P], lr[:, :], start=True, stop=True).then_inc(made, 1)

                    @block.vector
                    def _(dve):
                        st = Steps(dve, step)
                        for t in range(4):
                            dve.wait_ge(made, t + 1)
                            dve.tensor_scalar(x[:, t, :], bank(t)[:, 0:T], blr[:, t // 2, t % 2:t % 2 + 1], None, ALU.add).then_inc(shifted, 1)
                        dve.wait_ge(shifted, 4)
                        dve.wait_ge(act_step, 1)
                        st.did(dve.tensor_scalar(flat(x[:, :, :]), flat(x[:, :, :]), 0.0, 1.0 / 16, ALU.min, ALU.mult))
                        st.settle()
                        dve.wait_ge(act_step, 3)
                        st.did(dve.scalar_tensor_tensor(out=flat(g[:, :, :]), in0=flat(a[:, :, :]), scalar=-1.0 / 16, in1=flat(x[:, :, :]),
                                                        op0=ALU.mult, op1=ALU.add))
                        st.settle()
                        st.did(dve.tensor_tensor_scan(flat(b[:, :, :]), K["chunk_start"][:, :], flat(g[:, :, :]), 0.0, ALU.mult, ALU.add))
                        st.settle()
                        ends = flat(b[:, :, :]).rearrange("p (a c n) -> p a c n", a=4, c=NC)
                        st.did(dve.tensor_copy(tot[:, :, :], ends[:, :, :, 63]))
                        st.settle()
                        back, gb = flat(b[:, 2:4, :]), flat(g[:, 2:4, :])
                        st.did(dve.tensor_tensor(back, gb, back, ALU.subtract)); st.settle()
                        for t in range(2, 4):
                            for n in range(NC):
                                dve.tensor_scalar(b[:, t, n * 64:(n + 1) * 64], b[:, t, n * 64:(n + 1) * 64], tot[:, t, n:n + 1], None, ALU.add).then_inc(cumulated, 1)

                    @block.scalar
                    def _(act):
                        act.wait_ge(shifted, 4)
                        act.activation(flat(a[:, :, :]), flat(x[:, :, :]), ACT.Abs).then_inc(act_step, 1)
                        act.wait_ge(act_step, 1)
                        act.activation(flat(a[:, :, :]), flat(a[:, :, :]), ACT.Exp, scale=-1.0).then_inc(act_step, 1)
                        act.wait_ge(act_step, 2)
                        act.activation(flat(a[:, :, :]), flat(a[:, :, :]), ACT.Ln, bias=1.0).then_inc(act_step, 1)
                qd, kd, kst = x, a, g
                with stage("e_up", "e_down", "e_rest", "rest", "made") as (block, e_up, e_down, e_rest, rest_, made):
                    ex, en = scratch(5, 0, 4, T), scratch(5, 1, 4, T)
                    @block.gpsimd
                    def _(pool):
                        for t in range(4):
                            for n in range(NC):
                                op = pool.tensor_scalar(kst[:, t, n * 64:(n + 1) * 64], b[:, t, n * 64:(n + 1) * 64], tot[:, t, n:n + 1], None, ALU.subtract)
                        op.then_inc(rest_, 1)

                    @block.scalar
                    def _(act):
                        act.activation(flat(ex[:, :, :]), flat(b[:, :, :]), ACT.Exp).then_inc(e_up, 1)
                        act.activation(flat(en[:, :, :]), flat(b[:, :, :]), ACT.Exp, scale=-1.0).then_inc(e_down, 1)
                        act.activation(flat(dec[:, :, :]), flat(tot[:, :, :]), ACT.Exp).then_inc(e_down, 1)
                        act.wait_ge(rest_, 1)
                        act.activation(flat(kst[:, :, :]), flat(kst[:, :, :]), ACT.Exp, scale=-1.0).then_inc(e_rest, 1)

                    @block.vector
                    def _(dve):
                        dve.wait_ge(e_up, 1)
                        for d in range(2):
                            dve.scalar_tensor_tensor(out=flat(qd[:, 2 * d:2 * d + 2, :]), in0=flat(gq[:, :, :]), scalar=64 ** -0.5,
                                                     in1=flat(ex[:, 2 * d:2 * d + 2, :]), op0=ALU.mult, op1=ALU.mult).then_inc(made, 1)
                        dve.wait_ge(e_down, 1)
                        for d in range(2):
                            dve.tensor_tensor(flat(kd[:, 2 * d:2 * d + 2, :]), flat(gk[:, :, :]), flat(en[:, 2 * d:2 * d + 2, :]), ALU.mult).then_inc(made, 1)
                        dve.wait_ge(e_rest, 1)
                        for d in range(2):
                            dve.tensor_tensor(flat(kst[:, 2 * d:2 * d + 2, :]), flat(gk[:, :, :]), flat(kst[:, 2 * d:2 * d + 2, :]), ALU.mult).then_inc(made, 1)
                kT = scratch(0, 1, TT, 512)
                transposes([([(kst[:, t, tt * P:(tt + 1) * P], t * P) for t in range(4)], kT[:, tt, :]) for tt in range(TT)])
                ent = scratch(4, 0, 4, NC, P)
                order = {0: [0, 1, 2, 3], 1: [3, 2, 1, 0]}
                place = {}
                for par in range(2):
                    n = 0
                    for d in range(2):
                        for ch in order[d][:3]:
                            if ch % 2 == par:
                                for p in range(2):
                                    place[d, ch, p] = (2 * par + n // 4, n % 4)
                                    n += 1
                with stage("grown", "carried") as (block, grown, carried):
                    @block.tensor
                    def _(pe):
                        for (d, ch, p), (bk, col) in place.items():
                            r = ch % 2 * 64
                            for hp in range(2):
                                h = 2 * p + hp
                                mm = pe.matmul(bank(bk)[hp * 64:hp * 64 + 64, col * P:(col + 1) * P], kT[r:r + 64, ch // 2, d * 256 + h * 64:d * 256 + h * 64 + 64],
                                               gv[r:r + 64, ch // 2, h * P:(h + 1) * P], start=True, stop=True)
                        mm.then_inc(grown, 1)

                    @block.vector
                    def _(dve):
                        dve.wait_ge(grown, 1)
                        n = 0
                        for i in range(3):
                            for d in range(2):
                                now, nxt = order[d][i], order[d][i + 1]
                                for p in range(2):
                                    t = 2 * d + p
                                    bk, col = place[d, now, p]
                                    src, dst = bank(bk)[:, col * P:(col + 1) * P], ent[:, t, nxt, :]
                                    if i == 0:
                                        dve.tensor_copy(dst, src).then_inc(carried, 1)
                                    else:
                                        dve.wait_ge(carried, n - 3)
                                        dve.scalar_tensor_tensor(out=dst, in0=ent[:, t, now, :], scalar=dec[:, t, now:now + 1], in1=src,
                                                                 op0=ALU.mult, op1=ALU.add).then_inc(carried, 1)
                                    n += 1
                o = scratch(3, 1, 4, T)
                am = scratch(1, 1, 3, 2 * P)
                U = [(h, tt) for h in range(H) for tt in range(TT)]
                with stage("scored", "masked", "summed", "out") as (block, scored, masked, summed, outed):
                    @block.tensor
                    def _(pe):
                        for i in range(len(U) + 1):
                            if i < len(U):
                                h, tt = U[i]
                                lo = h % 2 * 64
                                if i >= 3:
                                    pe.wait_ge(masked, i - 2)
                                for d in range(2):
                                    t = 2 * d + h // 2
                                    mm = pe.matmul(bank(i % 3)[:, d * P:(d + 1) * P], kd[lo:lo + 64, t, tt * P:(tt + 1) * P], qd[lo:lo + 64, t, tt * P:(tt + 1) * P],
                                                   start=True, stop=True)
                                mm.then_inc(scored, 1)
                            if i >= 1:
                                j = i - 1
                                h, tt = U[j]
                                lo = h % 2 * 64
                                pe.wait_ge(masked, j + 1)
                                if j >= 3:
                                    pe.wait_ge(outed, j - 2)
                                bk = bank(3 + j % 3)
                                for d in range(2):
                                    pe.matmul(bk[:, 0:P], gv[:, tt, h * P:(h + 1) * P], am[:, j % 3, d * P:(d + 1) * P], start=(d == 0), stop=(d == 1))
                                for d in range(2):
                                    for ch in (2 * tt, 2 * tt + 1):
                                        if ch == order[d][0]:
                                            continue
                                        cc = ch % 2 * 64
                                        mm = pe.matmul(bk[:, cc:cc + 64], ent[lo:lo + 64, 2 * d + h // 2, ch, :], qd[lo:lo + 64, 2 * d + h // 2, ch * 64:(ch + 1) * 64],
                                                       start=False, stop=True, skip_group_check=True)
                                mm.then_inc(summed, 1)

                    @block.vector
                    def _(dve):
                        for j in range(len(U)):
                            dve.wait_ge(scored, j + 1)
                            if j >= 3:
                                dve.wait_ge(summed, j - 2)
                            dve.tensor_tensor(am[:, j % 3, :], bank(j % 3)[:, 0:2 * P], K["gla_keep"][:, :], ALU.mult).then_inc(masked, 1)

                    @block.scalar
                    def _(act):
                        for j, (h, tt) in enumerate(U):
                            act.wait_ge(summed, j + 1)
                            act.activation(o[:, h, tt * P:(tt + 1) * P], bank(3 + j % 3)[:, 0:P], ACT.Copy).then_inc(outed, 1)
                rmsnorm([(o[:, :, :], [[k] for k in range(4)], ones, 128, lambda k: G["onorm"][:, 0:1], o)])
                with stage("gated") as (block, gated):
                    @block.vector
                    def _(dve):
                        dve.tensor_tensor(flat(og[:, :, :]), flat(og[:, :, :]), flat(o[:, :, :]), ALU.mult).then_inc(gated, 1)

        def hyena(c, hc, skip, w1, w2, w3_dram, b3_dram, hb, hf, dst):
            consts = constant(c, "hy_pos", "hy_window", "dft", "idft")
            dft = K["dft"][:, :].rearrange("p (t s k) -> p t s k", t=TT, s=2)
            idft = K["idft"][:, :].rearrange("p (s k t) -> p s k t", s=2, k=TT)
            with ExitStack() as c:
                F = sb(c, "spectra", [P, 2, 4, 512])
                with ExitStack() as c1:
                    h2 = sb(c1, "filter_hidden", [65, T])
                    w3 = sb(c1, "hy_w3", [65, 2048])
                    load(consts + [(w3[0:64, :], w3_dram), (w3[64:65, :], b3_dram.rearrange("(a n) -> a n", a=1))])
                    an, tn, rr = sb(c1, "angle", [64, T]), sb(c1, "turns", [64, T]), sb(c1, "reduced", [64, T])
                    with stage("made", "step", "sined", "one") as (block, made, step, sined, one):
                        R = REDUCE_STEPS + 1
                        @block.gpsimd
                        def _(pool):
                            pool.memset(h2[64:65, :], 1.0).then_inc(one, 1)
                        @block.tensor
                        def _(pe):
                            pe.matmul(bank(0)[0:64, 0:T], w1[:, :], K["hy_pos"][:, :], start=True, stop=True).then_inc(made, 1)
                            pe.wait_ge(sined, 1)
                            pe.matmul(bank(1)[0:64, 0:T], w2[:, :], h2[0:64, :], start=True, stop=True).then_inc(made, 1)
                        @block.vector
                        def _(dve):
                            st = Steps(dve, step)
                            for j in range(2):
                                dve.wait_ge(made, j + 1)
                                st.did(dve.tensor_scalar(an[:, :], bank(j)[0:64, 0:T], hb[:, j:j + 1], hf[:, j:j + 1], ALU.add, ALU.mult)); st.settle()
                                if j:
                                    dve.wait_ge(sined, 1)
                                reduce_angle(dve, st, an[:, :], tn[:, :], rr[:, :])
                        @block.scalar
                        def _(act):
                            act.wait_ge(step, R)
                            act.activation(h2[0:64, :], rr[:, :], ACT.Sin).then_inc(sined, 1)
                            act.wait_ge(made, 2)
                            act.wait_ge(step, 2 * R)
                            act.activation(h2[0:64, :], rr[:, :], ACT.Sin).then_inc(sined, 1)
                    for o in range(2):
                        with ExitStack() as c2:
                            fb = slots[:, 0, :].rearrange("p (d t n) -> p d t n", d=2, t=TT)
                            ab = slots[:, 1, :].rearrange("p (d t n) -> p d t n", d=2, t=TT)
                            pq = slots[:, 2, :].rearrange("p (d t n) -> p d t n", d=2, t=TT)
                            sc = slots[:, 3, 0:512]
                            win = K["hy_window"][:, :].rearrange("p (t n) -> p t n", t=TT)
                            with stage("made", "windowed", "lag0", "absd", "mixed", "summed", "step", "transformed", "out") as \
                                    (block, made, windowed, lag0, absd, mixed, summed, step, transformed, outed):
                                @block.tensor
                                def _(pe):
                                    for d in range(2):
                                        for t in range(TT):
                                            pe.matmul(bank(2 * d + t), h2[:, t * P:(t + 1) * P], w3[:, (2 * o + d) * 512:(2 * o + d + 1) * 512], start=True, stop=True).then_inc(made, 1)
                                    pe.wait_ge(absd, 2)
                                    for n in range(4):
                                        mm = pe.matmul(bank(4), ones[:, :], ab[:, n // 2, n % 2, :], start=(n == 0), stop=(n == 3))
                                    mm.then_inc(summed, 1)
                                    pe.wait_ge(mixed, 2)
                                    for s in range(2):
                                        for k in range(2):
                                            for t in range(TT):
                                                mm = pe.matmul(bank(2 * s + k), dft[:, t, s, k * P:(k + 1) * P], pq[:, s, t, :], start=(t == 0), stop=(t == TT - 1))
                                            mm.then_inc(transformed, 1)
                                @block.vector
                                def _(dve):
                                    for d in range(2):
                                        for t in range(TT):
                                            dve.wait_ge(made, 2 * d + t + 1)
                                            dve.tensor_tensor(fb[:, d, t, :], bank(2 * d + t), win[:, t, :], ALU.mult).then_inc(windowed, 1)
                                    dve.wait_ge(windowed, 3)
                                    dve.memset(fb[0:1, 1, 0, :], 0.0).then_inc(lag0, 1)
                                    dve.wait_ge(lag0, 1)
                                    dve.wait_ge(windowed, 4)
                                    for s, op in enumerate((ALU.add, ALU.subtract)):
                                        dve.tensor_tensor(flat(pq[:, s]), flat(fb[:, 0]), flat(fb[:, 1]), op).then_inc(mixed, 1)
                                    dve.wait_ge(summed, 1)
                                    st = Steps(dve, step)
                                    st.did(dve.tensor_scalar(sc[:, :], bank(4), EPS, None, ALU.add)); st.settle()
                                    st.did(dve.reciprocal(sc[:, :], sc[:, :])); st.settle()
                                    for n in range(4):
                                        dve.wait_ge(transformed, n + 1)
                                        dve.tensor_tensor(F[:, o, n, :], bank(n), sc[:, :], ALU.mult).then_inc(outed, 1)
                                @block.scalar
                                def _(act):
                                    act.wait_ge(windowed, 4)
                                    act.wait_ge(lag0, 1)
                                    for d in range(2):
                                        act.activation(flat(ab[:, d]), flat(fb[:, d]), ACT.Abs).then_inc(absd, 1)
                u = sb(c, "tokens", [P, TT, 512])
                y = slots[:, 0, :].rearrange("p (a n) -> p a n", a=4)
                t2 = slots[:, 1, :].rearrange("p (a n) -> p a n", a=4)
                z = sb(c, "z", [P, 4, T])
                src = [hc[:, 0:4, :], z[:, :, :]]
                for o in range(2):
                    transposes([([(src[o][:, k, t * P:(t + 1) * P], k * P) for k in range(4)], u[:, t, :]) for t in range(TT)])
                    res_ = z if o == 0 else dst
                    with stage("transformed", "first", "second", "product", "back", "skipped", "out") as \
                            (block, transformed, first_, second_, product, back, skipped, outed):
                        @block.tensor
                        def _(pe):
                            for n in range(4):
                                for t in range(TT):
                                    mm = pe.matmul(bank(n), dft[:, t, n // 2, n % 2 * P:(n % 2 + 1) * P], u[:, t, :], start=(t == 0), stop=(t == TT - 1))
                                mm.then_inc(transformed, 1)
                            pe.wait_ge(product, 4)
                            for m in range(4):
                                for n in range(4):
                                    mm = pe.matmul(bank(4 + m)[:, 0:T], y[:, n, m * P:(m + 1) * P], idft[:, n // 2, n % 2, :], start=(n == 0), stop=(n == 3))
                                mm.then_inc(back, 1)
                        @block.vector
                        def _(dve):
                            dve.wait_ge(transformed, 4)
                            for k in range(2):
                                Ak, Bk, Fc, Fs = bank(k), bank(2 + k), F[:, o, k, :], F[:, o, 2 + k, :]
                                dve.tensor_tensor(y[:, k, :], Ak, Fc, ALU.mult).then_inc(first_, 1)
                                dve.tensor_tensor(y[:, 2 + k, :], Ak, Fs, ALU.mult).then_inc(first_, 1)
                                dve.tensor_tensor(t2[:, k, :], Bk, Fs, ALU.mult).then_inc(second_, 1)
                                dve.tensor_tensor(t2[:, 2 + k, :], Bk, Fc, ALU.mult).then_inc(second_, 1)
                            for m in range(4):
                                dve.wait_ge(back, m + 1)
                                dve.scalar_tensor_tensor(out=res_[:, m, :], in0=src[o][:, m, :], scalar=skip[:, o, m:m + 1], in1=bank(4 + m)[:, 0:T],
                                                         op0=ALU.mult, op1=ALU.add).then_inc(skipped, 1)
                            for m in range(4):
                                dve.wait_ge(skipped, m + 1)
                                dve.tensor_tensor(res_[:, m, :], res_[:, m, :], hc[:, 4 * (o + 1) + m, :], ALU.mult).then_inc(outed, 1)
                        @block.gpsimd
                        def _(pool):
                            for k in range(2):
                                pool.wait_ge(first_, 2 * k + 2)
                                pool.wait_ge(second_, 2 * k + 2)
                                pool.tensor_tensor(y[:, k, :], y[:, k, :], t2[:, k, :], ALU.subtract).then_inc(product, 1)
                                pool.tensor_tensor(y[:, 2 + k, :], y[:, 2 + k, :], t2[:, 2 + k, :], ALU.add).then_inc(product, 1)

        with nc.Fori(0, 1 if stop == "layer" else 2) as L:
            layer(L)
        if stop == "layer":
            dump("mlp0", res[:, :, :])
            return

        with ExitStack() as c:
            y = sb(c, "y", [P, TT, D])
            transposes([([(res[:, 4 * g + k, t * P:(t + 1) * P], k * P) for k in range(4)], y[:, t, g * 512:(g + 1) * 512]) for t in range(TT) for g in range(2)])
            with stage("stored") as (block, stored):
                @block.sync
                def _(sp):
                    sp.dma_start(out[0].rearrange("(t p) d -> p t d", p=P), y[:, :, :]).then_inc(stored, 16)
                    sp.wait_ge(stored, 16)


REDUCE_STEPS = 6


def reduce_angle(dve, st, ang, turns, out):
    magic = 1.5 * 2.0 ** 23
    two_pi = 2 * math.pi
    c1 = float(np.float32(6.28125))
    c2 = float(np.float32(two_pi - c1))
    c2 = float(np.float32(np.round(c2 * 2 ** 20) / 2 ** 20))
    c3 = two_pi - c1 - c2
    st.did(dve.tensor_scalar(turns, ang, 1.0 / two_pi, magic, ALU.mult, ALU.add)); st.settle()
    st.did(dve.tensor_scalar(turns, turns, magic, None, ALU.subtract)); st.settle()
    st.did(dve.scalar_tensor_tensor(out=out, in0=turns, scalar=-c1, in1=ang, op0=ALU.mult, op1=ALU.add)); st.settle()
    st.did(dve.scalar_tensor_tensor(out=out, in0=turns, scalar=-c2, in1=out, op0=ALU.mult, op1=ALU.add)); st.settle()
    st.did(dve.scalar_tensor_tensor(out=out, in0=turns, scalar=-c3, in1=out, op0=ALU.mult, op1=ALU.add)); st.settle()
    st.did(dve.tensor_scalar(out, out, 3.1415925, -3.1415925, ALU.min, ALU.max)); st.settle()


def kernel(**inputs):
    import concourse.bacc as bacc
    from concourse.bass_utils import run_bass_kernel_spmd

    nc = bacc.Bacc("TRN2", target_bir_lowering=False, num_devices=1)
    arrays, A = {}, {}
    for name, a in list(inputs.items()) + [("c_" + n, a) for n, a in CONST.items()]:
        a = np.ascontiguousarray(a)
        arrays[f"in_{name}_dram"] = a
        A[name] = nc.dram_tensor(f"in_{name}_dram", a.shape, mybir.dt.from_np(a.dtype), kind="ExternalInput").ap()
    out = nc.dram_tensor("out_0_dram", (1, T, D), F32, kind="ExternalOutput").ap()
    program(nc, A, out)
    r = run_bass_kernel_spmd(nc, [arrays], core_ids=[0])
    return r.results[0]["out_0_dram"]
```
